# Optimizing a Trainium2 kernel written in Bass

```python
import jax, jax.numpy as jnp
from jax import lax
import numpy as np

D_MODEL = 1024
BATCH = 1
SEQ = 256
DEPTH = 2
DEC_BATCH = 8
DEC_SEQ = 4
PAST_LEN = 1024
PAGE_SIZE = 128

HEAD_DIM = 64
LRU_WIDTH = D_MODEL // 2
LRU_BLOCKS = 8
LRU_BLOCK_W = LRU_WIDTH // LRU_BLOCKS
LRU_C = 8.0
CONV_W = 4
SWA_HEADS = (D_MODEL // 2) // HEAD_DIM
SWA_KV_HEADS = 2
SWA_GROUP = SWA_HEADS // SWA_KV_HEADS
SWA_WINDOW = 128
EVEN_MIX = LRU_WIDTH + SWA_HEADS * HEAD_DIM
DIL_WINDOWS = (128, 512, 2048)
DIL_RATES = (1, 4, 16)
N_DIL = 3
DIL_HEADS = 8
ODD_IN = N_DIL * 3 * DIL_HEADS * HEAD_DIM
ODD_MIX = DIL_HEADS * HEAD_DIM
BAND_BLOCK = 128
N_EXPERTS = 64
N_EXPERT_GROUPS = 8
TOPK_GROUPS = 4
TOP_K = 8
D_EXPERT = 256
D_SHARED = 256
ROUTED_SCALE = 2.5
MOE_BLOCK = 128
LN_EPS = 1e-5
DEEPNORM_ALPHA = (2 * DEPTH) ** 0.25
DEEPNORM_BETA = (8 * DEPTH) ** -0.25
N_EVEN = (DEPTH + 1) // 2
N_ODD = DEPTH // 2

kernel_name = 'hybrid_lru_swa_dilated_moe_step'

F32 = jnp.float32

def alibi_slopes(n):
    return jnp.exp2(-8.0 * jnp.arange(1, n + 1, dtype=F32) / n)

def post_norm(x, f, g, b):
    z = DEEPNORM_ALPHA * x.astype(F32) + f.astype(F32)
    zc = z - jnp.mean(z, -1, keepdims=True)
    var = jnp.mean(zc * zc, -1, keepdims=True)
    return (zc * lax.rsqrt(var + LN_EPS) * g.astype(F32) + b.astype(F32)).astype(x.dtype)

def causal_conv(x_full, w, b):
    T = x_full.shape[1] - (CONV_W - 1)
    y = b.astype(F32)
    for j in range(CONV_W):
        y = y + w[j].astype(F32) * x_full[:, j:j + T].astype(F32)
    return y

def rg_lru(x, h0, w_r, b_r, w_i, b_i, lam):
    B, T, C = x.shape
    xb = x.reshape(B, T, LRU_BLOCKS, LRU_BLOCK_W)
    r = jax.nn.sigmoid(jnp.einsum('btnc,ncd->btnd', xb, w_r.astype(F32)).reshape(B, T, C) + b_r.astype(F32))
    i = jax.nn.sigmoid(jnp.einsum('btnc,ncd->btnd', xb, w_i.astype(F32)).reshape(B, T, C) + b_i.astype(F32))
    log_a = -LRU_C * r * jax.nn.softplus(-lam.astype(F32))
    a = jnp.exp(log_a)
    u = jnp.sqrt(-jnp.expm1(2.0 * log_a)) * (i * x)

    def combine(lhs, rhs):
        a1, b1 = lhs
        a2, b2 = rhs
        return a1 * a2, a2 * b1 + b2

    a_cum, u_cum = lax.associative_scan(combine, (a, u), axis=1)
    return a_cum * h0.astype(F32)[:, None] + u_cum

def banded_attention(q, k, v, slopes, window_idx, dist_scale):
    B, L, KV, G, Dh = q.shape
    nb = -(-L // BAND_BLOCK)
    pad = nb * BAND_BLOCK - L
    qb = jnp.pad(q, ((0, 0), (0, pad), (0, 0), (0, 0), (0, 0))).reshape(B, nb, BAND_BLOCK, KV, G, Dh)

    def with_prev_block(a):
        ap = jnp.pad(a, ((0, 0), (BAND_BLOCK, pad), (0, 0), (0, 0))).reshape(B, nb + 1, BAND_BLOCK, KV, Dh)
        return jnp.concatenate([ap[:, :-1], ap[:, 1:]], axis=2)

    kb, vb = with_prev_block(k), with_prev_block(v)
    s = jnp.einsum('bnqkgd,bnskd->bnkgqs', qb, kb, preferred_element_type=F32) * (Dh ** -0.5)
    qi = jnp.arange(BAND_BLOCK)[:, None]
    kj = jnp.arange(2 * BAND_BLOCK)[None, :]
    dist = qi + BAND_BLOCK - kj
    key_pos = jnp.arange(nb)[:, None, None] * BAND_BLOCK - BAND_BLOCK + kj[None]
    valid = (dist >= 0) & (dist <= window_idx) & (key_pos >= 0)
    s = s - slopes.astype(F32)[None, None, :, :, None, None] * (dist_scale * dist).astype(F32)
    s = jnp.where(valid[None, :, None, None], s, -jnp.inf)
    lse = jax.nn.logsumexp(s, axis=-1)
    p = jnp.exp(s - lse[..., None])
    o = jnp.einsum('bnkgqs,bnskd->bnqkgd', p, vb)
    o = o.reshape(B, nb * BAND_BLOCK, KV, G, Dh)[:, :L]
    lse = lse.transpose(0, 1, 4, 2, 3).reshape(B, nb * BAND_BLOCK, KV, G)[:, :L]
    return o, lse

def strided_window_decode(q, k_all, v_all, n_past, window, dil, slopes):
    T, Dh = q.shape[1], q.shape[-1]
    steps = jnp.arange(window // dil + 1)
    idx = n_past + jnp.arange(T)[:, None] - dil * steps[None, :]
    valid = idx >= 0
    idx = jnp.maximum(idx, 0)
    kg = k_all[:, idx]
    vg = v_all[:, idx]
    s = jnp.einsum('btkgd,btnkd->btkgn', q, kg, preferred_element_type=F32) * (Dh ** -0.5)
    s = s - slopes.astype(F32)[None, None, :, :, None] * (dil * steps).astype(F32)
    s = jnp.where(valid[None, :, None, None, :], s, -jnp.inf)
    lse = jax.nn.logsumexp(s, axis=-1)
    p = jnp.exp(s - lse[..., None])
    o = jnp.einsum('btkgn,btnkd->btkgd', p, vg)
    return o, lse

def dilated_prompt_attention(q, k, v, window, dil, slopes):
    B, L, H, Dh = q.shape
    Lf = L // dil

    def fold(a):
        return a.reshape(B, Lf, dil, H, Dh).transpose(0, 2, 1, 3, 4).reshape(B * dil, Lf, H, Dh)

    o, lse = banded_attention(fold(q)[:, :, :, None], fold(k), fold(v), slopes, window // dil, dil)
    o = o[:, :, :, 0].reshape(B, dil, Lf, H, Dh).transpose(0, 2, 1, 3, 4).reshape(B, L, H, Dh)
    lse = lse[..., 0].reshape(B, dil, Lf, H).transpose(0, 2, 1, 3).reshape(B, L, H)
    return o, lse

def even_mixer(x, w_in, conv_w, conv_b, w_rgate, b_rgate, w_igate, b_igate, lru_lambda, sinks, w_out, past):
    B, T, _ = x.shape
    proj = jnp.einsum('btd,de->bte', x, w_in)
    o1 = LRU_WIDTH
    o2 = 2 * LRU_WIDTH
    o3 = o2 + SWA_HEADS * HEAD_DIM
    o4 = o3 + SWA_KV_HEADS * HEAD_DIM
    xr, yg = proj[..., :o1], proj[..., o1:o2]
    q = proj[..., o2:o3].reshape(B, T, SWA_KV_HEADS, SWA_GROUP, HEAD_DIM)
    k = proj[..., o3:o4].reshape(B, T, SWA_KV_HEADS, HEAD_DIM)
    v = proj[..., o4:].reshape(B, T, SWA_KV_HEADS, HEAD_DIM)
    if past is None:
        h0 = jnp.zeros((B, LRU_WIDTH), x.dtype)
        conv_buf = jnp.zeros((B, CONV_W - 1, LRU_WIDTH), x.dtype)
    else:
        h0, conv_buf, kv_buf = past
    xr_full = jnp.concatenate([conv_buf.astype(xr.dtype), xr], axis=1)
    h = rg_lru(causal_conv(xr_full, conv_w, conv_b), h0, w_rgate, b_rgate, w_igate, b_igate, lru_lambda)
    a_out = (h * jax.nn.gelu(yg.astype(F32))).astype(x.dtype)
    slopes = alibi_slopes(SWA_HEADS).reshape(SWA_KV_HEADS, SWA_GROUP)
    if past is None:
        o, lse = banded_attention(q, k, v, slopes, SWA_WINDOW, 1)
        keep = min(SWA_WINDOW, T)
        new_kv = jnp.stack([k[:, T - keep:], v[:, T - keep:]], axis=2)
    else:
        n_past = kv_buf.shape[1]
        k_all = jnp.concatenate([kv_buf[:, :, 0].astype(k.dtype), k], axis=1)
        v_all = jnp.concatenate([kv_buf[:, :, 1].astype(v.dtype), v], axis=1)
        o, lse = strided_window_decode(q, k_all, v_all, n_past, SWA_WINDOW, 1, slopes)
        new_kv = jnp.stack([k_all[:, T:], v_all[:, T:]], axis=2)
    sink = sinks.astype(F32).reshape(SWA_KV_HEADS, SWA_GROUP)
    o = o * jax.nn.sigmoid(lse - sink)[..., None]
    mix = jnp.concatenate([a_out, o.reshape(B, T, SWA_HEADS * HEAD_DIM).astype(x.dtype)], axis=-1)
    out = jnp.einsum('bte,ed->btd', mix, w_out)
    return out, (h[:, -1].astype(x.dtype), xr_full[:, -(CONV_W - 1):], new_kv)

def odd_mixer(x, w_in, w_out, past):
    B, T, _ = x.shape
    proj = jnp.einsum('btd,de->bte', x, w_in).reshape(B, T, N_DIL, 3, DIL_HEADS, HEAD_DIM)
    slopes = alibi_slopes(DIL_HEADS)[:, None]
    outs, lses, new = [], [], []
    for g in range(N_DIL):
        win, dil = DIL_WINDOWS[g], DIL_RATES[g]
        q, k, v = proj[:, :, g, 0], proj[:, :, g, 1], proj[:, :, g, 2]
        if past is None:
            o, lse = dilated_prompt_attention(q, k, v, win, dil, slopes)
            keep = min(win, T)
            new.append(jnp.stack([k[:, T - keep:], v[:, T - keep:]], axis=2))
        else:
            kv_buf = past[g]
            n_past = kv_buf.shape[1]
            k_all = jnp.concatenate([kv_buf[:, :, 0].astype(k.dtype), k], axis=1)
            v_all = jnp.concatenate([kv_buf[:, :, 1].astype(v.dtype), v], axis=1)
            o, lse = strided_window_decode(q[:, :, :, None], k_all, v_all, n_past, win, dil, slopes)
            o, lse = o[:, :, :, 0], lse[..., 0]
            new.append(jnp.stack([k_all[:, T:], v_all[:, T:]], axis=2))
        outs.append(o)
        lses.append(lse)
    wts = jax.nn.softmax(jnp.stack(lses, 0), axis=0)
    o = jnp.einsum('gbth,gbthd->bthd', wts, jnp.stack(outs, 0))
    out = jnp.einsum('bte,ed->btd', o.reshape(B, T, ODD_MIX).astype(x.dtype), w_out)
    return out, new

def moe_ffn(x, w_router, router_bias, w_gate, w_up, w_down, ws_gate, ws_up, ws_down):
    B, T, D = x.shape
    xf = x.reshape(-1, D)
    N = xf.shape[0]
    scores = jax.nn.sigmoid(jnp.einsum('nd,de->ne', xf, w_router, preferred_element_type=F32))
    biased = scores + router_bias.astype(F32)
    grp = biased.reshape(N, N_EXPERT_GROUPS, N_EXPERTS // N_EXPERT_GROUPS)
    grp_score = lax.top_k(grp, 2)[0].sum(-1)
    top_grp = lax.top_k(grp_score, TOPK_GROUPS)[1]
    grp_mask = jnp.any(top_grp[..., None] == jnp.arange(N_EXPERT_GROUPS), axis=1)
    exp_mask = jnp.repeat(grp_mask, N_EXPERTS // N_EXPERT_GROUPS, axis=1)
    top_e = lax.top_k(jnp.where(exp_mask, biased, -jnp.inf), TOP_K)[1]
    gate = jnp.take_along_axis(scores, top_e, axis=1)
    gate = gate / jnp.sum(gate, -1, keepdims=True) * ROUTED_SCALE
    flat_e = top_e.reshape(-1)
    order = jnp.argsort(flat_e)
    e_sorted = flat_e[order]
    tok_sorted = order // TOP_K
    counts = jnp.bincount(flat_e, length=N_EXPERTS)
    padded = (counts + MOE_BLOCK - 1) // MOE_BLOCK * MOE_BLOCK
    start = jnp.cumsum(counts) - counts
    pend = jnp.cumsum(padded)
    pstart = pend - padded
    dest = pstart[e_sorted] + (jnp.arange(N * TOP_K) - start[e_sorted])
    n_blocks = -(-(N * TOP_K) // MOE_BLOCK) + N_EXPERTS
    x_disp = jnp.zeros((n_blocks * MOE_BLOCK, D), x.dtype).at[dest].set(xf[tok_sorted])
    block_e = jnp.minimum(jnp.searchsorted(pend, jnp.arange(n_blocks) * MOE_BLOCK, side='right'), N_EXPERTS - 1)

    def expert_block(args):
        xb, e = args
        hb = jax.nn.silu(xb @ w_gate[e]) * (xb @ w_up[e])
        return hb @ w_down[e]

    y_disp = lax.map(expert_block, (x_disp.reshape(n_blocks, MOE_BLOCK, D), block_e))
    y_sorted = y_disp.reshape(-1, D)[dest]
    gate_sorted = gate.reshape(-1)[order]
    routed = jax.ops.segment_sum(y_sorted.astype(F32) * gate_sorted[:, None], tok_sorted, num_segments=N)
    shared = (jax.nn.silu(xf @ ws_gate) * (xf @ ws_up)) @ ws_down
    return (routed + shared.astype(F32)).astype(x.dtype).reshape(B, T, D)

def setup_inputs(seed: int = 0) -> dict:
    key = jax.random.key(seed)
    ks = iter(jax.random.split(key, 40))

    def nrm(shape, scale):
        return scale * jax.random.normal(next(ks), shape, F32)

    swa_buf = min(SWA_WINDOW, PAST_LEN)
    dil_buf = [min(w, PAST_LEN) for w in DIL_WINDOWS]
    u = jax.random.uniform(next(ks), (N_EVEN, LRU_WIDTH), F32, 0.9, 0.999)
    p = u ** (1.0 / LRU_C)
    lam = jnp.log(p) - jnp.log1p(-p)
    dil_kv = lambda n: (N_ODD, DEC_BATCH, n, 2, DIL_HEADS, HEAD_DIM)
    return {
        'x_prompt': nrm((BATCH, SEQ, D_MODEL), 1.0),
        'x_sample': nrm((DEC_BATCH, DEC_SEQ, D_MODEL), 1.0),
        'state_lru_h': nrm((N_EVEN, DEC_BATCH, LRU_WIDTH), 1.0),
        'state_lru_conv': nrm((N_EVEN, DEC_BATCH, CONV_W - 1, LRU_WIDTH), 1.0),
        'cache_swa_kv': nrm((N_EVEN, DEC_BATCH, swa_buf, 2, SWA_KV_HEADS, HEAD_DIM), 1.0),
        'cache_dil1_kv': nrm(dil_kv(dil_buf[0]), 1.0),
        'cache_dil2_kv': nrm(dil_kv(dil_buf[1]), 1.0),
        'cache_dil3_kv': nrm(dil_kv(dil_buf[2]), 1.0),
        'w_in_even': nrm((N_EVEN, D_MODEL, 2 * LRU_WIDTH + (SWA_HEADS + 2 * SWA_KV_HEADS) * HEAD_DIM), D_MODEL ** -0.5),
        'conv_w': nrm((N_EVEN, CONV_W, LRU_WIDTH), CONV_W ** -0.5),
        'conv_b': nrm((N_EVEN, LRU_WIDTH), 0.01),
        'w_rgate': nrm((N_EVEN, LRU_BLOCKS, LRU_BLOCK_W, LRU_BLOCK_W), LRU_BLOCK_W ** -0.5),
        'b_rgate': nrm((N_EVEN, LRU_WIDTH), 0.01),
        'w_igate': nrm((N_EVEN, LRU_BLOCKS, LRU_BLOCK_W, LRU_BLOCK_W), LRU_BLOCK_W ** -0.5),
        'b_igate': nrm((N_EVEN, LRU_WIDTH), 0.01),
        'lru_lambda': lam,
        'swa_sinks': nrm((N_EVEN, SWA_HEADS), 1.0),
        'w_out_even': nrm((N_EVEN, EVEN_MIX, D_MODEL), EVEN_MIX ** -0.5 * DEEPNORM_BETA),
        'w_in_odd': nrm((N_ODD, D_MODEL, ODD_IN), D_MODEL ** -0.5),
        'w_out_odd': nrm((N_ODD, ODD_MIX, D_MODEL), ODD_MIX ** -0.5 * DEEPNORM_BETA),
        'ln1_g': 1.0 + nrm((DEPTH, D_MODEL), 0.02),
        'ln1_b': nrm((DEPTH, D_MODEL), 0.02),
        'ln2_g': 1.0 + nrm((DEPTH, D_MODEL), 0.02),
        'ln2_b': nrm((DEPTH, D_MODEL), 0.02),
        'w_router': nrm((DEPTH, D_MODEL, N_EXPERTS), D_MODEL ** -0.5),
        'router_bias': nrm((DEPTH, N_EXPERTS), 0.01),
        'w_exp_gate': nrm((DEPTH, N_EXPERTS, D_MODEL, D_EXPERT), D_MODEL ** -0.5),
        'w_exp_up': nrm((DEPTH, N_EXPERTS, D_MODEL, D_EXPERT), D_MODEL ** -0.5),
        'w_exp_down': nrm((DEPTH, N_EXPERTS, D_EXPERT, D_MODEL), D_EXPERT ** -0.5 * DEEPNORM_BETA),
        'w_sh_gate': nrm((DEPTH, D_MODEL, D_SHARED), D_MODEL ** -0.5),
        'w_sh_up': nrm((DEPTH, D_MODEL, D_SHARED), D_MODEL ** -0.5),
        'w_sh_down': nrm((DEPTH, D_SHARED, D_MODEL), D_SHARED ** -0.5 * DEEPNORM_BETA),
    }

def reference(x_prompt, x_sample, state_lru_h, state_lru_conv, cache_swa_kv, cache_dil1_kv, cache_dil2_kv,
              cache_dil3_kv, w_in_even, conv_w, conv_b, w_rgate, b_rgate, w_igate, b_igate, lru_lambda,
              swa_sinks, w_out_even, w_in_odd, w_out_odd, ln1_g, ln1_b, ln2_g, ln2_b, w_router, router_bias,
              w_exp_gate, w_exp_up, w_exp_down, w_sh_gate, w_sh_up, w_sh_down):
    xp, xs = x_prompt, x_sample
    lru_h_p, lru_h_s, lru_c_p, lru_c_s, swa_p, swa_s = [], [], [], [], [], []
    dil_p, dil_s = [[], [], []], [[], [], []]
    for l in range(DEPTH):
        j = l // 2
        if l % 2 == 0:
            ew = (w_in_even[j], conv_w[j], conv_b[j], w_rgate[j], b_rgate[j], w_igate[j], b_igate[j],
                  lru_lambda[j], swa_sinks[j], w_out_even[j])
            mp, (hp, cp, kvp) = even_mixer(xp, *ew, past=None)
            ms, (hs, cs, kvs) = even_mixer(xs, *ew, past=(state_lru_h[j], state_lru_conv[j], cache_swa_kv[j]))
            lru_h_p.append(hp)
            lru_h_s.append(hs)
            lru_c_p.append(cp)
            lru_c_s.append(cs)
            swa_p.append(kvp)
            swa_s.append(kvs)
        else:
            mp, newp = odd_mixer(xp, w_in_odd[j], w_out_odd[j], past=None)
            ms, news = odd_mixer(xs, w_in_odd[j], w_out_odd[j],
                                 past=(cache_dil1_kv[j], cache_dil2_kv[j], cache_dil3_kv[j]))
            for g in range(N_DIL):
                dil_p[g].append(newp[g])
                dil_s[g].append(news[g])
        xp = post_norm(xp, mp, ln1_g[l], ln1_b[l])
        xs = post_norm(xs, ms, ln1_g[l], ln1_b[l])
        mw = (w_router[l], router_bias[l], w_exp_gate[l], w_exp_up[l], w_exp_down[l],
              w_sh_gate[l], w_sh_up[l], w_sh_down[l])
        xp = post_norm(xp, moe_ffn(xp, *mw), ln2_g[l], ln2_b[l])
        xs = post_norm(xs, moe_ffn(xs, *mw), ln2_g[l], ln2_b[l])
    y_prompt, y_sample = xp, xs
    lru_h_prompt, lru_h_sample = jnp.stack(lru_h_p), jnp.stack(lru_h_s)
    lru_conv_prompt, lru_conv_sample = jnp.stack(lru_c_p), jnp.stack(lru_c_s)
    swa_kv_prompt, swa_kv_sample = jnp.stack(swa_p), jnp.stack(swa_s)
    dil1_kv_prompt, dil1_kv_sample = jnp.stack(dil_p[0]), jnp.stack(dil_s[0])
    dil2_kv_prompt, dil2_kv_sample = jnp.stack(dil_p[1]), jnp.stack(dil_s[1])
    dil3_kv_prompt, dil3_kv_sample = jnp.stack(dil_p[2]), jnp.stack(dil_s[2])
    return (y_prompt, y_sample, lru_h_prompt, lru_h_sample, lru_conv_prompt, lru_conv_sample,
            swa_kv_prompt, swa_kv_sample, dil1_kv_prompt, dil1_kv_sample, dil2_kv_prompt, dil2_kv_sample,
            dil3_kv_prompt, dil3_kv_sample)


_drawn_inputs = setup_inputs


def setup_inputs(seed=0):
    import zlib

    import numpy as np

    out = dict(_drawn_inputs(seed))
    spreads = {}
    factors = {'b_rgate': 23.119, 'b_igate': 9.36}
    for name, (base, spread) in spreads.items():
        noise = np.random.default_rng([zlib.crc32(name.encode()), seed]).standard_normal(out[name].shape)
        drawn = base * np.exp(spread * noise) if base else spread * noise
        out[name] = __import__('jax').numpy.asarray(drawn.astype(out[name].dtype))
    for name, factor in factors.items():
        out[name] = (out[name] * factor).astype(out[name].dtype)
    return out
```

```python
from contextlib import ExitStack

import numpy as np

import concourse.bass as bass
from concourse import mybir

F32 = mybir.dt.float32
I32 = mybir.dt.int32
ALU = mybir.AluOpType
ACT = mybir.ActivationFunctionType
AX = mybir.AxisListType

P = 128
D = 1024
NC = D // P
NPR, NSA = 256, 32
NT = NPR + NSA
NTP = 3 * P
NB, TS = 8, 4
ROWS = (P, P, NSA)
HD = 64
NH = 8
NE = 64
DE = 256
CAP = 64
PASSES = -(-NT // CAP)
SLOT = 6144
RING = 4
BANK = 512
ALPHA = float(4 ** 0.25)
EPS = 1e-5
SCALE = HD ** -0.5
NEG = -1e30
BIG = 1e30
LRU_TILES = 4
CONVW = 4
SEQ_S = CONVW - 1 + TS
XRW = CONVW - 1 + NPR + NB * SEQ_S
CW = XRW - (CONVW - 1)
SAMP0 = NPR + CONVW - 1
WIN = (P, 512, 1024)
DIL = (1, 4, 16)
OLD = 7 * P
DEC_W = OLD + 3 * NSA
EV_COLS = 1792
OD_TILES = 36
OUT0 = 16 * 8
OUT1 = OUT0 + 16 * 8
MISC = 6 + PASSES + PASSES * CAP + 64 + 1 + NH


def tables():
    slopes = 2.0 ** -(np.arange(1, NH + 1))
    row = np.arange(P)
    bb, h, t = row // 32, (row % 32) // TS, row % TS
    far = 1e30

    def dist(d, ok):
        return np.where(ok, d, far).astype(np.float32)

    q, k = np.arange(NPR)[:, None], np.arange(NPR)[None, :]
    d = q - k
    win = dist(d, (d >= 0) & (d <= P))
    d4 = dist(d, (d >= 0) & (d % 4 == 0) & (d <= 512))
    d16 = dist(d, (d >= 0) & (d % 16 == 0) & (d <= 2048))
    prompt = np.concatenate([m[:P, :P] for m in (win, d4, d16)] + [m[P:] for m in (win, d4, d16)], axis=1)
    old1 = P + t[:, None] - np.arange(P)[None, :]
    old1 = dist(old1, (old1 <= P) & (old1 >= 0))
    d2 = WIN[1] + t[:, None] - np.arange(WIN[1])[None, :]
    d2 = dist(d2, (d2 % 4 == 0) & (d2 <= 512))
    pos3 = (np.arange(256) // TS) * 16 + np.arange(256) % TS
    d3 = WIN[2] + t[:, None] - pos3[None, :]
    d3 = dist(d3, d3 % 16 == 0)
    even, odd = [], []
    for g in range(2):
        nb_, nt_ = np.arange(NSA) // TS, np.arange(NSA) % TS
        same = (4 * g + bb)[:, None] == nb_[None, :]
        dn = t[:, None] - nt_[None, :]
        n1 = dist(dn, same & (dn >= 0))
        n4 = dist(dn, same & (dn == 0))
        even.append(np.concatenate([old1, n1], axis=1))
        odd.append(np.concatenate([d2, old1, d3, n1, n4, n4], axis=1))
    tri = (row[:, None] < row[None, :]).astype(np.float32)
    square = np.concatenate([np.eye(P), tri, np.ones((P, P))], axis=1)
    valid = np.ones((P, 3))
    valid[NSA:, 2] = 0
    g8 = np.arange(NH)
    before = (g8[None, :] < g8[:, None]).astype(np.float32).reshape(1, 64)
    misc = np.concatenate([
        valid, 1 - valid, np.tile(np.arange(1, PASSES + 1) * CAP, (P, 1)),
        np.tile(np.arange(PASSES * CAP), (P, 1)), np.tile(before, (P, 1)), (-8 * slopes[h])[:, None],
        (h[:, None] == g8[None, :])], axis=1)
    f = lambda a: np.ascontiguousarray(a, np.float32)
    return {"c_square": f(square), "c_misc": f(misc), "c_prompt": f(prompt),
            "c_even": f(np.stack(even)), "c_odd": f(np.stack(odd))}


class Chain:

    def __init__(self, eng, sem):
        self.eng, self.sem, self.n = eng, sem, 0

    def __call__(self, ins):
        self.n += 1
        ins.then_inc(self.sem, 1)
        self.eng.wait_ge(self.sem, self.n)


def slope8(h):
    return -8.0 * 2.0 ** -(h + 1)


def build(nc, a, o):
    ctx = ExitStack()
    with ctx:
        def sb(name, shape, dt=F32):
            return ctx.enter_context(nc.sbuf_tensor(name, shape, dt))

        def sem(name):
            return ctx.enter_context(nc.semaphore(name))

        def per_layer(name):
            return [sem(f"{name}_{layer}") for layer in range(2)]

        ps = ctx.enter_context(nc.psum_tensor("ps", [P, 8, BANK], F32))
        ring = sb("ring", [P, RING, SLOT])
        x_tok = sb("x_tok", [P, 3, D])
        xT = sb("xT", [P, NC, NTP])
        mixT = sb("mixT", [P, 8, NT])
        square = sb("square", [P, 3 * P])
        misc = sb("misc", [P, MISC])
        gb = sb("gb", [P, 2, D])
        stats = sb("stats", [P, 3, 16])
        ident, tri, ones = (square[:, i * P:(i + 1) * P] for i in range(3))
        valid, invalid = misc[:, 0:3], misc[:, 3:6]
        thresholds = misc[:, 6:6 + PASSES]
        iota0 = 6 + PASSES
        before = misc[:, iota0 + PASSES * CAP:iota0 + PASSES * CAP + 64]
        row_slope = misc[:, iota0 + PASSES * CAP + 64:iota0 + PASSES * CAP + 65]

        row_head = misc[:, MISC - NH:MISC]

        arena = sb("arena", [P, 16900])

        def cut(sizes, base=0):
            views, at = {}, base
            for name, shape in sizes:
                n = int(np.prod(shape))
                v = arena[:, at:at + n]
                if len(shape) == 2:
                    v = v.rearrange("p (a b) -> p a b", b=shape[1])
                elif len(shape) == 3:
                    v = v.rearrange("p (a b c) -> p a b c", b=shape[1], c=shape[2])
                views[name] = v
                at += n
            assert at <= 16900, at
            return views, at

        EV, _ = cut([("xr", (LRU_TILES, XRW)), ("xc", (LRU_TILES, CW)), ("rg", (LRU_TILES, CW)),
                     ("ig", (LRU_TILES, CW)), ("gel", (4, NT)), ("q", (4, NT)),
                     ("kv", (2, NT)), ("vtok", (3, P)), ("ktok", (3, P)), ("ktd", (NB, P)), ("qz", (NB, 32)),
                     ("s", (2, 256)), ("pt", (2, 256)), ("dist", (384,)), ("dd", (2, 160)), ("sd", (2, 160)),
                     ("ptd", (2, 2 * P)), ("osb", (512,)), ("st_in", (512,)), ("stc", (4, 36)), ("st_out", (512,)),
                     ("wg", (8, P)), ("st", (4, 40)), ("sp", (8, 4)), ("sink", (25,)), ("sm", (8, 16))])
        OD, _ = cut([("qk", (2, 3, 4 * NT)), ("v", (3, 3, 512)), ("work", (5380,))])
        OD["q"] = OD["qk"][:, 0].rearrange("p g (i t) -> p g i t", t=NT)
        OD["k"] = OD["qk"][:, 1].rearrange("p g (i t) -> p g i t", t=NT)
        MO, _ = cut([("acc", (NC, NT)), ("z", (D,)), ("xg", (NC, P)), ("y", (D,)), ("h", (2, 2, CAP)),
                     ("sg", (2, 2, CAP)), ("pgt", (2, NT)), ("pm", (2, 3, P)), ("pg", (2, 3, P)),
                     ("wr", (NC, NE)), ("rb", (NE,)), ("scores", (3, NE)), ("biased", (3, NE)), ("top", (24, 8)),
                     ("gs", (3, 8)), ("gt", (3, 64)), ("eq", (3, 64)), ("rank", (3, 8)), ("t8", (3, 8)),
                     ("rep", (3, NE)), ("sel", (3, NE)), ("gate", (3, NE)), ("pos", (3, NE)), ("cnt", (16,)), ("cur", (2, CAP + 12)),
                     ("sh", (2, NT)), ("shg", (2, NT))])
        n_iter = sb("n_iter", [P, 1], I32)

        s_const = sem("s_const")
        s_x = sem("s_x")
        s_pad = sem("s_pad")
        s_ring = [[sem(f"s_ring_{layer}_{s}") for s in range(RING)] for layer in range(2)]
        s_free = [[sem(f"s_free_{layer}_{s}") for s in range(RING)] for layer in range(2)]
        EXP0 = (6, 16)
        SHARED = (5, 15)
        n_dma = [{0: 1, 1: 9, 2: 1, 3: 3, 4: 3, 5: 3},
                 {**{m: 1 for m in range(6)}, **{m: 3 for m in range(6, 14)}, 14: 1, 15: 3}]

        def slot_of(m):
            return m % RING

        def loaded(layer, m):
            return 16 * sum(n for k, n in n_dma[layer].items() if k % RING == m % RING and k <= m)

        def reads_before(layer, m):
            return len([k for k in n_dma[layer] if k % RING == m % RING and k < m])

        static_dma = [[16 * sum(n for k, n in n_dma[layer].items() if k % RING == s) for s in range(RING)]
                      for layer in range(2)]
        static_reads = [[len([k for k in n_dma[layer] if k % RING == s]) for s in range(RING)] for layer in range(2)]

        def wait_slot(eng, layer, m):
            eng.wait_ge(s_ring[layer][slot_of(m)], loaded(layer, m))
            return ring[:, slot_of(m), :]

        def free_slot(ins, layer, m):
            ins.then_inc(s_free[layer][slot_of(m)], 1)

        s_tp = sem("s_tp")
        s_tp_copied = [sem("s_tp_copied_act"), sem("s_tp_copied_dve")]

        def xt_pe(pe, turn):
            for t in range(3):
                if turn == 0:
                    pe.wait_ge(s_x, 16 * 3)
                else:
                    pe.wait_ge(s_xn, 3 * (turn - 1) + t + 1)
                for hf in range(2):
                    n = turn * 3 + t
                    if n:
                        pe.wait_ge(s_tp_copied[hf], n)
                    for j in range(4):
                        c = 4 * hf + j
                        src = x_tok[0:ROWS[t], t, :].rearrange("t (p c) -> t c p", c=NC)[:, c, :]
                        ins = pe.transpose(ps[:, hf, j * P:j * P + ROWS[t]], src, ident[0:ROWS[t], 0:ROWS[t]])
                    ins.then_inc(s_tp, 1)

        def xt_copy(eng, copy, turn, hf):
            for t in range(3):
                eng.wait_ge(s_tp, 2 * (turn * 3 + t) + hf + 1)
                m = ROWS[t]
                src = ps[:, hf, :].rearrange("p (c t) -> p c t", t=P)[:, :, 0:m]
                copy(xT[:, 4 * hf:4 * hf + 4, t * P:t * P + m], src).then_inc(s_tp_copied[hf], 1)

        s_f = sem("s_f")
        s_ln = sem("s_ln")
        s_gb = sem("s_gb")
        s_gb_free = sem("s_gb_free")
        s_xn = sem("s_xn")
        s_var = sem("s_var")
        s_rstd = sem("s_rstd")
        ln = {"n": 0}

        def ln_act(act, turn):
            for t in range(3):
                act.wait_ge(s_var, 3 * turn + t + 1)
                st = stats[0:ROWS[t], t, :]
                act.activation(st[:, 14:15], st[:, 13:14], ACT.Sqrt).then_inc(s_rstd, 1)

        def ln_dve(v, turn, permuted):
            z = MO["z"]
            def step(ins):
                ln["n"] += 1
                ins.then_inc(s_ln, 1)
                v.wait_ge(s_ln, ln["n"])
            for t in range(3):
                m = ROWS[t]
                v.wait_ge(s_f, 3 * turn + t + 1)
                if permuted:
                    for hf in range(2):
                        f = ps[0:m, 2 * t + hf, :].rearrange("t (c p) -> t p c", c=4)
                        xin = x_tok[0:m, t, :].rearrange("t (p h c) -> t h p c", h=2, c=4)[:, hf]
                        zo = z[0:m, :].rearrange("t (p h c) -> t h p c", h=2, c=4)[:, hf]
                        ins = v.scalar_tensor_tensor(out=zo, in0=xin, scalar=ALPHA, in1=f, op0=ALU.mult, op1=ALU.add)
                        ins.then_inc(s_ln, 1)
                    ln["n"] += 2
                    v.wait_ge(s_ln, ln["n"])
                else:
                    for hf in range(2):
                        ins = v.scalar_tensor_tensor(out=z[0:m, hf * BANK:(hf + 1) * BANK],
                                                     in0=x_tok[0:m, t, hf * BANK:(hf + 1) * BANK], scalar=ALPHA,
                                                     in1=ps[0:m, 2 * t + hf, :], op0=ALU.mult, op1=ALU.add)
                        ins.then_inc(s_ln, 1)
                    ln["n"] += 2
                    v.wait_ge(s_ln, ln["n"])
                st = stats[0:m, t, :]
                for hf in range(2):
                    ins = v.bn_stats(st[:, 6 * hf:6 * hf + 6], z[0:m, hf * BANK:(hf + 1) * BANK])
                    ins.then_inc(s_ln, 1)
                ln["n"] += 2
                v.wait_ge(s_ln, ln["n"])
                step(v.bn_aggr(st[:, 12:14], st[:, 0:12]))
                step(v.tensor_scalar(st[:, 13:14], st[:, 13:14], EPS, None, ALU.add))
                v.sem_inc(s_var, 1)
                v.wait_ge(s_rstd, 3 * turn + t + 1)
                step(v.reciprocal(st[:, 14:15], st[:, 14:15]))
                step(v.tensor_scalar(z[0:m, :], z[0:m, :], st[:, 12:13], st[:, 14:15], ALU.subtract, ALU.mult))
                v.wait_ge(s_gb, 32 * (turn + 1))
                step(v.tensor_tensor(z[0:m, :], z[0:m, :], gb[0:m, 0, :], ALU.mult))
                step(v.tensor_tensor(x_tok[0:m, t, :], z[0:m, :], gb[0:m, 1, :], ALU.add))
                v.sem_inc(s_xn, 1)
            v.sem_inc(s_gb_free, 1)

        s_ep = sem("s_ep")
        s_ep_copied = [sem("s_ep_copied_act"), sem("s_ep_copied_dve")]
        s_ev_in = sem("s_ev_in")
        s_ev_par = sem("s_ev_par")
        s_wg0 = sem("s_wg0")
        s_wg = sem("s_wg")
        s_arg = sem("s_arg")
        s_root = sem("s_root")
        s_st = sem("s_st")
        s_xr = sem("s_xr")
        s_conv = sem("s_conv")
        s_gate = sem("s_gate")
        s_gate_act = sem("s_gate_act")
        s_lru = sem("s_lru")
        s_lru_act = sem("s_lru_act")
        s_aout = sem("s_aout")
        s_so = sem("s_so")
        s_so_copied = sem("s_so_copied")
        s_kvt = sem("s_kvt")
        s_kvt_copied = sem("s_kvt_copied")
        s_qz = sem("s_qz")
        s_kd = sem("s_kd")
        s_kd_copied = sem("s_kd_copied")
        s_sd = sem("s_sd")
        s_sd_dve = sem("s_sd_dve")
        s_sd_exp = sem("s_sd_exp")
        s_ptd = sem("s_ptd")
        s_ptd_copied = sem("s_ptd_copied")
        s_od = sem("s_od")
        s_mix = [sem("s_mix_0"), sem("s_mix_1")]
        s_sout = sem("s_sout")
        q0, k0, v0 = D, D + 512, D + 640
        ACT_TILES, DVE_TILES = range(4, 14), range(4)

        def copied_value(k):
            return (s_ep_copied[0], k - 4 + 1) if k >= 4 else (s_ep_copied[1], k + 1)

        def ev_proj_pe(pe):
            pe.wait_ge(s_tp_copied[0], 3)
            pe.wait_ge(s_tp_copied[1], 3)
            for k in range(14):
                m = k // 6
                w = wait_slot(pe, 0, m)
                w = w[:, 0:NC * min(768, EV_COLS - 768 * m)].rearrange("p (c n) -> p c n", c=NC)
                if k >= 4:
                    pe.wait_ge(*copied_value(k - 4))
                bank = 2 + k % 4
                for c in range(NC):
                    lhs = w[:, c, k * P - 768 * m:(k + 1) * P - 768 * m]
                    ins = pe.matmul(ps[:, bank, 0:NT], lhs, xT[:, c, 0:NT], start=c == 0, stop=c == NC - 1)
                ins.then_inc(s_ep, 1)
                if k % 6 == 5 or k == 13:
                    pe.wait_ge(s_ep, k + 1)
                    pe.sem_inc(s_free[0][slot_of(m)], 1)

        def ev_xr_dst(j):
            samp = EV["xr"][:, j, SAMP0:XRW].rearrange("p (b s) -> p b s", s=SEQ_S)
            return EV["xr"][:, j, CONVW - 1:CONVW - 1 + NPR], samp
        def ev_proj_act(act):
            for k in ACT_TILES:
                act.wait_ge(s_ep, k + 1)
                src = ps[:, 2 + k % 4, 0:NT]
                if k < 8:
                    ins = act.activation(EV["gel"][:, k - 4, :], src, ACT.Gelu_apprx_tanh)
                else:
                    dst = EV["q"][:, k - 8, :] if k < 12 else EV["kv"][:, k - 12, :]
                    ins = act.activation(dst, src, ACT.Copy)
                ins.then_inc(s_ep_copied[0], 1)

        lru = {}

        def ev_proj_dve(v):
            ch = lru["chain"] = Chain(v, s_lru)
            ch(v.memset(EV["xr"][:, :, 0:CONVW - 1], 0.0))
            for k in DVE_TILES:
                v.wait_ge(s_ep, k + 1)
                prompt, samp = ev_xr_dst(k)
                ch(v.tensor_copy(prompt, ps[:, 2 + k, 0:NPR]))
                v.tensor_copy(samp[:, :, CONVW - 1:SEQ_S],
                              ps[:, 2 + k, NPR:NT].rearrange("p (b s) -> p b s", s=TS)).then_inc(s_ep_copied[1], 1)
            v.wait_ge(s_st, 1)
            st = EV["st"]
            ch(v.tensor_copy(st, ps[:, 6, 0:160].rearrange("p (j n) -> p j n", n=40)))
            for j in range(LRU_TILES):
                _, samp = ev_xr_dst(j)
                ch(v.tensor_copy(samp[:, :, 0:CONVW - 1], st[:, j, 0:24].rearrange("p (b s) -> p b s", s=CONVW - 1)))
            v.wait_ge(s_ep_copied[1], 4)

            lam, sp = st[:, :, 39], EV["sp"]
            ch(v.scalar_tensor_tensor(out=sp[:, 0, :], in0=lam, scalar=-1.0, in1=lam, op0=ALU.mult, op1=ALU.max))
            v.sem_inc(s_xr, 1)
            v.wait_ge(s_lru_act, 1)
            ch(v.tensor_scalar(sp[:, 2, :], sp[:, 1, :], 2.0, None, ALU.add))
            ch(v.reciprocal(sp[:, 3, :], sp[:, 2, :]))
            ch(v.tensor_tensor(sp[:, 2, :], sp[:, 1, :], sp[:, 3, :], ALU.mult))
            ch(v.tensor_tensor(sp[:, 3, :], sp[:, 2, :], sp[:, 2, :], ALU.mult))
            ch(v.tensor_scalar(sp[:, 4, :], sp[:, 3, :], 1 / 19, 1 / 17, ALU.mult, ALU.add))
            for n in range(15, 0, -2):
                ch(v.tensor_tensor(sp[:, 4, :], sp[:, 4, :], sp[:, 3, :], ALU.mult))
                ch(v.tensor_scalar(sp[:, 4, :], sp[:, 4, :], 1 / n, None, ALU.add))
            ch(v.scalar_tensor_tensor(out=sp[:, 4, :], in0=sp[:, 2, :], scalar=2.0, in1=sp[:, 4, :], op0=ALU.mult,
                                      op1=ALU.mult))
            ch(v.tensor_scalar(sp[:, 5, :], lam, -1.0, 0.0, ALU.mult, ALU.max))
            ch(v.tensor_tensor(sp[:, 5, :], sp[:, 5, :], sp[:, 4, :], ALU.add))
            ch(v.tensor_scalar(sp[:, 6, :], sp[:, 5, :], 8.0, None, ALU.mult))
            ch(v.tensor_scalar(sp[:, 7, :], sp[:, 5, :], -8.0, None, ALU.mult))

        def ev_lru_dve(v):
            ch, st = lru["chain"], EV["st"]
            xr, xc = EV["xr"], EV["xc"]
            for j in range(LRU_TILES):
                ch(v.tensor_scalar(xc[:, j, :], xr[:, j, 0:CW], st[:, j, 32:33], st[:, j, 36:37], ALU.mult, ALU.add))
                for tap in range(1, CONVW):
                    ch(v.scalar_tensor_tensor(out=xc[:, j, :], in0=xr[:, j, tap:tap + CW],
                                              scalar=st[:, j, 32 + tap:33 + tap], in1=xc[:, j, :],
                                              op0=ALU.mult, op1=ALU.add))
                v.sem_inc(s_conv, 1)

            def scan_input(j):
                v.wait_ge(s_lru_act, 1 + LRU_TILES + j + 1)
                aa, rg, ig = xT[:, j, 0:CW], EV["rg"][:, j, :], EV["ig"][:, j, :]
                ch(v.tensor_tensor(ig, ig, xc[:, j, :], ALU.mult))
                ch(v.tensor_tensor(xc[:, j, :], aa, aa, ALU.mult))
                ch(v.scalar_tensor_tensor(out=rg, in0=xc[:, j, :], scalar=1.0, in1=rg, op0=ALU.add, op1=ALU.mult))
                v.sem_inc(s_arg, 1)

            def scan(j):
                aa, rg, ig = xT[:, j, 0:CW], EV["rg"][:, j, :], EV["ig"][:, j, :]
                v.wait_ge(s_root, j + 1)
                ch(v.tensor_tensor(ig, ig, rg, ALU.mult))
                first = slice(SAMP0 - 1, SAMP0 - 1 + SEQ_S * (NB - 1) + 1, SEQ_S)
                ch(v.memset(aa[:, first], 0.0))
                ch(v.tensor_copy(ig[:, first], st[:, j, 24:32]))
                ch(v.tensor_tensor_scan(xc[:, j, :], aa, ig, 0.0, ALU.mult, ALU.add))
                gel = EV["gel"][:, j, :]
                v.wait_ge(s_ep_copied[0], j + 1)
                ch(v.tensor_tensor(mixT[:, j, 0:NPR], xc[:, j, 0:NPR], gel[:, 0:NPR], ALU.mult))
                samp = EV["xc"].rearrange("p j n -> p (j n)")[:, j * CW + SAMP0:j * CW + SAMP0 + (NB - 1) * SEQ_S]
                dst = mixT[:, j, NPR:NT].rearrange("p (b s) -> p b s", s=TS)
                g3 = gel[:, NPR:NT].rearrange("p (b s) -> p b s", s=TS)
                ch(v.tensor_tensor(dst[:, 0:NB - 1], samp.rearrange("p (b s) -> p b s", s=SEQ_S)[:, :, 0:TS],
                                   g3[:, 0:NB - 1], ALU.mult))
                last = SAMP0 + (NB - 1) * SEQ_S
                ch(v.tensor_tensor(dst[:, NB - 1], xc[:, j, last:last + TS], g3[:, NB - 1], ALU.mult))

            scan_input(0)
            for j in range(LRU_TILES):
                if j + 1 < LRU_TILES:
                    scan_input(j + 1)
                scan(j)
            stc = EV["stc"]
            ch(v.tensor_copy(stc[:, :, 0:1], xc[:, :, NPR - 1:NPR]))
            ch(v.tensor_copy(stc[:, :, 1:9], xc[:, :, SAMP0 + TS - 1:SAMP0 + TS + SEQ_S * (NB - 1):SEQ_S]))
            ch(v.tensor_copy(stc[:, :, 9:12], xr[:, :, NPR:NPR + 3]))
            for j in range(LRU_TILES):
                _, samp = ev_xr_dst(j)
                ch(v.tensor_copy(stc[:, j, 12:36].rearrange("p (b s) -> p b s", s=3), samp[:, :, TS:SEQ_S]))
            v.sem_inc(s_aout, 1)

        def ev_lru_act(act):
            sp, st = EV["sp"], EV["st"]
            act.wait_ge(s_xr, 1)
            act.activation(sp[:, 1, :], sp[:, 0, :], ACT.Exp, scale=-1.0).then_inc(s_lru_act, 1)
            for n in range(8):
                j = n // 2
                act.wait_ge(s_gate, n + 1)
                dst = EV["ig"] if n % 2 else EV["rg"]
                act.activation(dst[:, j, :], ps[:, n % 4, 0:CW], ACT.Sigmoid,
                               bias=st[:, j, 37 + n % 2:38 + n % 2]).then_inc(s_gate_act, 1)
            act.wait_ge(s_gate_act, 8)
            act.wait_ge(s_ep, 14)
            for j in range(LRU_TILES):
                act.activation(xT[:, j, 0:CW], EV["rg"][:, j, :], ACT.Exp,
                               scale=sp[:, 7, j:j + 1]).then_inc(s_lru_act, 1)
            act.wait_ge(s_lru_act, 1 + LRU_TILES)
            for j in range(LRU_TILES):
                act.activation(EV["rg"][:, j, :], EV["rg"][:, j, :], ACT.Tanh,
                               scale=sp[:, 6, j:j + 1]).then_inc(s_lru_act, 1)
            for j in range(LRU_TILES):
                act.wait_ge(s_arg, j + 1)
                act.activation(EV["rg"][:, j, :], EV["rg"][:, j, :], ACT.Sqrt).then_inc(s_root, 1)

        def ev_state_pe(pe):
            pe.wait_ge(s_ev_par, 16 * 7)
            for j in range(4):
                ins = pe.transpose(ps[:, 6, 40 * j:40 * j + 40], EV["st_in"][0:40, j * P:(j + 1) * P], ident[0:40, 0:40])
            ins.then_inc(s_st, 1)

        def ev_gate_pe(pe):
            pe.wait_ge(s_wg, 16 * 4)
            for n in range(8):
                j = n // 2
                pe.wait_ge(s_conv, j + 1)
                if n >= 4:
                    pe.wait_ge(s_gate_act, n - 3)
                pe.matmul(ps[:, n % 4, 0:CW], EV["wg"][:, n, :], EV["xc"][:, j, :], start=True,
                          stop=True).then_inc(s_gate, 1)

        def ev_state_out_pe(pe):
            pe.wait_ge(s_aout, 1)
            pe.wait_ge(s_kvt_copied, 2)
            for j in range(4):
                ins = pe.transpose(ps[0:36, 7, j * P:(j + 1) * P], EV["stc"][:, j, :], ident)
            ins.then_inc(s_so, 1)

        def ev_kvt_pe(pe):
            pe.wait_ge(s_ep_copied[0], 10)
            pe.wait_ge(s_lru, 7)
            for kind, bank in ((1, 6), (0, 7)):
                for t in range(3):
                    m = ROWS[t]
                    ins = pe.transpose(ps[0:m, bank, t * P:(t + 1) * P], EV["kv"][:, kind, t * P:t * P + m], ident)
                ins.then_inc(s_kvt, 1)

        def ev_kvt_act(act):
            for n, (dst, bank) in enumerate((("vtok", 6), ("ktok", 7))):
                act.wait_ge(s_kvt, n + 1)
                act.activation(EV[dst][:, 0:2, :], ps[:, bank, 0:2 * P].rearrange("p (t n) -> p t n", n=P), ACT.Copy)
                act.activation(EV[dst][0:NSA, 2, :], ps[0:NSA, bank, 2 * P:3 * P], ACT.Copy).then_inc(s_kvt_copied, 1)

        s_s = sem("s_s")
        s_sp = sem("s_sp")
        s_mx = sem("s_mx")
        s_nb = sem("s_nb")
        s_exp = sem("s_exp")
        s_pt = sem("s_pt")
        s_ptc = sem("s_ptc")
        s_pv = sem("s_pv")
        s_den = per_layer("s_den")
        s_sinkx = sem("s_sinkx")
        s_oc = sem("s_oc")
        s_ot = sem("s_ot")
        s_otc = sem("s_otc")

        class Prompt:
            def __init__(self, layer, groups, s, pt, osb, sm, dist, score, value, out_col):
                self.layer, self.groups, self.s, self.pt, self.osb = layer, groups, s, pt, osb
                self.sm, self.dist, self.score, self.value, self.out_col = sm, dist, score, value, out_col

            def width(self, qb):
                return self.groups * P * (qb + 1)

        def banks(first, width):
            return ps[:, first:first + 2, :].rearrange("p b n -> p (b n)")[:, 0:width]

        def prompt_pe(pe, c):
            L = c.layer

            def scores(n):
                qb, h = divmod(n, NH)
                if n >= 2:
                    pe.wait_ge(s_sp, 16 * L + n - 1)
                for g in range(c.groups):
                    nk = P * (qb + 1)
                    lhs, rhs = c.score(g, h, qb)
                    ins = pe.matmul(banks(2 * (n % 2), 2 * BANK)[:, g * nk:(g + 1) * nk], lhs, rhs, start=True, stop=True)
                ins.then_inc(s_s, 1)

            def weights_t(n):
                qb = n // NH
                pe.wait_ge(s_exp, 16 * L + n + 1)
                if n:
                    pe.wait_ge(s_ptc, 16 * L + n)
                for u in range(c.groups * (qb + 1)):
                    ins = pe.transpose(banks(4, 2 * BANK)[:, u * P:(u + 1) * P], c.s[:, n % 2, u * P:(u + 1) * P], ident)
                ins.then_inc(s_pt, 1)

            def values(n):
                qb, h = divmod(n, NH)
                pe.wait_ge(s_ptc, 16 * L + n + 1)
                if h == 0 and qb:
                    pe.wait_ge(s_oc, 2 * L + qb)
                units = c.groups * (qb + 1)
                col = c.out_col(h)
                for u in range(units):
                    g, kb = divmod(u, qb + 1)
                    ins = pe.matmul(ps[:, 6, col:col + HD], c.pt[:, n % 2, u * P:(u + 1) * P], c.value(g, h, kb),
                                    start=u == 0, stop=u == units - 1)
                ins.then_inc(s_pv, 1)

            def turn(qb):
                pe.wait_ge(s_oc, 2 * L + qb + 1)
                if qb:
                    pe.wait_ge(s_otc, 2 * L + qb)
                for i in range(4):
                    ins = pe.transpose(ps[:, 7, i * P:(i + 1) * P], c.osb[:, i * P:(i + 1) * P], ident)
                ins.then_inc(s_ot, 1)

            scores(0)
            for n in range(2 * NH):
                if n + 1 < 2 * NH:
                    scores(n + 1)
                weights_t(n)
                if n:
                    values(n - 1)
                if n == NH + 1:
                    turn(0)
            values(2 * NH - 1)
            turn(1)

        def prompt_dve(v, c):
            L = c.layer
            mx, nb, den, rin, snb, sx = (c.sm[:, i, :] for i in range(6))
            ch = Chain(v, s_den[L])

            def finish(qb):
                cols = slice(NH * qb, NH * qb + NH)
                v.wait_ge(s_exp, 16 * L + NH * (qb + 1))
                if L == 0:
                    ch(v.tensor_tensor(snb[:, cols], nb[:, cols], EV["sink"][:, 0:NH], ALU.add))
                    v.wait_ge(s_sinkx, qb + 1)
                    ch(v.tensor_tensor(den[:, cols], den[:, cols], sx[:, cols], ALU.add))
                ch(v.reciprocal(rin[:, cols], den[:, cols]))
                v.wait_ge(s_pv, 16 * L + NH * (qb + 1))
                if qb:
                    v.wait_ge(s_ot, 2 * L + qb)
                scale = rin[:, cols]
                if L == 0:
                    scale = scale.rearrange("p (s i) -> p i s", s=2)
                    dst = c.osb.rearrange("p (i s d) -> p i s d", i=4, s=2)
                    src = ps[:, 6, :].rearrange("p (i s d) -> p i s d", i=4, s=2)
                    scale = scale.unsqueeze(3).broadcast_to([P, 4, 2, HD])
                else:
                    dst = c.osb.rearrange("p (h d) -> p h d", h=NH)
                    src = ps[:, 6, :].rearrange("p (h d) -> p h d", h=NH)
                    scale = scale.unsqueeze(2).broadcast_to([P, NH, HD])
                v.tensor_tensor(dst, src, scale, ALU.mult).then_inc(s_oc, 1)

            for n in range(2 * NH):
                qb, h = divmod(n, NH)
                w = c.width(qb)
                v.wait_ge(s_s, 16 * L + n + 1)
                if n >= 2:
                    v.wait_ge(s_pt, 16 * L + n - 1)
                v.scalar_tensor_tensor(out=c.s[:, n % 2, 0:w], in0=c.dist[qb], scalar=slope8(h),
                                       in1=banks(2 * (n % 2), w), op0=ALU.mult, op1=ALU.add).then_inc(s_sp, 1)
                v.wait_ge(s_sp, 16 * L + n + 1)
                v.tensor_reduce(mx[:, n:n + 1], c.s[:, n % 2, 0:w], AX.X, ALU.max).then_inc(s_mx, 1)
                v.wait_ge(s_mx, 16 * L + n + 1)
                if L == 0:
                    ins = v.tensor_scalar(nb[:, n:n + 1], mx[:, n:n + 1], -SCALE, EV["sink"][:, NH + h:NH + h + 1],
                                          ALU.mult, ALU.min)
                else:
                    ins = v.tensor_scalar(nb[:, n:n + 1], mx[:, n:n + 1], -SCALE, None, ALU.mult)
                ins.then_inc(s_nb, 1)
                if n == NH + 1:
                    finish(0)
            finish(1)

        def prompt_act(act, c):
            L = c.layer
            mx, nb, den, rin, snb, sx = (c.sm[:, i, :] for i in range(6))

            def exps(n):
                w = c.width(n // NH)
                act.wait_ge(s_nb, 16 * L + n + 1)
                act.activation(c.s[:, n % 2, 0:w], c.s[:, n % 2, 0:w], ACT.Exp, bias=nb[:, n:n + 1], scale=SCALE,
                               accum_out=den[:, n:n + 1]).then_inc(s_exp, 1)

            def copy(n):
                w = c.width(n // NH)
                act.wait_ge(s_pt, 16 * L + n + 1)
                if n >= 2:
                    act.wait_ge(s_pv, 16 * L + n - 1)
                act.activation(c.pt[:, n % 2, 0:w], banks(4, w), ACT.Copy).then_inc(s_ptc, 1)

            def sinks(qb):
                if L == 0:
                    cols = slice(NH * qb, NH * qb + NH)
                    act.wait_ge(s_den[L], 1 + 3 * qb)
                    act.activation(sx[:, cols], snb[:, cols], ACT.Exp).then_inc(s_sinkx, 1)

            def turned(qb):
                act.wait_ge(s_ot, 2 * L + qb + 1)
                tile0 = 4 if L == 0 else 0
                act.activation(mixT[:, tile0:tile0 + 4, qb * P:(qb + 1) * P],
                               ps[:, 7, :].rearrange("p (i t) -> p i t", i=4), ACT.Copy).then_inc(s_otc, 1)

            exps(0)
            for n in range(2 * NH):
                if n == NH + 1:
                    sinks(0)
                if n + 1 < 2 * NH:
                    exps(n + 1)
                copy(n)
                if n == NH + 1:
                    turned(0)
            sinks(1)
            turned(1)

        s_cache = sem("s_cache")

        def ev_dec_qz(eng_copy, v):
            qz = EV["qz"].rearrange("p b (h t) -> p h b t", h=NH)
            ch = lru["chain"]
            ch(v.memset(EV["qz"], 0.0))
            v.wait_ge(s_ep_copied[0], 10)
            src = EV["q"][:, :, NPR:NT].rearrange("p i (b t) -> p i b t", t=TS)
            for s in range(2):
                rows = slice(HD * s, HD * s + HD)
                for i in range(4):
                    ch(v.tensor_copy(qz[rows, 4 * s + i], src[rows, i]))
            v.sem_inc(s_qz, 1)

        def ev_dec_pe(pe):
            pe.wait_ge(s_cache, 16)
            pe.wait_ge(s_ptc, 2 * NH)
            cache = gb.rearrange("p a n -> p (a n)").rearrange("p (b n) -> p b n", b=NB)
            for b in range(NB):
                ins = pe.transpose(ps[:, 4 + b // 4, (b % 4) * P:(b % 4 + 1) * P], cache[:, b, 0:P], ident)
                if b % 4 == 3:
                    ins.then_inc(s_kd, 1)
            pe.wait_ge(s_sp, 2 * NH)
            pe.wait_ge(s_qz, 1)
            for g in range(2):
                pe.wait_ge(s_kd_copied, g + 1)
                for bb in range(4):
                    b = 4 * g + bb
                    rows = slice(32 * bb, 32 * bb + 32)
                    pe.matmul(ps[rows, g, 0:P], EV["qz"][:, b, :], EV["ktd"][:, b, :], start=True, stop=True)
                    ins = pe.matmul(ps[rows, g, P:P + NSA], EV["qz"][:, b, :], EV["kv"][:, 0, NPR:NT], start=True,
                                    stop=True)
                ins.then_inc(s_sd, 1)
            for g in range(2):
                pe.wait_ge(s_sd_dve, 7 * g + 7)
                pe.transpose(ps[:, g, 0:P], EV["sd"][:, g, 0:P], ident)
                pe.transpose(ps[0:NSA, g, P:2 * P], EV["sd"][:, g, P:P + NSA],
                             ident).then_inc(s_ptd, 1)
            pe.wait_ge(s_kvt_copied, 1)
            for g in range(2):
                pe.wait_ge(s_ptd_copied, 2 * g + 2)
                for bb in range(4):
                    b = 4 * g + bb
                    out = ps[:, 3, b * 32:b * 32 + 32]
                    rhs = EV["ptd"][:, g, :].rearrange("p (k r) -> p k r", k=2)
                    pe.matmul(out, cache[:, b, P:2 * P], rhs[:, 0, 32 * bb:32 * bb + 32], start=True, stop=False)
                    ins = pe.matmul(out, EV["vtok"][0:NSA, 2, :], rhs[0:NSA, 1, 32 * bb:32 * bb + 32], start=False,
                                    stop=True)
            ins.then_inc(s_od, 1)

        def ev_dec_dve(v):
            dm, sm = EV["sd"], EV["sm"][:, 6, :]
            steps = 0
            for g in range(2):
                v.wait_ge(s_kd, g + 1)
                v.tensor_copy(EV["ktd"][:, 4 * g:4 * g + 4, :],
                              ps[:, 4 + g, :].rearrange("p (b n) -> p b n", b=4)).then_inc(s_kd_copied, 1)

            def step(ins):
                nonlocal steps
                steps += 1
                ins.then_inc(s_sd_dve, 1)
                v.wait_ge(s_sd_dve, steps)
            row_sink = EV["sink"][:, 24:25]
            for g in range(2):
                v.wait_ge(s_sd, g + 1)
                c = lambda k: sm[:, 8 * g + k:8 * g + k + 1]
                step(v.scalar_tensor_tensor(out=dm[:, g, :], in0=EV["dd"][:, g, :], scalar=row_slope,
                                            in1=ps[:, g, 0:160], op0=ALU.mult, op1=ALU.add))
                step(v.tensor_reduce(c(0), dm[:, g, :], AX.X, ALU.max))
                step(v.tensor_scalar(c(1), c(0), SCALE, row_sink, ALU.mult, ALU.max))
                step(v.tensor_scalar(c(2), c(1), -1.0, None, ALU.mult))
                v.wait_ge(s_sd_exp, 2 * g + 2)
                step(v.tensor_scalar(c(5), c(3), c(4), None, ALU.add))
                step(v.reciprocal(c(6), c(5)))
                step(v.tensor_scalar(dm[:, g, :], dm[:, g, :], c(6), None, ALU.mult))
            v.wait_ge(s_od, 1)
            src = ps[:, 3, 0:256].rearrange("p (b h t) -> p b h t", h=NH, t=TS)
            for s in range(2):
                rows = slice(HD * s, HD * s + HD)
                for i in range(4):
                    dst = mixT[rows, 4 + i, NPR:NT].rearrange("p (b t) -> p b t", t=TS)
                    v.tensor_copy(dst, src[rows, :, 4 * s + i, :]).then_inc(s_mix[0], 1)

        def ev_dec_act(act):
            sm = EV["sm"][:, 6, :]
            for g in range(2):
                c = lambda k: sm[:, 8 * g + k:8 * g + k + 1]
                act.wait_ge(s_sd_dve, 7 * g + 4)
                act.activation(EV["sd"][:, g, :], EV["sd"][:, g, :], ACT.Exp, bias=c(2), scale=SCALE,
                               accum_out=c(3)).then_inc(s_sd_exp, 1)
                act.activation(c(4), EV["sink"][:, 24:25], ACT.Exp, bias=c(2)).then_inc(s_sd_exp, 1)
            for g in range(2):
                act.wait_ge(s_ptd, g + 1)
                act.activation(EV["ptd"][:, g, 0:P], ps[:, g, 0:P], ACT.Copy).then_inc(s_ptd_copied, 1)
                act.activation(EV["ptd"][0:NSA, g, P:2 * P], ps[0:NSA, g, P:2 * P],
                               ACT.Copy).then_inc(s_ptd_copied, 1)

        s_mid = sem("s_mid")

        def out_proj_pe(pe, layer, tiles, loads):
            for hf, m in enumerate(loads):
                w = wait_slot(pe, layer, m)
                n = tiles * BANK
                for t in range(3):
                    rows = ROWS[t]
                    for j in range(tiles):
                        if len(loads) == 2:
                            rhs = w[:, j * BANK:(j + 1) * BANK]
                            outs = ((hf, rhs),)
                        else:
                            outs = tuple((x, w[:, j * D + x * BANK:j * D + (x + 1) * BANK]) for x in range(2))
                        for x, rhs in outs:
                            ins = pe.matmul(ps[0:rows, 2 * t + x, :], mixT[:, j, t * P:t * P + rows], rhs,
                                            start=j == 0, stop=j == tiles - 1)
                    if hf == len(loads) - 1:
                        ins.then_inc(s_f, 1)
                    elif t == 2:
                        ins.then_inc(s_mid, 1)
                if hf < len(loads) - 1:
                    pe.wait_ge(s_mid, 1)
                else:
                    pe.wait_ge(s_f, 6 * layer + 3)
                pe.sem_inc(s_free[layer][slot_of(m)], 1)

        s_wr = sem("s_wr")
        s_lg = sem("s_lg")
        s_sc = sem("s_sc")
        s_rt = per_layer("s_rt")
        s_sel = sem("s_sel")
        s_ps = sem("s_ps")
        s_disp = sem("s_disp")
        s_sgu = sem("s_sgu")
        s_sact = sem("s_sact")
        s_sh = sem("s_sh")
        s_sy = sem("s_sy")
        s_acc0 = sem("s_acc0")
        s_cur = per_layer("s_cur")
        s_pm = per_layer("s_pm")
        s_ga = per_layer("s_ga")
        s_pgt = per_layer("s_pgt")
        s_pgtc = per_layer("s_pgtc")
        s_xg = per_layer("s_xg")
        s_xgv = per_layer("s_xgv")
        s_gu = per_layer("s_gu")
        s_si = per_layer("s_si")
        s_h2 = per_layer("s_h2")
        s_dn = per_layer("s_dn")
        s_yc = per_layer("s_yc")
        s_scat = per_layer("s_scat")
        s_add = per_layer("s_add")
        s_moe = sem("s_moe")

        def iterations(eng):
            return eng.value_load(n_iter[0:1, 0:1], min_val=NE // 4 - 1, max_val=PASSES * NE // 4 - 1)

        def moe_route_pe(pe, L):
            pe.wait_ge(s_tp_copied[0], 3 * (2 * L + 2))
            pe.wait_ge(s_tp_copied[1], 3 * (2 * L + 2))
            pe.wait_ge(s_wr, 32 * (L + 1))
            for t in range(3):
                for c in range(NC):
                    ins = pe.matmul(ps[:, 2, t * NE:(t + 1) * NE], xT[:, c, t * P:(t + 1) * P], MO["wr"][:, c, :],
                                    start=c == 0, stop=c == NC - 1)
            ins.then_inc(s_lg, 1)

        def moe_pos_pe(pe, L):
            pe.wait_ge(s_sel, L + 1)
            sel = MO["sel"]
            for t in range(3):
                for u in range(t + 1):
                    ins = pe.matmul(ps[:, 2, t * NE:(t + 1) * NE], tri if u == t else ones, sel[:, u, :],
                                    start=u == 0, stop=u == t)
            for u in range(3):
                ins = pe.matmul(ps[:, 2, 3 * NE:4 * NE], ones, sel[:, u, :], start=u == 0, stop=u == 2)
            ins.then_inc(s_ps, 1)

        def moe_shared_pe(pe, L):
            w = wait_slot(pe, L, SHARED[L])
            wg, wu = (w[:, i * 2048:(i + 1) * 2048].rearrange("p (c n) -> p c n", c=NC) for i in range(2))
            wd = w[:, 4096:6144].rearrange("p (j n) -> p j n", j=2)
            for j in range(2):
                for c in range(NC):
                    pe.matmul(ps[:, 4 + j, 0:NT], wg[:, c, j * P:(j + 1) * P], xT[:, c, 0:NT], start=c == 0,
                              stop=c == NC - 1)
                for c in range(NC):
                    ins = pe.matmul(ps[:, 6 + j, 0:NT], wu[:, c, j * P:(j + 1) * P], xT[:, c, 0:NT], start=c == 0,
                                    stop=c == NC - 1)
                ins.then_inc(s_sgu, 1)

        def moe_shared_down_pe(pe, L):
            w = wait_slot(pe, L, SHARED[L])
            wd = w[:, 4096:6144].rearrange("p (j n) -> p j n", j=2)
            pe.wait_ge(s_sh, 2 * L + 2)
            for c in range(NC):
                if c >= 2:
                    pe.wait_ge(s_acc0, 8 * L + c - 1)
                for j in range(2):
                    lhs = wd[:, j, :].rearrange("p (f c) -> p c f", c=NC)[:, c, :]
                    ins = pe.matmul(ps[:, c % 2, 0:NT], lhs, MO["sh"][:, j, :], start=j == 0, stop=j == 1)
                ins.then_inc(s_sy, 1)
            pe.wait_ge(s_sy, 8 * L + NC)
            pe.sem_inc(s_free[L][slot_of(SHARED[L])], 1)

        route_chain = {}

        def moe_route_dve(v, L):
            ch = route_chain[L] = Chain(v, s_rt[L])
            M = MO
            sc, bi, sel, gate = M["scores"], M["biased"], M["sel"], M["gate"]
            v.wait_ge(s_sc, L + 1)
            v.wait_ge(s_wr, 32 * (L + 1))
            ch(v.tensor_tensor(bi, sc, M["rb"].unsqueeze(1).broadcast_to([P, 3, NE]), ALU.add))
            for n in range(24):
                t, g = divmod(n, 8)
                ins = v.max(M["top"][:, n, :], bi[:, t, g * 8:g * 8 + 8])
            ch(ins)
            ch(v.tensor_tensor(M["gs"], M["top"][:, :, 0].rearrange("p (t g) -> p t g", t=3),
                               M["top"][:, :, 1].rearrange("p (t g) -> p t g", t=3), ALU.add))
            gt = M["gt"].rearrange("p t (g f) -> p t g f", g=8)
            eq = M["eq"].rearrange("p t (g f) -> p t g f", g=8)
            tie = before.rearrange("p (g f) -> p g f", g=8)
            for t in range(3):
                mine = M["gs"][:, t, :].unsqueeze(2).broadcast_to([P, 8, 8])
                other = M["gs"][:, t, :].unsqueeze(1).broadcast_to([P, 8, 8])
                ch(v.tensor_tensor(gt[:, t], other, mine, ALU.is_gt))
                ch(v.tensor_tensor(eq[:, t], other, mine, ALU.is_equal))
                ch(v.tensor_tensor(eq[:, t], eq[:, t], tie, ALU.mult))
            ch(v.tensor_tensor(gt, gt, eq, ALU.add))
            ch(v.tensor_reduce(M["rank"], gt, AX.X, ALU.add))
            keep = M["rank"]
            ch(v.tensor_scalar(keep, keep, 3.5, None, ALU.is_lt))
            kb = keep.unsqueeze(3).broadcast_to([P, 3, 8, 8])
            b4 = bi.rearrange("p t (g f) -> p t g f", g=8)
            ch(v.tensor_tensor(b4, b4, kb, ALU.mult))
            ch(v.tensor_scalar(M["gs"], keep, BIG, -BIG, ALU.mult, ALU.add))
            ch(v.tensor_tensor(b4, b4, M["gs"].unsqueeze(3).broadcast_to([P, 3, 8, 8]), ALU.add))
            for t in range(3):
                ch(v.max(M["t8"][:, t, :], bi[:, t, :]))
                ch(v.match_replace(M["rep"][:, t, :], M["t8"][:, t, :], bi[:, t, :], -3e38))
            ch(v.tensor_tensor(sel, M["rep"], bi, ALU.not_equal))
            ch(v.tensor_tensor(sel, sel, valid.unsqueeze(2).broadcast_to([P, 3, NE]), ALU.mult))
            v.sem_inc(s_sel, 1)
            ch(v.tensor_tensor(gate, sc, sel, ALU.mult))
            sm = M["cnt"]
            ch(v.tensor_reduce(sm[:, 0:3], gate, AX.X, ALU.add))
            ch(v.tensor_tensor(sm[:, 0:3], sm[:, 0:3], invalid, ALU.add))
            ch(v.reciprocal(sm[:, 3:6], sm[:, 0:3]))
            ch(v.tensor_scalar(sm[:, 3:6], sm[:, 3:6], 2.5, None, ALU.mult))
            ch(v.tensor_tensor(gate, gate, sm[:, 3:6].unsqueeze(2).broadcast_to([P, 3, NE]), ALU.mult))

        def moe_pos_dve(v, L):
            M, ch = MO, route_chain[L]
            sm, sel, pos = M["cnt"], M["sel"], M["pos"]
            v.wait_ge(s_ps, L + 1)
            ch(v.scalar_tensor_tensor(out=pos, in0=ps[:, 2, 0:3 * NE].rearrange("p (t e) -> p t e", t=3), scalar=1.0,
                                      in1=sel, op0=ALU.add, op1=ALU.mult))
            ch(v.tensor_scalar(pos, pos, -1.0, None, ALU.add))
            ch(v.tensor_reduce(sm[:, 6:7], ps[:, 2, 3 * NE:4 * NE], AX.X, ALU.max))
            ch(v.tensor_scalar(sm[:, 8:8 + PASSES], thresholds, sm[:, 6:7], None, ALU.is_lt))
            ch(v.tensor_reduce(sm[:, 7:8], sm[:, 8:8 + PASSES], AX.X, ALU.add))
            ch(v.tensor_scalar(sm[:, 7:8], sm[:, 7:8], float(NE // 4), float(NE // 4 - 1), ALU.mult, ALU.add))
            ch(v.tensor_copy(n_iter[:, :], sm[:, 7:8]))
            v.sem_inc(s_disp, 1)

        def moe_shared_dve(v, L):
            for j in range(2):
                v.wait_ge(s_sact, 2 * L + j + 1)
                v.tensor_tensor(MO["sh"][:, j, :], MO["shg"][:, j, :], ps[:, 6 + j, 0:NT], ALU.mult).then_inc(s_sh, 1)

        def moe_shared_acc_act(act, L):
            for c in range(NC):
                act.wait_ge(s_sy, 8 * L + c + 1)
                act.activation(MO["acc"][:, c, :], ps[:, c % 2, 0:NT], ACT.Copy).then_inc(s_acc0, 1)

        def moe_act_head(act, L):
            act.wait_ge(s_lg, L + 1)
            act.activation(MO["scores"], ps[:, 2, 0:3 * NE].rearrange("p (t e) -> p t e", t=3),
                           ACT.Sigmoid).then_inc(s_sc, 1)
            for j in range(2):
                act.wait_ge(s_sgu, 2 * L + j + 1)
                act.activation(MO["shg"][:, j, :], ps[:, 4 + j, 0:NT], ACT.Silu).then_inc(s_sact, 1)

        def moe_pairs_pool(pool, L):
            pool.wait_ge(s_disp, L + 1)
            pool.sem_inc(s_pgt[L], 2)
            cur = MO["cur"]
            column = lambda q, k: cur[:, q, CAP + 6 * k:CAP + 6 * k + 6].rearrange("p (t u) -> p t u", u=2)
            with pool.Fori(0, iterations(pool) + 1) as i:
                for q in range(2):
                    n = 2 * i + q
                    pool.wait_ge(s_pgt[L], n + 1)
                    pool.sem_inc(s_cur[L], 1)
                    e = (i % 16) * 4 + 2 * q
                    slots, pos, gate = cur[:, q, 0:CAP], column(q, 0), column(q, 1)
                    pool.tensor_copy(slots, misc[:, bass.ds(iota0 + (i // 16) * CAP, CAP)]).then_inc(s_cur[L], 1)
                    pool.tensor_copy(pos, MO["pos"][:, :, bass.ds(e, 2)]).then_inc(s_cur[L], 1)
                    pool.tensor_copy(gate, MO["gate"][:, :, bass.ds(e, 2)]).then_inc(s_cur[L], 1)
                    pool.wait_ge(s_cur[L], 5 * n + 4)
                    pool.sem_inc(s_cur[L], 1)
                    for name in ("pm", "pg"):
                        for t in range(3):
                            for u in range(2):
                                out = MO[name][:, q, t, u * CAP:(u + 1) * CAP]
                                if name == "pm":
                                    ins = pool.tensor_scalar(out, slots, pos[:, t, u:u + 1], None, ALU.is_equal)
                                else:
                                    ins = pool.tensor_scalar(out, slots, pos[:, t, u:u + 1], gate[:, t, u:u + 1],
                                                             ALU.is_equal, ALU.mult)
                        ins.then_inc(s_pm[L], 1)

        def gather_pe(pe, L, n, q):
            pe.wait_ge(s_pm[L], 2 * n + 2)
            for c in range(NC):
                for t in range(3):
                    m = ROWS[t]
                    lhs = x_tok[0:m, t, :].rearrange("t (f c) -> t c f", c=NC)[:, c, :]
                    ins = pe.matmul(ps[:, c // 4, (c % 4) * P:(c % 4 + 1) * P], lhs, MO["pm"][0:m, q, t, :],
                                    start=t == 0, stop=t == 2)
                if c == 3:
                    ins.then_inc(s_ga[L], 1)
            ins.then_inc(s_ga[L], 1)

        def turn_pe(pe, L, n, q, first=False):
            if not first:
                pe.wait_ge(s_pgtc[L], n)
            for t in range(3):
                m = ROWS[t]
                ins = pe.transpose(ps[:, 3, t * P:t * P + m], MO["pg"][0:m, q, t, :], ident[0:m, 0:m])
            ins.then_inc(s_pgt[L], 1)

        def up_pe(pe, L, n, q, base):
            pe.wait_ge(s_xg[L], n + 1)
            pe.wait_ge(s_xgv[L], n + 1)
            for u in range(2):
                s = slot_of(EXP0[L] + 2 * q + u)
                pe.wait_ge(s_ring[L][s], base(s, 2 * q + u))
                for tile in range(4):
                    w = ring[:, s, (tile // 2) * 2048:(tile // 2 + 1) * 2048].rearrange("p (c n) -> p c n", c=NC)
                    for c in range(NC):
                        ins = pe.matmul(ps[:, 2, (u * 4 + tile) * CAP:(u * 4 + tile + 1) * CAP],
                                        w[:, c, (tile % 2) * P:(tile % 2 + 1) * P],
                                        MO["xg"][:, c, u * CAP:(u + 1) * CAP], start=c == 0, stop=c == NC - 1)
            ins.then_inc(s_gu[L], 1)

        def down_pe(pe, L, n, q):
            pe.wait_ge(s_h2[L], n + 1)
            for u in range(2):
                w = ring[:, slot_of(EXP0[L] + 2 * q + u), 4096:6144].rearrange("p (j n) -> p j n", j=2)
                for hf in range(2):
                    for j in range(2):
                        ins = pe.matmul(ps[64 * u:64 * u + CAP, 4 + hf, :], MO["h"][:, u, j, :],
                                        w[:, j, hf * BANK:(hf + 1) * BANK], start=j == 0, stop=j == 1)
            ins.then_inc(s_dn[L], 1)

        def scatter_pe(pe, L, n, q):
            pe.wait_ge(s_yc[L], 2 * n + 2)
            pe.wait_ge(s_pgtc[L], n + 1)
            for c in range(NC):
                pe.wait_ge(s_add[L], NC * n + c + NC - 1)
                lhs = MO["y"].rearrange("p (f c) -> p c f", c=NC)[:, c, :]
                pe.matmul(ps[:, 6 + c % 2, 0:NT], lhs, MO["pgt"][:, q, :], start=True, stop=True).then_inc(s_scat[L], 1)

        def over_pairs(eng, L, first, step, last):
            more = iterations(eng)
            first(0, 0, 0)
            with eng.Fori(0, more) as i:
                step(2 * i + 1, 1, i)
                step(2 * i + 2, 0, i + 1)
            step(2 * more + 1, 1, more)
            last(2 * more + 1, 1, more)
            return more

        def moe_pairs_pe(pe, L):
            pe.wait_ge(s_acc0, 8 * L + NC)
            pe.wait_ge(s_disp, L + 1)

            def front(n, q, it):
                gather_pe(pe, L, n, q)
                turn_pe(pe, L, n, q)

            def up(n, q, it):
                up_pe(pe, L, n, q, lambda s, u: static_dma[L][s] + (it + 1) * 48)

            def first(n, q, it):
                front(n, q, it)
                up(n, q, it)

            def step(n, q, it):
                front(n, q, it)
                down_pe(pe, L, n - 1, 1 - q)
                up(n, q, it)
                scatter_pe(pe, L, n - 1, 1 - q)

            def last(n, q, it):
                down_pe(pe, L, n, q)
                scatter_pe(pe, L, n, q)

            over_pairs(pe, L, first, step, last)
            pe.wait_ge(s_moe, L + 1)
            for t in range(3):
                m = ROWS[t]
                for c in range(NC):
                    ins = pe.transpose(ps[0:m, 2 * t + c // 4, (c % 4) * P:(c % 4 + 1) * P],
                                       MO["acc"][:, c, t * P:t * P + m], ident)
                ins.then_inc(s_f, 1)

        def moe_pairs_act(act, L):
            act.wait_ge(s_disp, L + 1)

            def front(n, q, it):
                act.wait_ge(s_ga[L], 2 * n + 1)
                act.activation(MO["xg"][:, 0:4, :], ps[:, 0, :].rearrange("p (c s) -> p c s", c=4),
                               ACT.Copy).then_inc(s_xg[L], 1)
                act.wait_ge(s_pgt[L], n + 3)
                act.activation(MO["pgt"][:, q, :], ps[:, 3, 0:NT], ACT.Copy).then_inc(s_pgtc[L], 1)

            def outputs(n):
                act.wait_ge(s_dn[L], n + 1)
                act.activation(MO["y"][:, 0:BANK], ps[:, 4, :], ACT.Copy).then_inc(s_yc[L], 1)

            def silu(n):
                act.wait_ge(s_gu[L], n + 1)
                act.activation(MO["sg"], ps[:, 2, :].rearrange("p (u k s) -> p u k s", u=2, k=4)[:, :, 0:2, :],
                               ACT.Silu).then_inc(s_si[L], 1)

            def first(n, q, it):
                front(n, q, it)
                silu(n)

            def step(n, q, it):
                front(n, q, it)
                outputs(n - 1)
                silu(n)

            over_pairs(act, L, first, step, lambda n, q, it: outputs(n))

        def moe_pairs_dve(v, L):
            v.wait_ge(s_disp, L + 1)
            v.wait_ge(s_acc0, 8 * L + NC)
            v.sem_inc(s_add[L], NC)

            def front(n):
                v.wait_ge(s_ga[L], 2 * n + 2)
                v.tensor_copy(MO["xg"][:, 4:8, :], ps[:, 1, :].rearrange("p (c s) -> p c s", c=4)).then_inc(s_xgv[L], 1)

            def outputs(n):
                v.wait_ge(s_dn[L], n + 1)
                v.tensor_copy(MO["y"][:, BANK:D], ps[:, 5, :]).then_inc(s_yc[L], 1)

            def hidden(n):
                v.wait_ge(s_si[L], n + 1)
                v.tensor_tensor(MO["h"], MO["sg"], ps[:, 2, :].rearrange("p (u k s) -> p u k s", u=2, k=4)[:, :, 2:4, :],
                                ALU.mult).then_inc(s_h2[L], 1)

            def add(n):
                for c in range(NC):
                    v.wait_ge(s_scat[L], NC * n + c + 1)
                    v.wait_ge(s_add[L], NC * n + c + 1)
                    v.tensor_tensor(MO["acc"][:, c, :], MO["acc"][:, c, :], ps[:, 6 + c % 2, 0:NT],
                                    ALU.add).then_inc(s_add[L], 1)

            def first(n, q, it):
                front(n)
                hidden(n)

            def step(n, q, it):
                front(n)
                outputs(n - 1)
                hidden(n)
                add(n - 1)

            def last(n, q, it):
                outputs(n)
                add(n)

            more = over_pairs(v, L, first, step, last)
            v.wait_ge(s_add[L], more * (2 * NC) + 3 * NC)
            v.sem_inc(s_moe, 1)

        s_op = sem("s_op")
        s_op_copied = [sem("s_op_copied_act"), sem("s_op_copied_dve")]
        s_tk = sem("s_tk")
        s_tk_copied = [sem("s_tk_copied_act"), sem("s_tk_copied_dve")]
        s_kst = [sem("s_kst_0"), sem("s_kst_1")]
        s_dp = sem("s_dp")
        s_qz1 = sem("s_qz1")
        s_g1 = [sem(f"s_g1_{b}") for b in range(4)]
        s_dd1 = sem("s_dd1")
        s_kt = sem("s_kt")
        s_kt_copied = [sem("s_kt_copied_act"), sem("s_kt_copied_dve")]
        s_sd1 = sem("s_sd1")
        s_sm1 = sem("s_sm1")
        s_ex1 = sem("s_ex1")
        s_p1 = sem("s_p1")
        s_p1c = sem("s_p1c")
        s_o1 = sem("s_o1")

        W = OD["work"]
        kst = W[:, 0:3072].rearrange("p (b t n) -> p b t n", b=2, t=3)
        vst = W[:, 3072:3072 + 2304].rearrange("p (b i n) -> p b i n", b=2, i=4)
        OP = {"s": W[:, 0:1536].rearrange("p (b n) -> p b n", b=2), "pt": W[:, 1536:3072].rearrange("p (b n) -> p b n", b=2),
              "osb": W[:, 3072:3584], "dist": W[:, 3584:4736], "sm": W[:, 4736:4864].rearrange("p (k n) -> p k n", k=8)}
        qz1 = W[:, 0:3072].rearrange("p (g i r) -> p g i r", g=3, i=4)
        kns = W[:, 3072:3456].rearrange("p (g i n) -> p g i n", g=3, i=4)
        sm1 = W[:, 3456:3472]
        QK = OD["qk"].rearrange("p a g n -> p (a g n)")
        kt1 = QK[:, 0:3584].rearrange("p (i n) -> p i n", i=4)
        pt1 = QK[:, 3584:4864].rearrange("p (k r) -> p k r", k=10)
        dd1 = QK[:, 4864:4864 + DEC_W]
        xflat = xT[:, :, :].rearrange("p c t -> p (c t)")
        g1c = [xflat[:, 0:D], xflat[:, D:2 * D], xflat[:, 2 * D:3 * D], W[:, 3584:3584 + D]]
        s1 = mixT[:, 4:8, :].rearrange("p j t -> p (j t)")[:, 0:DEC_W]

        def chunk_of(b, ck):
            if ck == 4:
                return g1c[b % 4]
            at = ck * D if ck < 4 else 4 * D + (ck - 5) * D
            return ring[:, slot_of(6 + b), at:at + D]

        def tile_copied(k):
            return s_op_copied[k % 2], k // 2 + 1

        def turn_copied(n):
            return s_tk_copied[n % 2], n // 2 + 1

        def od_proj_pe(pe):
            pe.wait_ge(s_tp_copied[0], 9)
            pe.wait_ge(s_tp_copied[1], 9)
            for k in range(OD_TILES):
                g, kind, i = k // 12, k % 12 // 4, k % 4
                m = k // 6
                w = wait_slot(pe, 1, m).rearrange("p (c n) -> p c n", c=NC)
                if k >= 4:
                    pe.wait_ge(*tile_copied(k - 4))
                for c in range(NC):
                    ins = pe.matmul(ps[:, 2 + k % 4, 0:NT], w[:, c, (k % 6) * P:(k % 6 + 1) * P], xT[:, c, 0:NT],
                                    start=c == 0, stop=c == NC - 1)
                ins.then_inc(s_op, 1)
                if k % 6 == 5:
                    pe.wait_ge(s_op, k + 1)
                    pe.sem_inc(s_free[1][slot_of(m)], 1)
                if k % 12 in (7, 11):
                    pe.wait_ge(*tile_copied(k))
                    pe.wait_ge(*tile_copied(k - 1))
                    for t in range(3):
                        n = (2 * g + (kind == 2)) * 3 + t
                        if n >= 2:
                            pe.wait_ge(*turn_copied(n - 2))
                        mrow = ROWS[t]
                        for ii in range(4):
                            src = OD["k"][:, g, ii] if kind == 1 else vst[:, g % 2, ii]
                            ins = pe.transpose(ps[0:mrow, 6 + n % 2, ii * P:(ii + 1) * P],
                                               src[:, t * P:t * P + mrow], ident)
                        ins.then_inc(s_tk, 1)

        def od_proj_copy(eng, copy, parity):
            for k in range(OD_TILES):
                g, kind, i = k // 12, k % 12 // 4, k % 4
                if k % 2 == parity:
                    eng.wait_ge(s_op, k + 1)
                    dst = (OD["q"][:, g, i], OD["k"][:, g, i], vst[:, g % 2, i])[kind]
                    copy(dst, ps[:, 2 + k % 4, 0:NT]).then_inc(s_op_copied[parity], 1)
                if k % 12 in (7, 11):
                    for t in range(3):
                        n = (2 * g + (kind == 2)) * 3 + t
                        if n % 2 != parity:
                            continue
                        eng.wait_ge(s_tk, n + 1)
                        mrow = ROWS[t]
                        if kind == 1:
                            if g == 2:
                                eng.wait_ge(s_kst[0], 16 * 2)
                            dst = kst[0:mrow, g % 2, t, :]
                        else:
                            dst = OD["v"][0:mrow, g, t, :]
                        copy(dst, ps[0:mrow, 6 + n % 2, :]).then_inc(s_tk_copied[parity], 1)

        def od_dec_prepare(v):
            v.wait_ge(s_ot, 2 + 2)
            ch = Chain(v, s_qz1)
            ch(v.memset(qz1, 0.0))
            q8 = qz1.rearrange("p g i (b h t) -> p g i h b t", h=NH, t=TS)
            for g in range(3):
                for i in range(4):
                    src = OD["q"][:, g, i, NPR:NT].rearrange("p (b t) -> p b t", t=TS)
                    for s in range(2):
                        rows = slice(HD * s, HD * s + HD)
                        v.tensor_copy(q8[rows, g, i, 2 * i + s], src[rows]).then_inc(s_qz1, 1)
            v.tensor_copy(kns, OD["k"][:, :, :, NPR:NT]).then_inc(s_qz1, 1)
            v.wait_ge(s_qz1, 26)

        def kt_copied(n):
            return s_kt_copied[n % 2], n // 2 + 1

        def od_dec_pe(pe):
            pe.wait_ge(s_qz1, 26)
            for g in range(2):
                for bb in range(4):
                    b = 4 * g + bb
                    wait_slot(pe, 1, 6 + b)
                    pe.wait_ge(s_g1[bb], 16 * (g + 1))
                    for ck in range(7):
                        n = 7 * b + ck
                        if n >= 2:
                            pe.wait_ge(*kt_copied(n - 2))
                        for i in range(4):
                            ins = pe.transpose(ps[:, n % 2, i * P:(i + 1) * P], chunk_of(b, ck)[:, i * P:(i + 1) * P], ident)
                        ins.then_inc(s_kt, 1)
                    pe.wait_ge(*kt_copied(7 * b + 5))
                    pe.wait_ge(*kt_copied(7 * b + 6))
                    if bb == 0 and g:
                        pe.wait_ge(s_sm1, 1)
                    rows = slice(32 * bb, 32 * bb + 32)
                    parts = [(2, 0, 512, 1, 0), (3, 0, P, 0, 512), (3, P, 256, 2, 640)]
                    for bank, col, w, gg, at in parts:
                        for i in range(4):
                            pe.matmul(ps[rows, bank, col:col + w], qz1[:, gg, i, 32 * b:32 * b + 32], kt1[:, i, at:at + w],
                                      start=i == 0, stop=i == 3)
                    for gg in range(3):
                        for i in range(4):
                            ins = pe.matmul(ps[rows, 3, 384 + 32 * gg:416 + 32 * gg], qz1[:, gg, i, 32 * b:32 * b + 32],
                                            kns[:, gg, i, :], start=i == 0, stop=i == 3)
                    ins.then_inc(s_sd1, 1)
                pe.wait_ge(s_sm1, 5 * g + 5)
                flat = ps[:, 4:7, :].rearrange("p b n -> p (b n)")
                if g:
                    pe.wait_ge(s_p1c, 2)
                for ck in range(7):
                    pe.transpose(flat[:, ck * P:(ck + 1) * P], s1[:, ck * P:(ck + 1) * P], ident)
                for gg in range(3):
                    ins = pe.transpose(flat[0:NSA, (7 + gg) * P:(8 + gg) * P], s1[:, OLD + gg * NSA:OLD + (gg + 1) * NSA],
                                       ident)
                ins.then_inc(s_p1, 1)
                pe.wait_ge(s_p1c, 2 * g + 2)
                for bb in range(4):
                    b = 4 * g + bb
                    for i in range(4):
                        out = ps[:, 7, 32 * b + 8 * i:32 * b + 8 * i + 8]
                        cols = slice(32 * bb + 8 * i, 32 * bb + 8 * i + 8)
                        for ck in range(7):
                            pe.matmul(out, chunk_of(b, ck)[:, 512 + i * P:512 + (i + 1) * P], pt1[:, ck, cols],
                                      start=ck == 0, stop=False)
                        for gg in range(3):
                            ins = pe.matmul(out, OD["v"][0:NSA, gg, 2, i * P:(i + 1) * P], pt1[0:NSA, 7 + gg, cols],
                                            start=False, stop=gg == 2)
                    ins.then_inc(s_o1, 1)
                    pe.wait_ge(s_o1, b + 1)
                    pe.sem_inc(s_free[1][slot_of(6 + b)], 1)

        def od_dec_keys(eng, copy, parity, b):
            for ck in range(7):
                n = 7 * b + ck
                if n % 2 == parity:
                    eng.wait_ge(s_kt, n + 1)
                    if b:
                        eng.wait_ge(s_sd1, b)
                    copy(kt1[:, :, ck * P:(ck + 1) * P],
                         ps[:, n % 2, :].rearrange("p (i n) -> p i n", i=4)).then_inc(s_kt_copied[parity], 1)

        def od_dec_dve(v):
            for g in range(2):
                for bb in range(4):
                    od_dec_keys(v, v.tensor_copy, 1, 4 * g + bb)
                steps = 5 * g

                def step(ins):
                    nonlocal steps
                    steps += 1
                    ins.then_inc(s_sm1, 1)
                    v.wait_ge(s_sm1, steps)
                v.wait_ge(s_sd1, 4 * g + 4)
                v.wait_ge(s_dd1, 16 * (g + 1))
                if g:
                    v.wait_ge(s_p1, 1)
                c = lambda k: sm1[:, 4 * g + k:4 * g + k + 1]
                step(v.scalar_tensor_tensor(out=s1, in0=dd1, scalar=row_slope,
                                            in1=banks(2, DEC_W), op0=ALU.mult, op1=ALU.add))
                step(v.tensor_reduce(c(0), s1, AX.X, ALU.max))
                step(v.tensor_scalar(c(1), c(0), -SCALE, None, ALU.mult))
                v.wait_ge(s_ex1, g + 1)
                step(v.reciprocal(c(3), c(2)))
                step(v.tensor_scalar(s1, s1, c(3), None, ALU.mult))
            v.wait_ge(s_o1, NB)
            src = ps[:, 7, 0:256].rearrange("p (b i s t) -> p i b s t", i=4, s=2, t=TS)
            for s in range(2):
                rows = slice(HD * s, HD * s + HD)
                for i in range(4):
                    v.tensor_copy(mixT[rows, i, NPR:NT].rearrange("p (b t) -> p b t", t=TS),
                                  src[rows, i, :, s, :]).then_inc(s_mix[1], 1)

        def od_dec_act(act):
            copy = lambda dst, src: act.activation(dst, src, ACT.Copy)
            for g in range(2):
                for bb in range(4):
                    od_dec_keys(act, copy, 0, 4 * g + bb)
                c = lambda k: sm1[:, 4 * g + k:4 * g + k + 1]
                act.wait_ge(s_sm1, 5 * g + 3)
                act.activation(s1, s1, ACT.Exp, bias=c(1), scale=SCALE, accum_out=c(2)).then_inc(s_ex1, 1)
                act.wait_ge(s_p1, g + 1)
                flat = ps[:, 4:7, :].rearrange("p b n -> p (b n)")
                if g:
                    act.wait_ge(s_o1, 4)
                act.activation(pt1[:, 0:7, :], flat[:, 0:7 * P].rearrange("p (k r) -> p k r", k=7),
                               ACT.Copy).then_inc(s_p1c, 1)
                act.activation(pt1[0:NSA, 7:10, :], flat[0:NSA, 7 * P:10 * P].rearrange("p (k r) -> p k r", k=3),
                               ACT.Copy).then_inc(s_p1c, 1)

        s_small = sem("s_small")
        s_sinkp = sem("s_sinkp")
        s_z0 = sem("s_z0")
        s_copy = sem("s_copy")
        s_y = sem("s_y")
        block = ctx.enter_context(nc.Block())

        even = Prompt(0, 1, EV["s"], EV["pt"], EV["osb"], EV["sm"],
                      (EV["dist"][:, 0:P], EV["dist"][:, P:3 * P]),
                      lambda g, h, qb: (EV["q"][64 * (h // 4):64 * (h // 4) + 64, h % 4, qb * P:(qb + 1) * P],
                                        EV["kv"][64 * (h // 4):64 * (h // 4) + 64, 0, 0:(qb + 1) * P]),
                      lambda g, h, kb: EV["vtok"][:, kb, 64 * (h // 4):64 * (h // 4) + 64],
                      lambda h: ((h % 4) * 2 + h // 4) * HD)
        odd = Prompt(1, 3, OP["s"], OP["pt"], OP["osb"], OP["sm"], (OP["dist"][:, 0:3 * P], OP["dist"][:, 3 * P:9 * P]),
                     lambda g, h, qb: (OD["q"][64 * (h % 2):64 * (h % 2) + 64, g, h // 2, qb * P:(qb + 1) * P],
                                       OD["k"][64 * (h % 2):64 * (h % 2) + 64, g, h // 2, 0:(qb + 1) * P]),
                     lambda g, h, kb: OD["v"][:, g, kb, h * HD:(h + 1) * HD],
                     lambda h: h * HD)
        N_OUT = {"l0": 0}

        @block.sync
        def _(sp):
            def load(layer, m, parts):
                n = reads_before(layer, m)
                if n:
                    sp.wait_ge(s_free[layer][slot_of(m)], n)
                for dst, src in parts:
                    sp.dma_start(dst, src).then_inc(s_ring[layer][slot_of(m)], 16)

            def rows8(w):
                return w.rearrange("(p c) n -> p c n", c=NC)

            def in_cols(w, m, total):
                n = min(768, total - 768 * m)
                dst = ring[:, slot_of(m), 0:NC * n].rearrange("p (c n) -> p c n", c=NC)
                return [(dst, rows8(w)[:, :, 768 * m:768 * m + n])]

            def glu(slot, wg, wu, wd):
                return [(ring[:, slot, 0:2048].rearrange("p (c n) -> p c n", c=NC), rows8(wg)),
                        (ring[:, slot, 2048:4096].rearrange("p (c n) -> p c n", c=NC), rows8(wu)),
                        (ring[:, slot, 4096:6144].rearrange("p (j n) -> p j n", j=2), wd.rearrange("(j p) n -> p j n", p=P))]

            def experts(L):
                w = (a["w_exp_gate"][L], a["w_exp_up"][L], a["w_exp_down"][L])

                def four(i, first):
                    for u in range(4):
                        s = slot_of(EXP0[L] + u)
                        if first:
                            sp.wait_ge(s_free[L][s], static_reads[L][s])
                        else:
                            sp.wait_ge(s_dn[L], 2 * i - 1 + u // 2)
                        e = u if first else (i % 16) * 4 + u
                        one = [x[e] if first else x[bass.ds(e, 1)].rearrange("a k n -> (a k) n") for x in w]
                        for dst, src in glu(s, *one):
                            sp.dma_start(dst, src).then_inc(s_ring[L][s], 16)

                four(0, True)
                with sp.Fori(1, NE // 4) as i:
                    four(i, False)
                sp.wait_ge(s_disp, L + 1)
                more = iterations(sp)
                with sp.If(more > NE // 4 - 1):
                    with sp.Fori(NE // 4, more + 1) as i:
                        four(i, False)
                with sp.Else():
                    sp.nop()
                return more

            def gain_bias(turn, g, b):
                if turn:
                    sp.wait_ge(s_gb_free, turn)
                else:
                    sp.wait_ge(s_od, 1)
                sp.dma_start(gb[:, 0, :], g.rearrange("(a n) -> a n", a=1).broadcast_to([P, D])).then_inc(s_gb, 16)
                sp.dma_start(gb[:, 1, :], b.rearrange("(a n) -> a n", a=1).broadcast_to([P, D])).then_inc(s_gb, 16)

            def router(L):
                sp.dma_start(MO["wr"], rows8(a["w_router"][L])).then_inc(s_wr, 16)
                sp.dma_start(MO["rb"], a["router_bias"][L:L + 1, :].broadcast_to([P, NE])).then_inc(s_wr, 16)

            sp.dma_start(square[:, :], a["c_square"]).then_inc(s_const, 16)
            sp.dma_start(misc[:, :], a["c_misc"]).then_inc(s_const, 16)
            xp = a["x_prompt"][0].rearrange("(t p) n -> t p n", p=P)
            for t in range(2):
                sp.dma_start(x_tok[:, t, :], xp[t]).then_inc(s_x, 16)
            sp.wait_ge(s_z0, 1)
            sp.dma_start(x_tok[0:NSA, 2, :], a["x_sample"].rearrange("b t n -> (b t) n")).then_inc(s_x, 16)
            load(0, 0, in_cols(a["w_in_even"][0], 0, EV_COLS))
            st = EV["st_in"]
            for dst, src in ((st[0:24, :], a["state_lru_conv"][0].rearrange("b k n -> (b k) n")),
                             (st[24:32, :], a["state_lru_h"][0]), (st[32:36, :], a["conv_w"][0]),
                             (st[36:37, :], a["conv_b"]), (st[37:38, :], a["b_rgate"]), (st[38:39, :], a["b_igate"]),
                             (st[39:40, :], a["lru_lambda"])):
                sp.dma_start(dst, src).then_inc(s_ev_par, 16)
            w1 = ring[:, 1, :].rearrange("p (c n) -> p c n", c=NC)
            src = rows8(a["w_in_even"][0])
            parts = [(w1[:, :, 0:256], src[:, :, 768:q0])]
            for h in range(NH):
                at = 256 + ((h % 4) * 2 + h // 4) * HD
                parts.append((w1[:, :, at:at + HD], src[:, :, q0 + h * HD:q0 + (h + 1) * HD]))
            load(0, 1, parts)
            sp.wait_ge(s_wg0, 1)
            for kind, w in enumerate((a["w_rgate"][0], a["w_igate"][0])):
                for s in range(2):
                    rows = slice(HD * s, HD * s + HD)
                    sp.dma_start(EV["wg"][rows, kind:8:2, rows],
                                 w.rearrange("(j s) c d -> s c j d", s=2)[s]).then_inc(s_wg, 16)
            load(0, 2, in_cols(a["w_in_even"][0], 2, EV_COLS))
            sp.dma_start(EV["sink"][:, 0:NH], a["swa_sinks"].broadcast_to([P, NH])).then_inc(s_small, 16)
            sp.dma_start(EV["dist"][:, 0:P], a["c_prompt"][:, 0:P]).then_inc(s_small, 16)
            sp.dma_start(EV["dist"][:, P:3 * P], a["c_prompt"][:, 3 * P:5 * P]).then_inc(s_small, 16)
            sp.dma_start(EV["dd"], a["c_even"].rearrange("g p n -> p g n")).then_inc(s_small, 16)
            sp.dma_start(gb[:, :, :].rearrange("p a n -> p (a n)").rearrange("p (b n) -> p b n", b=NB),
                         a["cache_swa_kv"][0].rearrange("b k a h d -> k b (a h d)")).then_inc(s_cache, 16)

            def out_even(hf):
                w = a["w_out_even"][0]
                s = slot_of(3 + hf)
                dst = ring[:, s, 0:8 * BANK].rearrange("p (j n) -> p j n", n=BANK)
                cols = slice(hf * BANK, (hf + 1) * BANK)
                parts = [(dst[:, 0:4, :], w[0:512, cols].rearrange("(j p) n -> p j n", p=P))]
                for x in range(2):
                    parts.append((dst[HD * x:HD * x + HD, 4:8, :],
                                  w[512 + 256 * x:768 + 256 * x, cols].rearrange("(i d) n -> d i n", d=HD)))
                return parts
            load(0, 3, out_even(0))
            load(0, 4, out_even(1))
            load(0, 5, glu(slot_of(5), a["w_sh_gate"][0], a["w_sh_up"][0], a["w_sh_down"][0]))
            gain_bias(0, a["ln1_g"][0], a["ln1_b"][0])
            sp.wait_ge(s_f, 3)
            sp.wait_ge(s_sout, OUT0)
            router(0)
            gain_bias(1, a["ln2_g"][0], a["ln2_b"][0])
            more = experts(0)

            for m in range(RING):
                sp.wait_ge(s_dn[0], 2 * more + 1 + (m - EXP0[0]) % RING // 2)
                load(1, m, in_cols(a["w_in_odd"][0], m, 6 * 768))
            gain_bias(2, a["ln1_g"][1], a["ln1_b"][1])
            for m in range(4, 6):
                load(1, m, in_cols(a["w_in_odd"][0], m, 6 * 768))
            sp.wait_ge(s_kst[0], 16 * 2)
            sp.wait_ge(s_kst[1], 16 * 6)
            sp.wait_ge(s_tk, 18)
            sp.dma_start(OP["dist"], a["c_prompt"]).then_inc(s_dp, 16)

            def sequence(b):
                s = slot_of(6 + b)
                d2 = a["cache_dil2_kv"][0, b].rearrange("(k p) a h d -> p k (a h d)", p=P)
                parts = [(ring[:, s, 0:4 * D].rearrange("p (k n) -> p k n", k=4), d2)]
                d3 = a["cache_dil3_kv"][0, b].rearrange("(s r) a h d -> s r (a h d)", r=16)
                for x in range(2):
                    parts.append((ring[:, s, (4 + x) * D:(5 + x) * D], d3[32 * x:32 * x + 32, 0:TS, :]))
                load(1, 6 + b, parts)

            def group1(b):
                sp.dma_start(g1c[b % 4], a["cache_dil1_kv"][0, b].rearrange("k a h d -> k (a h d)")).then_inc(s_g1[b % 4], 16)

            for b in range(4):
                sequence(b)
            sp.wait_ge(s_op, OD_TILES)
            for b in range(3):
                group1(b)
            sp.wait_ge(s_qz1, 26)
            group1(3)
            sp.dma_start(dd1, a["c_odd"][0]).then_inc(s_dd1, 16)
            sp.wait_ge(s_sm1, 1)
            sp.dma_start(dd1, a["c_odd"][1]).then_inc(s_dd1, 16)
            for b in range(4, 8):
                sequence(b)
                group1(b)
            load(1, 14, [(ring[:, slot_of(14), 0:4 * D].rearrange("p (j n) -> p j n", j=4),
                          a["w_out_odd"][0].rearrange("(j p) n -> p j n", p=P))])
            load(1, 15, glu(slot_of(15), a["w_sh_gate"][1], a["w_sh_up"][1], a["w_sh_down"][1]))
            sp.wait_ge(s_f, 9)
            sp.wait_ge(s_sout, OUT1)
            router(1)
            gain_bias(3, a["ln2_g"][1], a["ln2_b"][1])
            experts(1)
            for t in range(3):
                sp.wait_ge(s_xn, 9 + t + 1)
                if t < 2:
                    dst = o["y_prompt"][0].rearrange("(t p) n -> t p n", p=P)[t]
                else:
                    dst = o["y_sample"].rearrange("b t n -> (b t) n")
                sp.dma_start(dst, x_tok[0:ROWS[t], t, :]).then_inc(s_y, 16)
            sp.wait_ge(s_y, 48)

        @block.gpsimd
        def _(pool):
            pool.memset(EV["wg"], 0.0).then_inc(s_wg0, 1)

            def shift(dst, src, w):
                for b in range(NB):
                    pool.dma_start(dst[0, b, 0:w - TS].rearrange("k a h d -> k (a h d)"),
                                   src[0, b, TS:w].rearrange("k a h d -> k (a h d)")).then_inc(s_copy, 16)
            names = (("swa_kv_sample", "cache_swa_kv", P), ("dil1_kv_sample", "cache_dil1_kv", WIN[0]),
                     ("dil2_kv_sample", "cache_dil2_kv", WIN[1]), ("dil3_kv_sample", "cache_dil3_kv", WIN[2]))
            for dst, src, w in names:
                shift(o[dst], a[src], w)
            n = 0

            def store(dst, src):
                nonlocal n
                n += 1
                pool.dma_start(dst, src).then_inc(s_sout, 16)
            pool.wait_ge(s_kvt_copied, 2)
            for kind, name in enumerate(("ktok", "vtok")):
                store(o["swa_kv_prompt"][0, 0, :, kind].rearrange("t h d -> t (h d)"), EV[name][:, 1, :])
                store(o["swa_kv_sample"][0, :, P - TS:P, kind].rearrange("b t h d -> b t (h d)"), EV[name][0:NSA, 2, :])
            pool.wait_ge(s_so_copied, 1)
            so = EV["st_out"]
            store(o["lru_h_prompt"][0], so[0:1, :])
            store(o["lru_h_sample"][0], so[1:9, :])
            store(o["lru_conv_prompt"][0, 0], so[9:12, :])
            store(o["lru_conv_sample"][0].rearrange("b k n -> (b k) n"), so[12:36, :])
            assert 16 * n == OUT0
            moe_pairs_pool(pool, 0)
            for g in range(3):
                keep = WIN[g] if g == 0 else NPR
                o_p, o_s = o[f"dil{g + 1}_kv_prompt"], o[f"dil{g + 1}_kv_sample"]
                for kind in range(2):
                    for par in range(2):
                        last = (2 * g + kind) * 3 + 2
                        k, v_ = turn_copied(last if last % 2 == par else last - 1)
                        pool.wait_ge(k, v_)
                    src = (lambda t, m: kst[0:m, g % 2, t, :]) if kind == 0 else (lambda t, m: OD["v"][0:m, g, t, :])
                    for t in range(2):
                        at = t * P - (NPR - keep)
                        if at >= 0:
                            ins = (o_p[0, 0, at:at + P, kind].rearrange("t h d -> t (h d)"), src(t, P))
                            if kind == 0:
                                pool.dma_start(*ins).then_inc(s_kst[g > 0], 16)
                            else:
                                store(*ins)
                    ins = (o_s[0, :, WIN[g] - TS:WIN[g], kind].rearrange("b t h d -> b t (h d)"), src(2, NSA))
                    if kind == 0:
                        pool.dma_start(*ins).then_inc(s_kst[g > 0], 16)
                    else:
                        store(*ins)
            assert 16 * n == OUT1
            moe_pairs_pool(pool, 1)
            pool.wait_ge(s_sout, OUT1)
            pool.wait_ge(s_copy, 16 * 4 * NB)

        @block.scalar
        def _(act):
            copy = lambda dst, src: act.activation(dst, src, ACT.Copy)
            xt_copy(act, copy, 0, 0)
            ev_proj_act(act)
            ev_kvt_act(act)
            ev_lru_act(act)
            prompt_act(act, even)
            ev_dec_act(act)
            act.wait_ge(s_so, 1)
            copy(EV["st_out"][0:36, :], ps[0:36, 7, :]).then_inc(s_so_copied, 1)
            ln_act(act, 0)
            for L in range(2):
                xt_copy(act, copy, 2 * L + 1, 0)
                moe_act_head(act, L)
                moe_shared_acc_act(act, L)
                moe_pairs_act(act, L)
                ln_act(act, 2 * L + 1)
                if L == 0:
                    xt_copy(act, copy, 2, 0)
                    od_proj_copy(act, copy, 0)
                    prompt_act(act, odd)
                    od_dec_act(act)
                    ln_act(act, 2)

        @block.vector
        def _(v):
            v.memset(x_tok[:, 2, :], 0.0).then_inc(s_z0, 1)
            xt_copy(v, v.tensor_copy, 0, 1)
            ev_proj_dve(v)
            ev_lru_dve(v)
            v.memset(xT[:, :, NT:NTP], 0.0).then_inc(s_pad, 1)
            ev_dec_qz(None, v)
            v.wait_ge(s_small, 64)
            ch = lru["chain"]
            ch(v.tensor_scalar(EV["sink"][:, NH:2 * NH], EV["sink"][:, 0:NH], -1.0, None, ALU.mult))
            ch(v.tensor_tensor(EV["sink"][:, 2 * NH:3 * NH], EV["sink"][:, 0:NH], row_head, ALU.mult))
            ch(v.tensor_reduce(EV["sink"][:, 24:25], EV["sink"][:, 2 * NH:3 * NH], AX.X, ALU.add))
            prompt_dve(v, even)
            ev_dec_dve(v)
            ln_dve(v, 0, False)
            for L in range(2):
                xt_copy(v, v.tensor_copy, 2 * L + 1, 1)
                moe_route_dve(v, L)
                moe_shared_dve(v, L)
                moe_pos_dve(v, L)
                moe_pairs_dve(v, L)
                ln_dve(v, 2 * L + 1, True)
                if L == 0:
                    xt_copy(v, v.tensor_copy, 2, 1)
                    od_proj_copy(v, v.tensor_copy, 1)
                    v.wait_ge(s_dp, 16)
                    prompt_dve(v, odd)
                    od_dec_prepare(v)
                    od_dec_dve(v)
                    v.memset(xT[:, :, NT:NTP], 0.0).then_inc(s_pad, 1)
                    ln_dve(v, 2, False)

        @block.tensor
        def _(pe):
            pe.wait_ge(s_const, 32)
            xt_pe(pe, 0)
            ev_state_pe(pe)
            ev_proj_pe(pe)
            ev_kvt_pe(pe)
            ev_gate_pe(pe)
            pe.wait_ge(s_gate_act, 8)
            pe.wait_ge(s_kvt_copied, 2)
            prompt_pe(pe, even)
            ev_dec_pe(pe)
            pe.wait_ge(s_otc, 2)
            ev_state_out_pe(pe)
            pe.wait_ge(s_mix[0], 8)
            out_proj_pe(pe, 0, 8, (3, 4))
            for L in range(2):
                xt_pe(pe, 2 * L + 1)
                moe_route_pe(pe, L)
                moe_shared_pe(pe, L)
                moe_pos_pe(pe, L)
                moe_shared_down_pe(pe, L)
                moe_pairs_pe(pe, L)
                if L == 0:
                    xt_pe(pe, 2)
                    od_proj_pe(pe)
                    pe.wait_ge(s_op_copied[0], OD_TILES // 2)
                    pe.wait_ge(s_op_copied[1], OD_TILES // 2)
                    pe.wait_ge(s_tk_copied[0], 9)
                    pe.wait_ge(s_tk_copied[1], 9)
                    prompt_pe(pe, odd)
                    od_dec_pe(pe)
                    pe.wait_ge(s_mix[1], 8)
                    pe.wait_ge(s_otc, 2 + 2)
                    pe.wait_ge(s_pad, 2)
                    out_proj_pe(pe, 1, 4, (14,))


_INS = ['x_prompt', 'x_sample', 'state_lru_h', 'state_lru_conv', 'cache_swa_kv', 'cache_dil1_kv', 'cache_dil2_kv',
        'cache_dil3_kv', 'w_in_even', 'conv_w', 'conv_b', 'w_rgate', 'b_rgate', 'w_igate', 'b_igate', 'lru_lambda',
        'swa_sinks', 'w_out_even', 'w_in_odd', 'w_out_odd', 'ln1_g', 'ln1_b', 'ln2_g', 'ln2_b', 'w_router',
        'router_bias', 'w_exp_gate', 'w_exp_up', 'w_exp_down', 'w_sh_gate', 'w_sh_up', 'w_sh_down']
_OUTS = [("y_prompt", (1, 256, 1024)), ("y_sample", (8, 4, 1024)), ("lru_h_prompt", (1, 1, 512)),
         ("lru_h_sample", (1, 8, 512)), ("lru_conv_prompt", (1, 1, 3, 512)), ("lru_conv_sample", (1, 8, 3, 512)),
         ("swa_kv_prompt", (1, 1, 128, 2, 2, 64)), ("swa_kv_sample", (1, 8, 128, 2, 2, 64)),
         ("dil1_kv_prompt", (1, 1, 128, 2, 8, 64)), ("dil1_kv_sample", (1, 8, 128, 2, 8, 64)),
         ("dil2_kv_prompt", (1, 1, 256, 2, 8, 64)), ("dil2_kv_sample", (1, 8, 512, 2, 8, 64)),
         ("dil3_kv_prompt", (1, 1, 256, 2, 8, 64)), ("dil3_kv_sample", (1, 8, 1024, 2, 8, 64))]


def kernel(**inputs):
    import numpy as _np
    import concourse.bacc as _bacc
    from concourse import mybir as _mybir
    from concourse.bass_utils import run_bass_kernel_spmd as _run

    nc = _bacc.Bacc("TRN2", target_bir_lowering=False, num_devices=1)
    arrays, a, o = {}, {}, {}
    for name in _INS:
        arrays[f"in_{name}"] = _np.ascontiguousarray(inputs[name])
    for name, table in tables().items():
        arrays[f"in_{name}"] = table
    for name, x in arrays.items():
        a[name[3:]] = nc.dram_tensor(name, x.shape, _mybir.dt.from_np(x.dtype), kind="ExternalInput").ap()
    for name, shape in _OUTS:
        o[name] = nc.dram_tensor(f"out_{name}", shape, F32, kind="ExternalOutput").ap()
    build(nc, a, o)
    r = _run(nc, [arrays], core_ids=[0])
    return tuple(r.results[0][f"out_{name}"] for name, _ in _OUTS)
```

```python
from contextlib import ExitStack

import numpy as np

import concourse.bass as bass
from concourse import mybir

F32 = mybir.dt.float32
I32 = mybir.dt.int32
BF16 = mybir.dt.bfloat16
ALU = mybir.AluOpType
ACT = mybir.ActivationFunctionType
AX = mybir.AxisListType

P = 128
D = 1024
NC = D // P
NPR, NSA = 256, 32
NT = NPR + NSA
NTP = 3 * P
NB, TS = 8, 4
ROWS = (P, P, NSA)
HD = 64
NH = 8
NE = 64
DE = 256
CAP = 64
PASSES = -(-NT // CAP)
SLOT = 6144
RING = 4
BANK = 512
ALPHA = float(4 ** 0.25)
EPS = 1e-5
SCALE = HD ** -0.5
NEG = -1e30
BIG = 1e30
LRU_TILES = 4
CONVW = 4
SEQ_S = CONVW - 1 + TS
XRW = CONVW - 1 + NPR + NB * SEQ_S
CW = XRW - (CONVW - 1)
SAMP0 = NPR + CONVW - 1
WIN = (P, 512, 1024)
DIL = (1, 4, 16)
OLD = 7 * P
DEC_W = OLD + 3 * NSA
EV_COLS = 1792
OD_TILES = 36
OUT0 = 16 * 8
OUT1 = OUT0 + 16 * 8
MISC = 6 + PASSES + PASSES * CAP + 64 + 1 + NH


def tables():
    slopes = 2.0 ** -(np.arange(1, NH + 1))
    row = np.arange(P)
    bb, h, t = row // 32, (row % 32) // TS, row % TS
    far = 1e30

    def dist(d, ok):
        return np.where(ok, d, far).astype(np.float32)

    q, k = np.arange(NPR)[:, None], np.arange(NPR)[None, :]
    d = q - k
    win = dist(d, (d >= 0) & (d <= P))
    d4 = dist(d, (d >= 0) & (d % 4 == 0) & (d <= 512))
    d16 = dist(d, (d >= 0) & (d % 16 == 0) & (d <= 2048))
    prompt = np.concatenate([m[:P, :P] for m in (win, d4, d16)] + [m[P:] for m in (win, d4, d16)], axis=1)
    old1 = P + t[:, None] - np.arange(P)[None, :]
    old1 = dist(old1, (old1 <= P) & (old1 >= 0))
    d2 = WIN[1] + t[:, None] - np.arange(WIN[1])[None, :]
    d2 = dist(d2, (d2 % 4 == 0) & (d2 <= 512))
    pos3 = (np.arange(256) // TS) * 16 + np.arange(256) % TS
    d3 = WIN[2] + t[:, None] - pos3[None, :]
    d3 = dist(d3, d3 % 16 == 0)
    even, odd = [], []
    for g in range(2):
        nb_, nt_ = np.arange(NSA) // TS, np.arange(NSA) % TS
        same = (4 * g + bb)[:, None] == nb_[None, :]
        dn = t[:, None] - nt_[None, :]
        n1 = dist(dn, same & (dn >= 0))
        n4 = dist(dn, same & (dn == 0))
        even.append(np.concatenate([old1, n1], axis=1))
        odd.append(np.concatenate([d2, old1, d3, n1, n4, n4], axis=1))
    tri = (row[:, None] < row[None, :]).astype(np.float32)
    square = np.concatenate([np.eye(P), tri, np.ones((P, P))], axis=1)
    valid = np.ones((P, 3))
    valid[NSA:, 2] = 0
    g8 = np.arange(NH)
    before = (g8[None, :] < g8[:, None]).astype(np.float32).reshape(1, 64)
    misc = np.concatenate([
        valid, 1 - valid, np.tile(np.arange(1, PASSES + 1) * CAP, (P, 1)),
        np.tile(np.arange(PASSES * CAP), (P, 1)), np.tile(before, (P, 1)), (-8 * slopes[h])[:, None],
        (h[:, None] == g8[None, :])], axis=1)
    f = lambda a: np.ascontiguousarray(a, np.float32)
    return {"c_square": f(square), "c_misc": f(misc), "c_prompt": f(prompt),
            "c_even": f(np.stack(even)), "c_odd": f(np.stack(odd))}


class Chain:

    def __init__(self, eng, sem):
        self.eng, self.sem, self.n = eng, sem, 0

    def __call__(self, ins):
        self.n += 1
        ins.then_inc(self.sem, 1)
        self.eng.wait_ge(self.sem, self.n)


def slope8(h):
    return -8.0 * 2.0 ** -(h + 1)


def build(nc, a, o):
    ctx = ExitStack()
    with ctx:
        def sb(name, shape, dt=F32):
            return ctx.enter_context(nc.sbuf_tensor(name, shape, dt))

        def sem(name):
            return ctx.enter_context(nc.semaphore(name))

        def per_layer(name):
            return [sem(f"{name}_{layer}") for layer in range(2)]

        ps = ctx.enter_context(nc.psum_tensor("ps", [P, 8, BANK], F32))
        ring = sb("ring", [P, RING, SLOT])
        x_tok = sb("x_tok", [P, 3, D])
        xT = sb("xT", [P, NC, NTP])
        mixT = sb("mixT", [P, 8, NT])
        square = sb("square", [P, 3 * P])
        misc = sb("misc", [P, MISC])
        gb = sb("gb", [P, 2, D])
        stats = sb("stats", [P, 3, 16])
        ident, tri, ones = (square[:, i * P:(i + 1) * P] for i in range(3))
        ident_b = sb("ident_b", [P, P], BF16)
        valid, invalid = misc[:, 0:3], misc[:, 3:6]
        thresholds = misc[:, 6:6 + PASSES]
        iota0 = 6 + PASSES
        before = misc[:, iota0 + PASSES * CAP:iota0 + PASSES * CAP + 64]
        row_slope = misc[:, iota0 + PASSES * CAP + 64:iota0 + PASSES * CAP + 65]

        row_head = misc[:, MISC - NH:MISC]

        arena = sb("arena", [P, 16900])

        def cut(sizes, base=0):
            views, at = {}, base
            for name, shape in sizes:
                n = int(np.prod(shape))
                v = arena[:, at:at + n]
                if len(shape) == 2:
                    v = v.rearrange("p (a b) -> p a b", b=shape[1])
                elif len(shape) == 3:
                    v = v.rearrange("p (a b c) -> p a b c", b=shape[1], c=shape[2])
                views[name] = v
                at += n
            assert at <= 16900, at
            return views, at

        EV, _ = cut([("xr", (LRU_TILES, XRW)), ("xc", (LRU_TILES, CW)), ("rg", (LRU_TILES, CW)),
                     ("ig", (LRU_TILES, CW)), ("gel", (4, NT)), ("q", (4, NT)),
                     ("kv", (2, NT)), ("vtok", (3, P)), ("ktok", (3, P)), ("ktd", (NB, P)), ("qz", (NB, 32)),
                     ("s", (2, 256)), ("pt", (2, 256)), ("dist", (384,)), ("dd", (2, 160)), ("sd", (2, 160)),
                     ("ptd", (2, 2 * P)), ("osb", (512,)), ("st_in", (512,)), ("stc", (4, 36)), ("st_out", (512,)),
                     ("wg", (8, P)), ("st", (4, 40)), ("sp", (8, 4)), ("sink", (25,)), ("sm", (8, 16))])
        OD, _ = cut([("qk", (2, 3, 4 * NT)), ("v", (3, 3, 512)), ("work", (5380,))])
        OD["q"] = OD["qk"][:, 0].rearrange("p g (i t) -> p g i t", t=NT)
        OD["k"] = OD["qk"][:, 1].rearrange("p g (i t) -> p g i t", t=NT)
        MO, _ = cut([("acc", (NC, NT)), ("z", (D,)), ("xg", (NC, P)), ("yb", (3, D // 2)), ("y_rest", (D,)),
                     ("xb", (8, D // 2)), ("own_gate", (2,)), ("h", (DE,)), ("hT", (2, P)),
                     ("sg", (DE,)), ("pgt", (2, NT // 2)), ("pm", (2, 3, P // 2)), ("pg", (2, 3, P)),
                     ("wr", (NC, NE)), ("rb", (NE,)), ("scores", (3, NE)), ("biased", (3, NE)), ("top", (24, 8)),
                     ("gs", (3, 8)), ("gt", (3, 64)), ("eq", (3, 64)), ("rank", (3, 8)), ("t8", (3, 8)),
                     ("rep", (3, NE)), ("sel", (3, NE)), ("gate", (3, NE)), ("pos", (3, NE)), ("cnt", (16,)), ("cur", (2, CAP + 12))])
        MO["shg"], MO["sh"] = (MO["yb"].rearrange("p k n -> p (k n)")[:, k * 2 * NT:(k + 1) * 2 * NT].rearrange(
            "p (j t) -> p j t", j=2) for k in range(2))
        xb = MO["xb"].rearrange("p k n -> p (k n)").bitcast(BF16).rearrange("p (k n) -> p k n", k=8)
        x_rest = [mixT[:, :, :].rearrange("p j t -> p (j t)")[:, t * D:(t + 1) * D] for t in range(2)] + [MO["z"]]
        yb = MO["yb"].rearrange("p k n -> p (k n)").bitcast(BF16).rearrange("p (k n) -> p k n", k=3)
        pgt = MO["pgt"].rearrange("p q n -> p (q n)").bitcast(BF16).rearrange("p (q n) -> p q n", q=2)
        pm = MO["pm"].rearrange("p q t n -> p (q t n)").bitcast(BF16).rearrange("p (q t n) -> p q t n", q=2, t=3)
        n_iter = sb("n_iter", [P, 1], I32)

        s_const = sem("s_const")
        s_x = sem("s_x")
        s_pad = sem("s_pad")
        s_ring = [[sem(f"s_ring_{layer}_{s}") for s in range(RING)] for layer in range(2)]
        s_free = [[sem(f"s_free_{layer}_{s}") for s in range(RING)] for layer in range(2)]
        s_ring_dn = [[sem(f"s_ring_dn_{layer}_{q}") for q in range(2)] for layer in range(2)]
        EXP0 = (6, 16)
        SHARED = (5, 15)
        n_dma = [{0: 1, 1: 9, 2: 1, 3: 3, 4: 3, 5: 3},
                 {**{m: 1 for m in range(6)}, **{m: 3 for m in range(6, 10)}, **{m: 0 for m in range(10, 14)}, 14: 1, 15: 3}]

        def slot_of(m):
            return m % RING

        def loaded(layer, m):
            return 16 * sum(n for k, n in n_dma[layer].items() if k % RING == m % RING and k <= m)

        def reads_before(layer, m):
            return len([k for k in n_dma[layer] if k % RING == m % RING and k < m])

        static_dma = [[16 * sum(n for k, n in n_dma[layer].items() if k % RING == s) for s in range(RING)]
                      for layer in range(2)]
        static_reads = [[len([k for k in n_dma[layer] if k % RING == s]) for s in range(RING)] for layer in range(2)]

        def wait_slot(eng, layer, m):
            eng.wait_ge(s_ring[layer][slot_of(m)], loaded(layer, m))
            return ring[:, slot_of(m), :]

        def free_slot(ins, layer, m):
            ins.then_inc(s_free[layer][slot_of(m)], 1)

        s_tp = sem("s_tp")
        s_tp_copied = [sem("s_tp_copied_act"), sem("s_tp_copied_dve")]

        def xt_pe(pe, turn):
            for t in range(3):
                if turn == 0:
                    pe.wait_ge(s_x, 16 * 3)
                else:
                    pe.wait_ge(s_xn, 3 * (turn - 1) + t + 1)
                for hf in range(2):
                    n = turn * 3 + t
                    if n:
                        pe.wait_ge(s_tp_copied[hf], n)
                    for j in range(4):
                        c = 4 * hf + j
                        src = x_tok[0:ROWS[t], t, :].rearrange("t (p c) -> t c p", c=NC)[:, c, :]
                        ins = pe.transpose(ps[:, hf, j * P:j * P + ROWS[t]], src, ident[0:ROWS[t], 0:ROWS[t]])
                    ins.then_inc(s_tp, 1)

        def xt_copy(eng, copy, turn, hf):
            for t in range(3):
                eng.wait_ge(s_tp, 2 * (turn * 3 + t) + hf + 1)
                m = ROWS[t]
                src = ps[:, hf, :].rearrange("p (c t) -> p c t", t=P)[:, :, 0:m]
                copy(xT[:, 4 * hf:4 * hf + 4, t * P:t * P + m], src).then_inc(s_tp_copied[hf], 1)

        s_f = sem("s_f")
        s_ln = sem("s_ln")
        s_gb = sem("s_gb")
        s_gb_free = sem("s_gb_free")
        s_xn = sem("s_xn")
        s_var = sem("s_var")
        s_rstd = sem("s_rstd")
        ln = {"n": 0}

        def ln_act(act, turn):
            for t in range(3):
                act.wait_ge(s_var, 3 * turn + t + 1)
                st = stats[0:ROWS[t], t, :]
                act.activation(st[:, 14:15], st[:, 13:14], ACT.Sqrt).then_inc(s_rstd, 1)

        def ln_dve(v, turn, permuted):
            z = MO["z"]
            def step(ins):
                ln["n"] += 1
                ins.then_inc(s_ln, 1)
                v.wait_ge(s_ln, ln["n"])
            for t in range(3):
                m = ROWS[t]
                v.wait_ge(s_f, 3 * turn + t + 1)
                if permuted:
                    for hf in range(2):
                        f = ps[0:m, 2 * t + hf, :].rearrange("t (c p) -> t p c", c=4)
                        xin = x_tok[0:m, t, :].rearrange("t (p h c) -> t h p c", h=2, c=4)[:, hf]
                        zo = z[0:m, :].rearrange("t (p h c) -> t h p c", h=2, c=4)[:, hf]
                        ins = v.scalar_tensor_tensor(out=zo, in0=xin, scalar=ALPHA, in1=f, op0=ALU.mult, op1=ALU.add)
                        ins.then_inc(s_ln, 1)
                    ln["n"] += 2
                    v.wait_ge(s_ln, ln["n"])
                else:
                    for hf in range(2):
                        ins = v.scalar_tensor_tensor(out=z[0:m, hf * BANK:(hf + 1) * BANK],
                                                     in0=x_tok[0:m, t, hf * BANK:(hf + 1) * BANK], scalar=ALPHA,
                                                     in1=ps[0:m, 2 * t + hf, :], op0=ALU.mult, op1=ALU.add)
                        ins.then_inc(s_ln, 1)
                    ln["n"] += 2
                    v.wait_ge(s_ln, ln["n"])
                st = stats[0:m, t, :]
                for hf in range(2):
                    ins = v.bn_stats(st[:, 6 * hf:6 * hf + 6], z[0:m, hf * BANK:(hf + 1) * BANK])
                    ins.then_inc(s_ln, 1)
                ln["n"] += 2
                v.wait_ge(s_ln, ln["n"])
                step(v.bn_aggr(st[:, 12:14], st[:, 0:12]))
                step(v.tensor_scalar(st[:, 13:14], st[:, 13:14], EPS, None, ALU.add))
                v.sem_inc(s_var, 1)
                v.wait_ge(s_rstd, 3 * turn + t + 1)
                step(v.reciprocal(st[:, 14:15], st[:, 14:15]))
                step(v.tensor_scalar(z[0:m, :], z[0:m, :], st[:, 12:13], st[:, 14:15], ALU.subtract, ALU.mult))
                v.wait_ge(s_gb, 32 * (turn + 1))
                step(v.tensor_tensor(z[0:m, :], z[0:m, :], gb[0:m, 0, :], ALU.mult))
                step(v.tensor_tensor(x_tok[0:m, t, :], z[0:m, :], gb[0:m, 1, :], ALU.add))
                v.sem_inc(s_xn, 1)
            v.sem_inc(s_gb_free, 1)

        s_ep = sem("s_ep")
        s_ep_copied = [sem("s_ep_copied_act"), sem("s_ep_copied_dve")]
        s_ev_par = sem("s_ev_par")
        s_wg0 = sem("s_wg0")
        s_wg = sem("s_wg")
        s_arg = sem("s_arg")
        s_root = sem("s_root")
        s_st = sem("s_st")
        s_xr = sem("s_xr")
        s_conv = sem("s_conv")
        s_gate = sem("s_gate")
        s_gate_act = sem("s_gate_act")
        s_lru = sem("s_lru")
        s_lru_act = sem("s_lru_act")
        s_aout = sem("s_aout")
        s_so = sem("s_so")
        s_so_copied = sem("s_so_copied")
        s_kvt = sem("s_kvt")
        s_kvt_copied = sem("s_kvt_copied")
        s_qz = sem("s_qz")
        s_kd = sem("s_kd")
        s_kd_copied = sem("s_kd_copied")
        s_sd = sem("s_sd")
        s_sd_dve = sem("s_sd_dve")
        s_sd_exp = sem("s_sd_exp")
        s_ptd = sem("s_ptd")
        s_ptd_copied = sem("s_ptd_copied")
        s_od = sem("s_od")
        s_mix = [sem("s_mix_0"), sem("s_mix_1")]
        s_sout = sem("s_sout")
        q0, k0, v0 = D, D + 512, D + 640
        ACT_TILES, DVE_TILES = range(4, 14), range(4)

        def copied_value(k):
            return (s_ep_copied[0], k - 4 + 1) if k >= 4 else (s_ep_copied[1], k + 1)

        def ev_proj_pe(pe):
            pe.wait_ge(s_tp_copied[0], 3)
            pe.wait_ge(s_tp_copied[1], 3)
            for k in range(14):
                m = k // 6
                w = wait_slot(pe, 0, m)
                w = w[:, 0:NC * min(768, EV_COLS - 768 * m)].rearrange("p (c n) -> p c n", c=NC)
                if k >= 4:
                    pe.wait_ge(*copied_value(k - 4))
                bank = 2 + k % 4
                for c in range(NC):
                    lhs = w[:, c, k * P - 768 * m:(k + 1) * P - 768 * m]
                    ins = pe.matmul(ps[:, bank, 0:NT], lhs, xT[:, c, 0:NT], start=c == 0, stop=c == NC - 1)
                ins.then_inc(s_ep, 1)
                if k % 6 == 5 or k == 13:
                    pe.wait_ge(s_ep, k + 1)
                    pe.sem_inc(s_free[0][slot_of(m)], 1)

        def ev_xr_dst(j):
            samp = EV["xr"][:, j, SAMP0:XRW].rearrange("p (b s) -> p b s", s=SEQ_S)
            return EV["xr"][:, j, CONVW - 1:CONVW - 1 + NPR], samp
        def ev_proj_act(act):
            for k in ACT_TILES:
                act.wait_ge(s_ep, k + 1)
                src = ps[:, 2 + k % 4, 0:NT]
                if k < 8:
                    ins = act.activation(EV["gel"][:, k - 4, :], src, ACT.Gelu_apprx_tanh)
                else:
                    dst = EV["q"][:, k - 8, :] if k < 12 else EV["kv"][:, k - 12, :]
                    ins = act.activation(dst, src, ACT.Copy)
                ins.then_inc(s_ep_copied[0], 1)

        lru = {}

        def ev_proj_dve(v):
            ch = lru["chain"] = Chain(v, s_lru)
            ch(v.memset(EV["xr"][:, :, 0:CONVW - 1], 0.0))
            for k in DVE_TILES:
                v.wait_ge(s_ep, k + 1)
                prompt, samp = ev_xr_dst(k)
                ch(v.tensor_copy(prompt, ps[:, 2 + k, 0:NPR]))
                v.tensor_copy(samp[:, :, CONVW - 1:SEQ_S],
                              ps[:, 2 + k, NPR:NT].rearrange("p (b s) -> p b s", s=TS)).then_inc(s_ep_copied[1], 1)
            v.wait_ge(s_st, 1)
            st = EV["st"]
            ch(v.tensor_copy(st, ps[:, 6, 0:160].rearrange("p (j n) -> p j n", n=40)))
            for j in range(LRU_TILES):
                _, samp = ev_xr_dst(j)
                ch(v.tensor_copy(samp[:, :, 0:CONVW - 1], st[:, j, 0:24].rearrange("p (b s) -> p b s", s=CONVW - 1)))
            v.wait_ge(s_ep_copied[1], 4)

            lam, sp = st[:, :, 39], EV["sp"]
            ch(v.scalar_tensor_tensor(out=sp[:, 0, :], in0=lam, scalar=-1.0, in1=lam, op0=ALU.mult, op1=ALU.max))
            v.sem_inc(s_xr, 1)
            v.wait_ge(s_lru_act, 1)
            ch(v.tensor_scalar(sp[:, 2, :], sp[:, 1, :], 2.0, None, ALU.add))
            ch(v.reciprocal(sp[:, 3, :], sp[:, 2, :]))
            ch(v.tensor_tensor(sp[:, 2, :], sp[:, 1, :], sp[:, 3, :], ALU.mult))
            ch(v.tensor_tensor(sp[:, 3, :], sp[:, 2, :], sp[:, 2, :], ALU.mult))
            ch(v.tensor_scalar(sp[:, 4, :], sp[:, 3, :], 1 / 19, 1 / 17, ALU.mult, ALU.add))
            for n in range(15, 0, -2):
                ch(v.tensor_tensor(sp[:, 4, :], sp[:, 4, :], sp[:, 3, :], ALU.mult))
                ch(v.tensor_scalar(sp[:, 4, :], sp[:, 4, :], 1 / n, None, ALU.add))
            ch(v.scalar_tensor_tensor(out=sp[:, 4, :], in0=sp[:, 2, :], scalar=2.0, in1=sp[:, 4, :], op0=ALU.mult,
                                      op1=ALU.mult))
            ch(v.tensor_scalar(sp[:, 5, :], lam, -1.0, 0.0, ALU.mult, ALU.max))
            ch(v.tensor_tensor(sp[:, 5, :], sp[:, 5, :], sp[:, 4, :], ALU.add))
            ch(v.tensor_scalar(sp[:, 6, :], sp[:, 5, :], 8.0, None, ALU.mult))
            ch(v.tensor_scalar(sp[:, 7, :], sp[:, 5, :], -8.0, None, ALU.mult))

        def ev_lru_dve(v):
            ch, st = lru["chain"], EV["st"]
            xr, xc = EV["xr"], EV["xc"]
            for j in range(LRU_TILES):
                ch(v.tensor_scalar(xc[:, j, :], xr[:, j, 0:CW], st[:, j, 32:33], st[:, j, 36:37], ALU.mult, ALU.add))
                for tap in range(1, CONVW):
                    ch(v.scalar_tensor_tensor(out=xc[:, j, :], in0=xr[:, j, tap:tap + CW],
                                              scalar=st[:, j, 32 + tap:33 + tap], in1=xc[:, j, :],
                                              op0=ALU.mult, op1=ALU.add))
                v.sem_inc(s_conv, 1)

            def scan_input(j):
                v.wait_ge(s_lru_act, 1 + LRU_TILES + j + 1)
                aa, rg, ig = xT[:, j, 0:CW], EV["rg"][:, j, :], EV["ig"][:, j, :]
                ch(v.tensor_tensor(ig, ig, xc[:, j, :], ALU.mult))
                ch(v.tensor_tensor(xc[:, j, :], aa, aa, ALU.mult))
                ch(v.scalar_tensor_tensor(out=rg, in0=xc[:, j, :], scalar=1.0, in1=rg, op0=ALU.add, op1=ALU.mult))
                v.sem_inc(s_arg, 1)

            def scan(j):
                aa, rg, ig = xT[:, j, 0:CW], EV["rg"][:, j, :], EV["ig"][:, j, :]
                v.wait_ge(s_root, j + 1)
                ch(v.tensor_tensor(ig, ig, rg, ALU.mult))
                first = slice(SAMP0 - 1, SAMP0 - 1 + SEQ_S * (NB - 1) + 1, SEQ_S)
                ch(v.memset(aa[:, first], 0.0))
                ch(v.tensor_copy(ig[:, first], st[:, j, 24:32]))
                ch(v.tensor_tensor_scan(xc[:, j, :], aa, ig, 0.0, ALU.mult, ALU.add))
                gel = EV["gel"][:, j, :]
                v.wait_ge(s_ep_copied[0], j + 1)
                ch(v.tensor_tensor(mixT[:, j, 0:NPR], xc[:, j, 0:NPR], gel[:, 0:NPR], ALU.mult))
                samp = EV["xc"].rearrange("p j n -> p (j n)")[:, j * CW + SAMP0:j * CW + SAMP0 + (NB - 1) * SEQ_S]
                dst = mixT[:, j, NPR:NT].rearrange("p (b s) -> p b s", s=TS)
                g3 = gel[:, NPR:NT].rearrange("p (b s) -> p b s", s=TS)
                ch(v.tensor_tensor(dst[:, 0:NB - 1], samp.rearrange("p (b s) -> p b s", s=SEQ_S)[:, :, 0:TS],
                                   g3[:, 0:NB - 1], ALU.mult))
                last = SAMP0 + (NB - 1) * SEQ_S
                ch(v.tensor_tensor(dst[:, NB - 1], xc[:, j, last:last + TS], g3[:, NB - 1], ALU.mult))

            scan_input(0)
            for j in range(LRU_TILES):
                if j + 1 < LRU_TILES:
                    scan_input(j + 1)
                scan(j)
            stc = EV["stc"]
            ch(v.tensor_copy(stc[:, :, 0:1], xc[:, :, NPR - 1:NPR]))
            ch(v.tensor_copy(stc[:, :, 1:9], xc[:, :, SAMP0 + TS - 1:SAMP0 + TS + SEQ_S * (NB - 1):SEQ_S]))
            ch(v.tensor_copy(stc[:, :, 9:12], xr[:, :, NPR:NPR + 3]))
            for j in range(LRU_TILES):
                _, samp = ev_xr_dst(j)
                ch(v.tensor_copy(stc[:, j, 12:36].rearrange("p (b s) -> p b s", s=3), samp[:, :, TS:SEQ_S]))
            v.sem_inc(s_aout, 1)

        def ev_lru_act(act):
            sp, st = EV["sp"], EV["st"]
            act.wait_ge(s_xr, 1)
            act.activation(sp[:, 1, :], sp[:, 0, :], ACT.Exp, scale=-1.0).then_inc(s_lru_act, 1)
            for n in range(8):
                j = n // 2
                act.wait_ge(s_gate, n + 1)
                dst = EV["ig"] if n % 2 else EV["rg"]
                act.activation(dst[:, j, :], ps[:, n % 4, 0:CW], ACT.Sigmoid,
                               bias=st[:, j, 37 + n % 2:38 + n % 2]).then_inc(s_gate_act, 1)
            act.wait_ge(s_gate_act, 8)
            act.wait_ge(s_ep, 14)
            for j in range(LRU_TILES):
                act.activation(xT[:, j, 0:CW], EV["rg"][:, j, :], ACT.Exp,
                               scale=sp[:, 7, j:j + 1]).then_inc(s_lru_act, 1)
            act.wait_ge(s_lru_act, 1 + LRU_TILES)
            for j in range(LRU_TILES):
                act.activation(EV["rg"][:, j, :], EV["rg"][:, j, :], ACT.Tanh,
                               scale=sp[:, 6, j:j + 1]).then_inc(s_lru_act, 1)
            for j in range(LRU_TILES):
                act.wait_ge(s_arg, j + 1)
                act.activation(EV["rg"][:, j, :], EV["rg"][:, j, :], ACT.Sqrt).then_inc(s_root, 1)

        def ev_state_pe(pe):
            pe.wait_ge(s_ev_par, 16 * 7)
            for j in range(4):
                ins = pe.transpose(ps[:, 6, 40 * j:40 * j + 40], EV["st_in"][0:40, j * P:(j + 1) * P], ident[0:40, 0:40])
            ins.then_inc(s_st, 1)

        def ev_gate_pe(pe):
            pe.wait_ge(s_wg, 16 * 4)
            for n in range(8):
                j = n // 2
                pe.wait_ge(s_conv, j + 1)
                if n >= 4:
                    pe.wait_ge(s_gate_act, n - 3)
                pe.matmul(ps[:, n % 4, 0:CW], EV["wg"][:, n, :], EV["xc"][:, j, :], start=True,
                          stop=True).then_inc(s_gate, 1)

        def ev_state_out_pe(pe):
            pe.wait_ge(s_aout, 1)
            pe.wait_ge(s_kvt_copied, 2)
            for j in range(4):
                ins = pe.transpose(ps[0:36, 7, j * P:(j + 1) * P], EV["stc"][:, j, :], ident)
            ins.then_inc(s_so, 1)

        def ev_kvt_pe(pe):
            pe.wait_ge(s_ep_copied[0], 10)
            pe.wait_ge(s_lru, 7)
            for kind, bank in ((1, 6), (0, 7)):
                for t in range(3):
                    m = ROWS[t]
                    ins = pe.transpose(ps[0:m, bank, t * P:(t + 1) * P], EV["kv"][:, kind, t * P:t * P + m], ident)
                ins.then_inc(s_kvt, 1)

        def ev_kvt_act(act):
            for n, (dst, bank) in enumerate((("vtok", 6), ("ktok", 7))):
                act.wait_ge(s_kvt, n + 1)
                act.activation(EV[dst][:, 0:2, :], ps[:, bank, 0:2 * P].rearrange("p (t n) -> p t n", n=P), ACT.Copy)
                act.activation(EV[dst][0:NSA, 2, :], ps[0:NSA, bank, 2 * P:3 * P], ACT.Copy).then_inc(s_kvt_copied, 1)

        s_s = sem("s_s")
        s_sp = sem("s_sp")
        s_mx = sem("s_mx")
        s_nb = sem("s_nb")
        s_exp = sem("s_exp")
        s_pt = sem("s_pt")
        s_ptc = sem("s_ptc")
        s_pv = sem("s_pv")
        s_den = per_layer("s_den")
        s_sinkx = sem("s_sinkx")
        s_oc = sem("s_oc")
        s_ot = sem("s_ot")
        s_otc = sem("s_otc")

        class Prompt:
            def __init__(self, layer, groups, s, pt, osb, sm, dist, score, value, out_col):
                self.layer, self.groups, self.s, self.pt, self.osb = layer, groups, s, pt, osb
                self.sm, self.dist, self.score, self.value, self.out_col = sm, dist, score, value, out_col

            def width(self, qb):
                return self.groups * P * (qb + 1)

        def banks(first, width):
            return ps[:, first:first + 2, :].rearrange("p b n -> p (b n)")[:, 0:width]

        def prompt_pe(pe, c):
            L = c.layer

            def scores(n):
                qb, h = divmod(n, NH)
                if n >= 2:
                    pe.wait_ge(s_sp, 16 * L + n - 1)
                for g in range(c.groups):
                    nk = P * (qb + 1)
                    lhs, rhs = c.score(g, h, qb)
                    ins = pe.matmul(banks(2 * (n % 2), 2 * BANK)[:, g * nk:(g + 1) * nk], lhs, rhs, start=True, stop=True)
                ins.then_inc(s_s, 1)

            def weights_t(n):
                qb = n // NH
                pe.wait_ge(s_exp, 16 * L + n + 1)
                if n:
                    pe.wait_ge(s_ptc, 16 * L + n)
                for u in range(c.groups * (qb + 1)):
                    ins = pe.transpose(banks(4, 2 * BANK)[:, u * P:(u + 1) * P], c.s[:, n % 2, u * P:(u + 1) * P], ident)
                ins.then_inc(s_pt, 1)

            def values(n):
                qb, h = divmod(n, NH)
                pe.wait_ge(s_ptc, 16 * L + n + 1)
                if h == 0 and qb:
                    pe.wait_ge(s_oc, 2 * L + qb)
                units = c.groups * (qb + 1)
                col = c.out_col(h)
                for u in range(units):
                    g, kb = divmod(u, qb + 1)
                    ins = pe.matmul(ps[:, 6, col:col + HD], c.pt[:, n % 2, u * P:(u + 1) * P], c.value(g, h, kb),
                                    start=u == 0, stop=u == units - 1)
                ins.then_inc(s_pv, 1)

            def turn(qb):
                pe.wait_ge(s_oc, 2 * L + qb + 1)
                if qb:
                    pe.wait_ge(s_otc, 2 * L + qb)
                for i in range(4):
                    ins = pe.transpose(ps[:, 7, i * P:(i + 1) * P], c.osb[:, i * P:(i + 1) * P], ident)
                ins.then_inc(s_ot, 1)

            scores(0)
            for n in range(2 * NH):
                if n + 1 < 2 * NH:
                    scores(n + 1)
                weights_t(n)
                if n:
                    values(n - 1)
                if n == NH + 1:
                    turn(0)
            values(2 * NH - 1)
            turn(1)

        def prompt_dve(v, c):
            L = c.layer
            mx, nb, den, rin, snb, sx = (c.sm[:, i, :] for i in range(6))
            ch = Chain(v, s_den[L])

            def finish(qb):
                cols = slice(NH * qb, NH * qb + NH)
                v.wait_ge(s_exp, 16 * L + NH * (qb + 1))
                if L == 0:
                    ch(v.tensor_tensor(snb[:, cols], nb[:, cols], EV["sink"][:, 0:NH], ALU.add))
                    v.wait_ge(s_sinkx, qb + 1)
                    ch(v.tensor_tensor(den[:, cols], den[:, cols], sx[:, cols], ALU.add))
                ch(v.reciprocal(rin[:, cols], den[:, cols]))
                v.wait_ge(s_pv, 16 * L + NH * (qb + 1))
                if qb:
                    v.wait_ge(s_ot, 2 * L + qb)
                scale = rin[:, cols]
                if L == 0:
                    scale = scale.rearrange("p (s i) -> p i s", s=2)
                    dst = c.osb.rearrange("p (i s d) -> p i s d", i=4, s=2)
                    src = ps[:, 6, :].rearrange("p (i s d) -> p i s d", i=4, s=2)
                    scale = scale.unsqueeze(3).broadcast_to([P, 4, 2, HD])
                else:
                    dst = c.osb.rearrange("p (h d) -> p h d", h=NH)
                    src = ps[:, 6, :].rearrange("p (h d) -> p h d", h=NH)
                    scale = scale.unsqueeze(2).broadcast_to([P, NH, HD])
                v.tensor_tensor(dst, src, scale, ALU.mult).then_inc(s_oc, 1)

            for n in range(2 * NH):
                qb, h = divmod(n, NH)
                w = c.width(qb)
                v.wait_ge(s_s, 16 * L + n + 1)
                if n >= 2:
                    v.wait_ge(s_pt, 16 * L + n - 1)
                v.scalar_tensor_tensor(out=c.s[:, n % 2, 0:w], in0=c.dist[qb], scalar=slope8(h),
                                       in1=banks(2 * (n % 2), w), op0=ALU.mult, op1=ALU.add).then_inc(s_sp, 1)
                v.wait_ge(s_sp, 16 * L + n + 1)
                v.tensor_reduce(mx[:, n:n + 1], c.s[:, n % 2, 0:w], AX.X, ALU.max).then_inc(s_mx, 1)
                v.wait_ge(s_mx, 16 * L + n + 1)
                if L == 0:
                    ins = v.tensor_scalar(nb[:, n:n + 1], mx[:, n:n + 1], -SCALE, EV["sink"][:, NH + h:NH + h + 1],
                                          ALU.mult, ALU.min)
                else:
                    ins = v.tensor_scalar(nb[:, n:n + 1], mx[:, n:n + 1], -SCALE, None, ALU.mult)
                ins.then_inc(s_nb, 1)
                if n == NH + 1:
                    finish(0)
            finish(1)

        def prompt_act(act, c):
            L = c.layer
            mx, nb, den, rin, snb, sx = (c.sm[:, i, :] for i in range(6))

            def exps(n):
                w = c.width(n // NH)
                act.wait_ge(s_nb, 16 * L + n + 1)
                act.activation(c.s[:, n % 2, 0:w], c.s[:, n % 2, 0:w], ACT.Exp, bias=nb[:, n:n + 1], scale=SCALE,
                               accum_out=den[:, n:n + 1]).then_inc(s_exp, 1)

            def copy(n):
                w = c.width(n // NH)
                act.wait_ge(s_pt, 16 * L + n + 1)
                if n >= 2:
                    act.wait_ge(s_pv, 16 * L + n - 1)
                act.activation(c.pt[:, n % 2, 0:w], banks(4, w), ACT.Copy).then_inc(s_ptc, 1)

            def sinks(qb):
                if L == 0:
                    cols = slice(NH * qb, NH * qb + NH)
                    act.wait_ge(s_den[L], 1 + 3 * qb)
                    act.activation(sx[:, cols], snb[:, cols], ACT.Exp).then_inc(s_sinkx, 1)

            def turned(qb):
                act.wait_ge(s_ot, 2 * L + qb + 1)
                tile0 = 4 if L == 0 else 0
                act.activation(mixT[:, tile0:tile0 + 4, qb * P:(qb + 1) * P],
                               ps[:, 7, :].rearrange("p (i t) -> p i t", i=4), ACT.Copy).then_inc(s_otc, 1)

            exps(0)
            for n in range(2 * NH):
                if n == NH + 1:
                    sinks(0)
                if n + 1 < 2 * NH:
                    exps(n + 1)
                copy(n)
                if n == NH + 1:
                    turned(0)
            sinks(1)
            turned(1)

        s_cache = sem("s_cache")

        def ev_dec_qz(eng_copy, v):
            qz = EV["qz"].rearrange("p b (h t) -> p h b t", h=NH)
            ch = lru["chain"]
            ch(v.memset(EV["qz"], 0.0))
            v.wait_ge(s_ep_copied[0], 10)
            src = EV["q"][:, :, NPR:NT].rearrange("p i (b t) -> p i b t", t=TS)
            for s in range(2):
                rows = slice(HD * s, HD * s + HD)
                for i in range(4):
                    ch(v.tensor_copy(qz[rows, 4 * s + i], src[rows, i]))
            v.sem_inc(s_qz, 1)

        def ev_dec_pe(pe):
            pe.wait_ge(s_cache, 16)
            pe.wait_ge(s_ptc, 2 * NH)
            cache = gb.rearrange("p a n -> p (a n)").rearrange("p (b n) -> p b n", b=NB)
            for b in range(NB):
                ins = pe.transpose(ps[:, 4 + b // 4, (b % 4) * P:(b % 4 + 1) * P], cache[:, b, 0:P], ident)
                if b % 4 == 3:
                    ins.then_inc(s_kd, 1)
            pe.wait_ge(s_sp, 2 * NH)
            pe.wait_ge(s_qz, 1)
            for g in range(2):
                pe.wait_ge(s_kd_copied, g + 1)
                for bb in range(4):
                    b = 4 * g + bb
                    rows = slice(32 * bb, 32 * bb + 32)
                    pe.matmul(ps[rows, g, 0:P], EV["qz"][:, b, :], EV["ktd"][:, b, :], start=True, stop=True)
                    ins = pe.matmul(ps[rows, g, P:P + NSA], EV["qz"][:, b, :], EV["kv"][:, 0, NPR:NT], start=True,
                                    stop=True)
                ins.then_inc(s_sd, 1)
            for g in range(2):
                pe.wait_ge(s_sd_dve, 7 * g + 7)
                pe.transpose(ps[:, g, 0:P], EV["sd"][:, g, 0:P], ident)
                pe.transpose(ps[0:NSA, g, P:2 * P], EV["sd"][:, g, P:P + NSA],
                             ident).then_inc(s_ptd, 1)
            pe.wait_ge(s_kvt_copied, 1)
            for g in range(2):
                pe.wait_ge(s_ptd_copied, 2 * g + 2)
                for bb in range(4):
                    b = 4 * g + bb
                    out = ps[:, 3, b * 32:b * 32 + 32]
                    rhs = EV["ptd"][:, g, :].rearrange("p (k r) -> p k r", k=2)
                    pe.matmul(out, cache[:, b, P:2 * P], rhs[:, 0, 32 * bb:32 * bb + 32], start=True, stop=False)
                    ins = pe.matmul(out, EV["vtok"][0:NSA, 2, :], rhs[0:NSA, 1, 32 * bb:32 * bb + 32], start=False,
                                    stop=True)
            ins.then_inc(s_od, 1)

        def ev_dec_dve(v):
            dm, sm = EV["sd"], EV["sm"][:, 6, :]
            steps = 0
            for g in range(2):
                v.wait_ge(s_kd, g + 1)
                v.tensor_copy(EV["ktd"][:, 4 * g:4 * g + 4, :],
                              ps[:, 4 + g, :].rearrange("p (b n) -> p b n", b=4)).then_inc(s_kd_copied, 1)

            def step(ins):
                nonlocal steps
                steps += 1
                ins.then_inc(s_sd_dve, 1)
                v.wait_ge(s_sd_dve, steps)
            row_sink = EV["sink"][:, 24:25]
            for g in range(2):
                v.wait_ge(s_sd, g + 1)
                c = lambda k: sm[:, 8 * g + k:8 * g + k + 1]
                step(v.scalar_tensor_tensor(out=dm[:, g, :], in0=EV["dd"][:, g, :], scalar=row_slope,
                                            in1=ps[:, g, 0:160], op0=ALU.mult, op1=ALU.add))
                step(v.tensor_reduce(c(0), dm[:, g, :], AX.X, ALU.max))
                step(v.tensor_scalar(c(1), c(0), SCALE, row_sink, ALU.mult, ALU.max))
                step(v.tensor_scalar(c(2), c(1), -1.0, None, ALU.mult))
                v.wait_ge(s_sd_exp, 2 * g + 2)
                step(v.tensor_scalar(c(5), c(3), c(4), None, ALU.add))
                step(v.reciprocal(c(6), c(5)))
                step(v.tensor_scalar(dm[:, g, :], dm[:, g, :], c(6), None, ALU.mult))
            v.wait_ge(s_od, 1)
            src = ps[:, 3, 0:256].rearrange("p (b h t) -> p b h t", h=NH, t=TS)
            for s in range(2):
                rows = slice(HD * s, HD * s + HD)
                for i in range(4):
                    dst = mixT[rows, 4 + i, NPR:NT].rearrange("p (b t) -> p b t", t=TS)
                    v.tensor_copy(dst, src[rows, :, 4 * s + i, :]).then_inc(s_mix[0], 1)

        def ev_dec_act(act):
            sm = EV["sm"][:, 6, :]
            for g in range(2):
                c = lambda k: sm[:, 8 * g + k:8 * g + k + 1]
                act.wait_ge(s_sd_dve, 7 * g + 4)
                act.activation(EV["sd"][:, g, :], EV["sd"][:, g, :], ACT.Exp, bias=c(2), scale=SCALE,
                               accum_out=c(3)).then_inc(s_sd_exp, 1)
                act.activation(c(4), EV["sink"][:, 24:25], ACT.Exp, bias=c(2)).then_inc(s_sd_exp, 1)
            for g in range(2):
                act.wait_ge(s_ptd, g + 1)
                act.activation(EV["ptd"][:, g, 0:P], ps[:, g, 0:P], ACT.Copy).then_inc(s_ptd_copied, 1)
                act.activation(EV["ptd"][0:NSA, g, P:2 * P], ps[0:NSA, g, P:2 * P],
                               ACT.Copy).then_inc(s_ptd_copied, 1)

        s_mid = sem("s_mid")

        def out_proj_pe(pe, layer, tiles, loads):
            for hf, m in enumerate(loads):
                w = wait_slot(pe, layer, m)
                n = tiles * BANK
                for t in range(3):
                    rows = ROWS[t]
                    for j in range(tiles):
                        if len(loads) == 2:
                            rhs = w[:, j * BANK:(j + 1) * BANK]
                            outs = ((hf, rhs),)
                        else:
                            outs = tuple((x, w[:, j * D + x * BANK:j * D + (x + 1) * BANK]) for x in range(2))
                        for x, rhs in outs:
                            ins = pe.matmul(ps[0:rows, 2 * t + x, :], mixT[:, j, t * P:t * P + rows], rhs,
                                            start=j == 0, stop=j == tiles - 1)
                    if hf == len(loads) - 1:
                        ins.then_inc(s_f, 1)
                    elif t == 2:
                        ins.then_inc(s_mid, 1)
                if hf < len(loads) - 1:
                    pe.wait_ge(s_mid, 1)
                else:
                    pe.wait_ge(s_f, 6 * layer + 3)
                pe.sem_inc(s_free[layer][slot_of(m)], 1)

        s_wr = sem("s_wr")
        s_lg = sem("s_lg")
        s_sc = sem("s_sc")
        s_rt = per_layer("s_rt")
        s_sel = sem("s_sel")
        s_ps = sem("s_ps")
        s_disp = sem("s_disp")
        s_sgu = sem("s_sgu")
        s_sact = sem("s_sact")
        s_sh = sem("s_sh")
        s_sy = sem("s_sy")
        s_acc0 = sem("s_acc0")
        s_xb = sem("s_xb")
        s_pm = per_layer("s_pm")
        s_ga = per_layer("s_ga")
        s_pgt = per_layer("s_pgt")
        s_pgtc = per_layer("s_pgtc")
        s_xg = per_layer("s_xg")
        s_gu = per_layer("s_gu")
        s_si = per_layer("s_si")
        s_h2 = per_layer("s_h2")
        s_ht = per_layer("s_ht")
        s_htc = per_layer("s_htc")
        s_dn = per_layer("s_dn")
        s_yb = per_layer("s_yb")
        s_yc = per_layer("s_yc")
        s_scat = per_layer("s_scat")
        s_add = per_layer("s_add")

        def iterations(eng):
            return eng.value_load(n_iter[0:1, 0:1], min_val=NE // 4 - 1, max_val=PASSES * NE // 4 - 1)

        def moe_route_pe(pe, L):
            pe.wait_ge(s_tp_copied[0], 3 * (2 * L + 2))
            pe.wait_ge(s_tp_copied[1], 3 * (2 * L + 2))
            pe.wait_ge(s_wr, 32 * (L + 1))
            for t in range(3):
                for c in range(NC):
                    ins = pe.matmul(ps[:, 2, t * NE:(t + 1) * NE], xT[:, c, t * P:(t + 1) * P], MO["wr"][:, c, :],
                                    start=c == 0, stop=c == NC - 1)
            ins.then_inc(s_lg, 1)

        def moe_pos_pe(pe, L):
            pe.wait_ge(s_sel, L + 1)
            sel = MO["sel"]
            for t in range(3):
                for u in range(t + 1):
                    ins = pe.matmul(ps[:, 2, t * NE:(t + 1) * NE], tri if u == t else ones, sel[:, u, :],
                                    start=u == 0, stop=u == t)
            for u in range(3):
                ins = pe.matmul(ps[:, 2, 3 * NE:4 * NE], ones, sel[:, u, :], start=u == 0, stop=u == 2)
            ins.then_inc(s_ps, 1)

        def moe_shared_pe(pe, L):
            w = wait_slot(pe, L, SHARED[L])
            wg, wu = (w[:, i * 2048:(i + 1) * 2048].rearrange("p (c n) -> p c n", c=NC) for i in range(2))
            wd = w[:, 4096:6144].rearrange("p (j n) -> p j n", j=2)
            for j in range(2):
                for c in range(NC):
                    pe.matmul(ps[:, 4 + j, 0:NT], wg[:, c, j * P:(j + 1) * P], xT[:, c, 0:NT], start=c == 0,
                              stop=c == NC - 1)
                for c in range(NC):
                    ins = pe.matmul(ps[:, 6 + j, 0:NT], wu[:, c, j * P:(j + 1) * P], xT[:, c, 0:NT], start=c == 0,
                                    stop=c == NC - 1)
                ins.then_inc(s_sgu, 1)

        def moe_shared_down_pe(pe, L):
            w = wait_slot(pe, L, SHARED[L])
            wd = w[:, 4096:6144].rearrange("p (j n) -> p j n", j=2)
            pe.wait_ge(s_sh, 2 * L + 2)
            for c in range(NC):
                if c >= 2:
                    pe.wait_ge(s_acc0, 8 * L + c - 1)
                for j in range(2):
                    lhs = wd[:, j, :].rearrange("p (f c) -> p c f", c=NC)[:, c, :]
                    ins = pe.matmul(ps[:, c % 2, 0:NT], lhs, MO["sh"][:, j, :], start=j == 0, stop=j == 1)
                ins.then_inc(s_sy, 1)
            pe.wait_ge(s_sy, 8 * L + NC)
            pe.sem_inc(s_free[L][slot_of(SHARED[L])], 1)

        route_chain = {}

        def moe_route_dve(v, L):
            ch = route_chain[L] = Chain(v, s_rt[L])
            M = MO
            sc, bi, sel, gate = M["scores"], M["biased"], M["sel"], M["gate"]
            v.wait_ge(s_sc, L + 1)
            v.wait_ge(s_wr, 32 * (L + 1))
            ch(v.tensor_tensor(bi, sc, M["rb"].unsqueeze(1).broadcast_to([P, 3, NE]), ALU.add))
            for n in range(24):
                t, g = divmod(n, 8)
                ins = v.max(M["top"][:, n, :], bi[:, t, g * 8:g * 8 + 8])
            ch(ins)
            ch(v.tensor_tensor(M["gs"], M["top"][:, :, 0].rearrange("p (t g) -> p t g", t=3),
                               M["top"][:, :, 1].rearrange("p (t g) -> p t g", t=3), ALU.add))
            gt = M["gt"].rearrange("p t (g f) -> p t g f", g=8)
            eq = M["eq"].rearrange("p t (g f) -> p t g f", g=8)
            tie = before.rearrange("p (g f) -> p g f", g=8)
            for t in range(3):
                mine = M["gs"][:, t, :].unsqueeze(2).broadcast_to([P, 8, 8])
                other = M["gs"][:, t, :].unsqueeze(1).broadcast_to([P, 8, 8])
                ch(v.tensor_tensor(gt[:, t], other, mine, ALU.is_gt))
                ch(v.tensor_tensor(eq[:, t], other, mine, ALU.is_equal))
                ch(v.tensor_tensor(eq[:, t], eq[:, t], tie, ALU.mult))
            ch(v.tensor_tensor(gt, gt, eq, ALU.add))
            ch(v.tensor_reduce(M["rank"], gt, AX.X, ALU.add))
            keep = M["rank"]
            ch(v.tensor_scalar(keep, keep, 3.5, None, ALU.is_lt))
            kb = keep.unsqueeze(3).broadcast_to([P, 3, 8, 8])
            b4 = bi.rearrange("p t (g f) -> p t g f", g=8)
            ch(v.tensor_tensor(b4, b4, kb, ALU.mult))
            ch(v.tensor_scalar(M["gs"], keep, BIG, -BIG, ALU.mult, ALU.add))
            ch(v.tensor_tensor(b4, b4, M["gs"].unsqueeze(3).broadcast_to([P, 3, 8, 8]), ALU.add))
            for t in range(3):
                ch(v.max(M["t8"][:, t, :], bi[:, t, :]))
                ch(v.match_replace(M["rep"][:, t, :], M["t8"][:, t, :], bi[:, t, :], -3e38))
            ch(v.tensor_tensor(sel, M["rep"], bi, ALU.not_equal))
            ch(v.tensor_tensor(sel, sel, valid.unsqueeze(2).broadcast_to([P, 3, NE]), ALU.mult))
            v.sem_inc(s_sel, 1)
            ch(v.tensor_tensor(gate, sc, sel, ALU.mult))
            sm = M["cnt"]
            ch(v.tensor_reduce(sm[:, 0:3], gate, AX.X, ALU.add))
            ch(v.tensor_tensor(sm[:, 0:3], sm[:, 0:3], invalid, ALU.add))
            ch(v.reciprocal(sm[:, 3:6], sm[:, 0:3]))
            ch(v.tensor_scalar(sm[:, 3:6], sm[:, 3:6], 2.5, None, ALU.mult))
            ch(v.tensor_tensor(gate, gate, sm[:, 3:6].unsqueeze(2).broadcast_to([P, 3, NE]), ALU.mult))

        def moe_pos_dve(v, L):
            M, ch = MO, route_chain[L]
            sm, sel, pos = M["cnt"], M["sel"], M["pos"]
            v.wait_ge(s_ps, L + 1)
            ch(v.scalar_tensor_tensor(out=pos, in0=ps[:, 2, 0:3 * NE].rearrange("p (t e) -> p t e", t=3), scalar=1.0,
                                      in1=sel, op0=ALU.add, op1=ALU.mult))
            ch(v.tensor_scalar(pos, pos, -1.0, None, ALU.add))
            for part in range(1, 3):
                v.tensor_copy(pos[NSA * part:NSA * (part + 1), 2, :], pos[0:NSA, 2, :]).then_inc(s_rt[L], 1)
                ch.n += 1
            v.wait_ge(s_rt[L], ch.n)
            ch(v.tensor_reduce(sm[:, 6:7], ps[:, 2, 3 * NE:4 * NE], AX.X, ALU.max))
            ch(v.tensor_scalar(sm[:, 8:8 + PASSES], thresholds, sm[:, 6:7], None, ALU.is_lt))
            ch(v.tensor_reduce(sm[:, 7:8], sm[:, 8:8 + PASSES], AX.X, ALU.add))
            ch(v.tensor_scalar(sm[:, 7:8], sm[:, 7:8], float(NE // 4), float(NE // 4 - 1), ALU.mult, ALU.add))
            ch(v.tensor_copy(n_iter[:, :], sm[:, 7:8]))
            v.sem_inc(s_disp, 1)

        def moe_shared_dve(v, L):
            for j in range(2):
                v.wait_ge(s_sact, 2 * L + j + 1)
                v.tensor_tensor(MO["sh"][:, j, :], MO["shg"][:, j, :], ps[:, 6 + j, 0:NT], ALU.mult).then_inc(s_sh, 1)

        def moe_shared_acc_act(act, L):
            for c in range(NC):
                act.wait_ge(s_sy, 8 * L + c + 1)
                act.activation(MO["acc"][:, c, :], ps[:, c % 2, 0:NT], ACT.Copy).then_inc(s_acc0, 1)

        def part_at(t, part):
            return 3 * t + part if t < 2 else 6 + part

        def moe_act_head(act, L):
            act.wait_ge(s_sout, (OUT0, OUT1)[L])
            for t in range(3):
                rows = slice(0, ROWS[t])
                act.activation(xb[rows, part_at(t, 0)], x_tok[rows, t, :], ACT.Copy).then_inc(s_xb, 1)
            act.wait_ge(s_lg, L + 1)
            act.activation(MO["scores"], ps[:, 2, 0:3 * NE].rearrange("p (t e) -> p t e", t=3),
                           ACT.Sigmoid).then_inc(s_sc, 1)
            for t in range(3):
                rows = slice(0, ROWS[t])
                act.wait_ge(s_pm[L], t + 1)
                act.activation(xb[rows, part_at(t, 1)], x_rest[t][rows], ACT.Copy).then_inc(s_xb, 1)
            act.activation(xb[NSA:2 * NSA, 6], x_rest[2][0:NSA], ACT.Copy).then_inc(s_xb, 1)
            for j in range(2):
                act.wait_ge(s_sgu, 2 * L + j + 1)
                act.activation(MO["shg"][:, j, :], ps[:, 4 + j, 0:NT], ACT.Silu).then_inc(s_sact, 1)
            for t in range(3):
                act.wait_ge(s_pm[L], 3 + t + 1)
                out, rows = (xb[:, 3 * t + 2], P) if t < 2 else (xb[2 * NSA:3 * NSA, 6], NSA)
                act.activation(out, x_rest[t][0:rows], ACT.Copy).then_inc(s_xb, 1)

        def moe_pairs_pool(pool, L):
            for part in range(2):
                for t in range(3):
                    rows = slice(0, ROWS[t])
                    pool.wait_ge(s_xb, 10 * L + (t + 1, (4, 5, 7)[t])[part])
                    pool.tensor_tensor(x_rest[t][rows], (x_rest[t] if part else x_tok[:, t, :])[rows],
                                       xb[rows, part_at(t, part)], ALU.subtract).then_inc(s_pm[L], 1)
            pool.wait_ge(s_pm[L], 6)
            pool.wait_ge(s_disp, L + 1)
            pool.sem_inc(s_pgt[L], 2)
            cur = MO["cur"]
            column = lambda q, k: cur[:, q, CAP + 6 * k:CAP + 6 * k + 6].rearrange("p (t u) -> p t u", u=2)
            with pool.Fori(0, iterations(pool) + 1) as i:
                for q in range(2):
                    n = 2 * i + q
                    pool.wait_ge(s_pgt[L], n + 1)
                    pool.sem_inc(s_pm[L], 1)
                    e = (i % 16) * 4 + 2 * q
                    slots, pos, gate = cur[:, q, 0:CAP], column(q, 0), column(q, 1)
                    pool.tensor_copy(slots, misc[:, bass.ds(iota0 + (i // 16) * CAP, CAP)]).then_inc(s_pm[L], 1)
                    pool.tensor_copy(pos, MO["pos"][:, :, bass.ds(e, 2)]).then_inc(s_pm[L], 1)
                    pool.tensor_copy(gate, MO["gate"][:, :, bass.ds(e, 2)]).then_inc(s_pm[L], 1)
                    pool.wait_ge(s_pm[L], 7 * n + 10)
                    pool.sem_inc(s_pm[L], 1)
                    for name in ("pm", "pg"):
                        for t in range(3):
                            for u in range(2):
                                out = (pm if name == "pm" else MO["pg"])[:, q, t, u * CAP:(u + 1) * CAP]
                                if name == "pm":
                                    ins = pool.tensor_scalar(out, slots, pos[:, t, u:u + 1], None, ALU.is_equal)
                                else:
                                    ins = pool.tensor_scalar(out, slots, pos[:, t, u:u + 1], gate[:, t, u:u + 1],
                                                             ALU.is_equal, ALU.mult)
                        ins.then_inc(s_pm[L], 1)
                    pool.wait_ge(s_pm[L], 7 * n + 13)

        def gather_pe(pe, L, n, q, hf):
            pe.wait_ge(s_pm[L], 7 * n + 13)
            for c in range(4 * hf, 4 * hf + 4):
                for k in range(7):
                    m = 3 * NSA if k == 6 else P
                    lhs = xb[0:m, k].rearrange("t (f c) -> t c f", c=NC)[:, c, :]
                    ins = pe.matmul(ps[:, hf, (c % 4) * P:(c % 4 + 1) * P], lhs, pm[0:m, q, k // 3, :],
                                    start=k == 0, stop=k == 6)
            ins.then_inc(s_ga[L], 1)

        def turn_pe(pe, L, n, q):
            for t in range(3):
                m = ROWS[t]
                pe.transpose(ps[:, 3, :].bitcast(BF16)[:, t * P:t * P + m], pm[0:m, q, t, :], ident_b[0:m, 0:m])
            for t in range(3):
                m = ROWS[t]
                ins = pe.matmul(ps[:, 3, NT:NT + 1], MO["pg"][0:m, q, t, :], ones[0:m, 0:1], start=t == 0, stop=t == 2)
            ins.then_inc(s_pgt[L], 1)

        def up_pe(pe, L, n, q, it, scatter=None):
            pe.wait_ge(s_xg[L], 2 * n + 2)
            for u in range(2):
                s = slot_of(EXP0[L] + 2 * q + u)
                pe.wait_ge(s_ring[L][s], static_dma[L][s] + (it + 1) * 32)
            for c in range(NC):
                for u in range(2):
                    w = ring[:, slot_of(EXP0[L] + 2 * q + u), 0:4096].rearrange("p (g c n) -> p c g n", g=2, c=NC)
                    ins = pe.matmul(ps[64 * u:64 * u + CAP, 2, :], MO["xg"][:, c, u * CAP:(u + 1) * CAP], w[:, c],
                                    start=c == 0, stop=c == NC - 1)
                if c == NC - 1:
                    ins.then_inc(s_gu[L], 1)
                for chunk in {4: (0, 1), 5: (2, 3), 6: (4, 5), 7: (6, 7)}.get(c, ()) if scatter else ():
                    scatter(chunk)

        def hidden_pe(pe, L, n):
            pe.wait_ge(s_h2[L], n + 1)
            for j in range(2):
                ins = pe.transpose(ps[:, 2, j * P:(j + 1) * P], MO["h"][:, j * P:(j + 1) * P], ident)
            ins.then_inc(s_ht[L], 1)

        def down_pe(pe, L, n, q, it):
            pe.wait_ge(s_htc[L], n + 1)
            pe.wait_ge(s_ring_dn[L][q], (it + 1) * 32)
            for hf in range(2):
                for j in range(2):
                    for u in range(2):
                        w = ring[:, slot_of(EXP0[L] + 2 * q + u), 4096:6144].rearrange("p (j n) -> p j n", j=2)
                        ins = pe.matmul(ps[64 * u:64 * u + CAP, 4 + hf, :], MO["hT"][:, j, 64 * u:64 * u + CAP],
                                        w[:, j, hf * BANK:(hf + 1) * BANK], start=j == 0, stop=j == 1)
            ins.then_inc(s_dn[L], 1)

        def scatter_pe(pe, L, n, q, c):
            if c == 0:
                pe.wait_ge(s_yc[L], 4 * n + 4)
                pe.wait_ge(s_pgtc[L], n + 1)
            pe.wait_ge(s_add[L], NC * n + c + NC - 1)
            for k in range(3):
                lhs = yb[:, k].rearrange("p (f c) -> p c f", c=NC)[:, c, :]
                ins = pe.matmul(ps[:, 6 + c % 2, 0:NT], lhs, pgt[:, q, :], start=k == 0, stop=k == 2)
            ins.then_inc(s_scat[L], 1)

        def over_pairs(eng, L, first, step, last):
            more = iterations(eng)
            first(0, 0, 0)
            with eng.Fori(0, more) as i:
                step(2 * i + 1, 1, i)
                step(2 * i + 2, 0, i + 1)
            step(2 * more + 1, 1, more)
            last(2 * more + 1, 1, more)
            return more

        def moe_pairs_pe(pe, L):
            pe.wait_ge(s_acc0, 8 * L + NC)
            pe.wait_ge(s_disp, L + 1)
            pe.wait_ge(s_xb, 10 * (L + 1))

            def first(n, q, it):
                gather_pe(pe, L, n, q, 0)
                gather_pe(pe, L, n, q, 1)
                turn_pe(pe, L, n, q)
                up_pe(pe, L, n, q, it)

            def step(n, q, it):
                gather_pe(pe, L, n, q, 0)
                hidden_pe(pe, L, n - 1)
                gather_pe(pe, L, n, q, 1)
                turn_pe(pe, L, n, q)
                down_pe(pe, L, n - 1, 1 - q, it if q else it - 1)
                up_pe(pe, L, n, q, it, lambda c: scatter_pe(pe, L, n - 1, 1 - q, c))

            def last(n, q, it):
                hidden_pe(pe, L, n)
                down_pe(pe, L, n, q, it)
                for c in range(NC):
                    scatter_pe(pe, L, n, q, c)

            more = over_pairs(pe, L, first, step, last)
            pe.wait_ge(s_add[L], more * (2 * NC) + 3 * NC)
            for t in range(3):
                m = ROWS[t]
                for c in range(NC):
                    ins = pe.transpose(ps[0:m, 2 * t + c // 4, (c % 4) * P:(c % 4 + 1) * P],
                                       MO["acc"][:, c, t * P:t * P + m], ident)
                ins.then_inc(s_f, 1)

        def moe_pairs_act(act, L):
            act.wait_ge(s_disp, L + 1)

            def tokens(n):
                act.wait_ge(s_ga[L], 2 * n + 1)
                act.activation(MO["xg"][:, 0:4, :], ps[:, 0, :].rearrange("p (c s) -> p c s", c=4),
                               ACT.Copy).then_inc(s_xg[L], 1)

            def tokens2(n):
                act.wait_ge(s_ga[L], 2 * n + 2)
                act.activation(MO["xg"][:, 4:8, :], ps[:, 1, :].rearrange("p (c s) -> p c s", c=4),
                               ACT.Copy).then_inc(s_xg[L], 1)

            def hidden(n):
                act.wait_ge(s_ht[L], n + 1)
                act.activation(MO["hT"], ps[:, 2, 0:2 * P].rearrange("p (j s) -> p j s", j=2),
                               ACT.Copy).then_inc(s_htc[L], 1)

            def turned(n, q):
                act.wait_ge(s_pgt[L], n + 3)
                act.activation(MO["own_gate"][:, q:q + 1], ps[:, 3, NT:NT + 1], ACT.Copy)
                act.activation(pgt[:, q, :], ps[:, 3, :].bitcast(BF16)[:, 0:NT], ACT.Copy).then_inc(s_pgtc[L], 1)

            def parts(n):
                act.wait_ge(s_dn[L], n + 1)
                for hf in range(2):
                    act.activation(yb[:, 0, hf * BANK:(hf + 1) * BANK], ps[:, 4 + hf, :], ACT.Copy).then_inc(s_yb[L], 1)
                for hf in range(2):
                    act.wait_ge(s_yc[L], 4 * n + hf + 1)
                    half = slice(hf * BANK, (hf + 1) * BANK)
                    act.activation(yb[:, 1, half], MO["y_rest"][:, half], ACT.Copy).then_inc(s_yb[L], 1)

            def silu(n):
                act.wait_ge(s_gu[L], n + 1)
                act.activation(MO["sg"], ps[:, 2, 0:DE], ACT.Silu).then_inc(s_si[L], 1)

            def first(n, q, it):
                tokens(n)
                tokens2(n)
                turned(n, q)
                silu(n)

            def step(n, q, it):
                tokens(n)
                hidden(n - 1)
                tokens2(n)
                turned(n, q)
                parts(n - 1)
                silu(n)

            def last(n, q, it):
                hidden(n)
                parts(n)

            over_pairs(act, L, first, step, last)

        def moe_pairs_dve(v, L):
            v.wait_ge(s_disp, L + 1)
            v.wait_ge(s_acc0, 8 * L + NC)
            v.sem_inc(s_add[L], NC)

            def outputs(n):
                for hf in range(2):
                    half = slice(hf * BANK, (hf + 1) * BANK)
                    v.wait_ge(s_yb[L], 4 * n + hf + 1)
                    v.tensor_tensor(MO["y_rest"][:, half], ps[:, 4 + hf, :], yb[:, 0, half],
                                    ALU.subtract).then_inc(s_yc[L], 1)
                for hf in range(2):
                    half = slice(hf * BANK, (hf + 1) * BANK)
                    v.wait_ge(s_yb[L], 4 * n + hf + 3)
                    v.tensor_tensor(yb[:, 2, half], MO["y_rest"][:, half], yb[:, 1, half],
                                    ALU.subtract).then_inc(s_yc[L], 1)

            def hidden(n, q):
                v.wait_ge(s_si[L], n + 1)
                v.scalar_tensor_tensor(out=MO["h"], in0=MO["sg"], scalar=MO["own_gate"][:, q:q + 1],
                                       in1=ps[:, 2, DE:2 * DE], op0=ALU.mult, op1=ALU.mult).then_inc(s_h2[L], 1)

            def add(n, chunks=range(NC)):
                for c in chunks:
                    v.wait_ge(s_scat[L], NC * n + c + 1)
                    v.wait_ge(s_add[L], NC * n + c + 1)
                    v.tensor_tensor(MO["acc"][:, c, :], MO["acc"][:, c, :], ps[:, 6 + c % 2, 0:NT],
                                    ALU.add).then_inc(s_add[L], 1)

            def first(n, q, it):
                hidden(n, q)

            def step(n, q, it):
                outputs(n - 1)
                add(n - 1, range(NC - 2))
                hidden(n, q)
                add(n - 1, range(NC - 2, NC))

            def last(n, q, it):
                outputs(n)
                add(n)

            more = over_pairs(v, L, first, step, last)
            v.wait_ge(s_add[L], more * (2 * NC) + 3 * NC)

        s_op = sem("s_op")
        s_op_copied = [sem("s_op_copied_act"), sem("s_op_copied_dve")]
        s_tk = sem("s_tk")
        s_tk_copied = [sem("s_tk_copied_act"), sem("s_tk_copied_dve")]
        s_kst = [sem("s_kst_0"), sem("s_kst_1")]
        s_dp = sem("s_dp")
        s_qz1 = sem("s_qz1")
        s_g1 = [sem(f"s_g1_{b}") for b in range(4)]
        s_dd1 = sem("s_dd1")
        s_kt = sem("s_kt")
        s_kt_copied = [sem("s_kt_copied_act"), sem("s_kt_copied_dve")]
        s_sd1 = sem("s_sd1")
        s_sm1 = sem("s_sm1")
        s_ex1 = sem("s_ex1")
        s_p1 = sem("s_p1")
        s_p1c = sem("s_p1c")
        s_o1 = sem("s_o1")
        s_ot1 = sem("s_ot1")
        s_k1 = [sem(f"s_k1_{ck}") for ck in range(4)]
        s_v1 = sem("s_v1")

        W = OD["work"]
        kst = W[:, 0:3072].rearrange("p (b t n) -> p b t n", b=2, t=3)
        vst = W[:, 3072:3072 + 2304].rearrange("p (b i n) -> p b i n", b=2, i=4)
        OP = {"s": W[:, 0:1536].rearrange("p (b n) -> p b n", b=2), "pt": W[:, 1536:3072].rearrange("p (b n) -> p b n", b=2),
              "osb": W[:, 3072:3584], "dist": W[:, 3584:4736], "sm": W[:, 4736:4864].rearrange("p (k n) -> p k n", k=8)}
        qz1 = W[:, 0:3072].rearrange("p (g i r) -> p g i r", g=3, i=4)
        kns = W[:, 3072:3456].rearrange("p (g i n) -> p g i n", g=3, i=4)
        sm1 = W[:, 3456:3472]
        QK = OD["qk"].rearrange("p a g n -> p (a g n)")
        kt1 = QK[:, 0:4096].rearrange("p (f b i n) -> p f b i n", f=2, b=4, i=4)
        pt1 = QK[:, 4096:5376].rearrange("p (k r) -> p k r", k=10)
        dd1 = QK[:, 5376:5376 + DEC_W]
        o_all, o_own, o_twice = W[:, 4608:5120], W[:, 5120:5184], W[:, 5184:5312]
        xflat = xT[:, :, :].rearrange("p c t -> p (c t)")
        g1c = [xflat[:, 0:D], xflat[:, D:2 * D], xflat[:, 2 * D:3 * D], W[:, 3584:3584 + D]]
        s1 = mixT[:, 4:8, :].rearrange("p j t -> p (j t)")[:, 0:DEC_W]

        def chunk_of(b, ck):
            if ck == 4:
                return g1c[b % 4]
            at = ck * D if ck < 4 else 4 * D + (ck - 5) * D
            return ring[:, slot_of(6 + b), at:at + D]

        def tile_copied(k):
            return s_op_copied[k % 2], k // 2 + 1

        def turn_copied(n):
            return s_tk_copied[n % 2], n // 2 + 1

        def od_proj_pe(pe):
            pe.wait_ge(s_tp_copied[0], 9)
            pe.wait_ge(s_tp_copied[1], 9)
            for k in range(OD_TILES):
                g, kind, i = k // 12, k % 12 // 4, k % 4
                m = k // 6
                w = wait_slot(pe, 1, m).rearrange("p (c n) -> p c n", c=NC)
                if k >= 4:
                    pe.wait_ge(*tile_copied(k - 4))
                for c in range(NC):
                    ins = pe.matmul(ps[:, 2 + k % 4, 0:NT], w[:, c, (k % 6) * P:(k % 6 + 1) * P], xT[:, c, 0:NT],
                                    start=c == 0, stop=c == NC - 1)
                ins.then_inc(s_op, 1)
                if k % 6 == 5:
                    pe.wait_ge(s_op, k + 1)
                    pe.sem_inc(s_free[1][slot_of(m)], 1)
                if k % 12 in (7, 11):
                    pe.wait_ge(*tile_copied(k))
                    pe.wait_ge(*tile_copied(k - 1))
                    for t in range(3):
                        n = (2 * g + (kind == 2)) * 3 + t
                        if n >= 2:
                            pe.wait_ge(*turn_copied(n - 2))
                        mrow = ROWS[t]
                        for ii in range(4):
                            src = OD["k"][:, g, ii] if kind == 1 else vst[:, g % 2, ii]
                            ins = pe.transpose(ps[0:mrow, 6 + n % 2, ii * P:(ii + 1) * P],
                                               src[:, t * P:t * P + mrow], ident)
                        ins.then_inc(s_tk, 1)

        def od_proj_copy(eng, copy, parity):
            for k in range(OD_TILES):
                g, kind, i = k // 12, k % 12 // 4, k % 4
                if k % 2 == parity:
                    eng.wait_ge(s_op, k + 1)
                    dst = (OD["q"][:, g, i], OD["k"][:, g, i], vst[:, g % 2, i])[kind]
                    copy(dst, ps[:, 2 + k % 4, 0:NT]).then_inc(s_op_copied[parity], 1)
                if k % 12 in (7, 11):
                    for t in range(3):
                        n = (2 * g + (kind == 2)) * 3 + t
                        if n % 2 != parity:
                            continue
                        eng.wait_ge(s_tk, n + 1)
                        mrow = ROWS[t]
                        if kind == 1:
                            if g == 2:
                                eng.wait_ge(s_kst[0], 16 * 2)
                            dst = kst[0:mrow, g % 2, t, :]
                        else:
                            dst = OD["v"][0:mrow, g, t, :]
                        copy(dst, ps[0:mrow, 6 + n % 2, :]).then_inc(s_tk_copied[parity], 1)

        def od_dec_prepare(v):
            v.wait_ge(s_ot, 2 + 2)
            ch = Chain(v, s_qz1)
            ch(v.memset(qz1, 0.0))
            q8 = qz1.rearrange("p g i (b h t) -> p g i h b t", h=NH, t=TS)
            for g in range(3):
                for i in range(4):
                    src = OD["q"][:, g, i, NPR:NT].rearrange("p (b t) -> p b t", t=TS)
                    for s in range(2):
                        rows = slice(HD * s, HD * s + HD)
                        v.tensor_copy(q8[rows, g, i, 2 * i + s], src[rows]).then_inc(s_qz1, 1)
            v.tensor_copy(kns, OD["k"][:, :, :, NPR:NT]).then_inc(s_qz1, 1)
            v.wait_ge(s_qz1, 26)

        def kt_copied(n):
            return s_kt_copied[n % 2], n // 2 + 1

        def od_dec_pe(pe):
            pe.wait_ge(s_qz1, 26)
            for g in range(2):
                def turn(ck):
                    for bb in range(4):
                        n = 28 * g + 4 * ck + bb
                        if g == 0 and ck == 0:
                            wait_slot(pe, 1, 6 + bb)
                        if g == 0 and ck == 4:
                            pe.wait_ge(s_g1[bb], 16)
                        if g and bb == 0:
                            pe.wait_ge(s_k1[ck // 2], 16 * (8 if ck < 6 else 4))
                        if n >= 2:
                            pe.wait_ge(*kt_copied(n - 2))
                        for i in range(4):
                            ins = pe.transpose(ps[:, n % 2, i * P:(i + 1) * P],
                                               chunk_of(4 * g + bb, ck)[:, i * P:(i + 1) * P], ident)
                        ins.then_inc(s_kt, 1)

                def scores(ck):
                    pe.wait_ge(*kt_copied(28 * g + 4 * ck + 2))
                    pe.wait_ge(*kt_copied(28 * g + 4 * ck + 3))
                    if ck == 0 and g:
                        pe.wait_ge(s_sm1, 1)
                    bank, col, gg = (2, ck * P, 1) if ck < 4 else (3, (ck - 4) * P, 0 if ck == 4 else 2)
                    for i in range(4):
                        for bb in range(4):
                            b = 4 * g + bb
                            ins = pe.matmul(ps[32 * bb:32 * bb + 32, bank, col:col + P],
                                            qz1[:, gg, i, 32 * b:32 * b + 32], kt1[:, ck % 2, bb, i, :],
                                            start=i == 0, stop=i == 3)
                    ins.then_inc(s_sd1, 1)

                turn(0)
                for ck in range(7):
                    if ck < 6:
                        turn(ck + 1)
                    scores(ck)
                    if g and ck == 0:
                        outputs_t(pe, 0)
                for gg in range(3):
                    for i in range(4):
                        ins = pe.matmul(ps[:, 3, 384 + 32 * gg:416 + 32 * gg], qz1[:, gg, i, P * g:P * g + P],
                                        kns[:, gg, i, :], start=i == 0, stop=i == 3)
                ins.then_inc(s_sd1, 1)
                pe.wait_ge(s_ex1, g + 1)
                flat = ps[:, 4:7, :].rearrange("p b n -> p (b n)")
                if g:
                    pe.wait_ge(s_p1c, 2)
                    pe.wait_ge(s_mix[1], 2)
                for ck in range(7):
                    pe.transpose(flat[:, ck * P:(ck + 1) * P], s1[:, ck * P:(ck + 1) * P], ident)
                for gg in range(3):
                    ins = pe.transpose(flat[0:NSA, (7 + gg) * P:(8 + gg) * P], s1[:, OLD + gg * NSA:OLD + (gg + 1) * NSA],
                                       ident)
                ins.then_inc(s_p1, 1)
                pe.wait_ge(s_p1c, 2 * g + 2)
                if g:
                    pe.wait_ge(s_sm1, 5)
                    pe.wait_ge(s_v1, 16 * 16)
                for ck in range(7):
                    for bb in range(4):
                        pe.matmul(ps[32 * bb:32 * bb + 32, 7, :], pt1[:, ck, 32 * bb:32 * bb + 32],
                                  chunk_of(4 * g + bb, ck)[:, 512:1024], start=ck == 0, stop=False)
                for gg in range(3):
                    ins = pe.matmul(ps[:, 7, :], pt1[0:NSA, 7 + gg, :], OD["v"][0:NSA, gg, 2, :], start=False,
                                    stop=gg == 2)
                ins.then_inc(s_o1, 1)
                pe.wait_ge(s_o1, g + 1)
                for bb in range(4):
                    pe.sem_inc(s_free[1][slot_of(6 + 4 * g + bb)], 1)
            outputs_t(pe, 1)

        def outputs_t(pe, g):
            pe.wait_ge(s_sm1, 8 * g + 8)
            pe.transpose(ps[:, 4, 0:P], o_twice, ident).then_inc(s_ot1, 1)

        def od_dec_keys(eng, copy, parity, g, ck):
            for bb in range(parity, 4, 2):
                n = 28 * g + 4 * ck + bb
                eng.wait_ge(s_kt, n + 1)
                if g or ck >= 2:
                    eng.wait_ge(s_sd1, 8 * g + max(ck - 1, 0))
                copy(kt1[:, ck % 2, bb], ps[:, n % 2, :].rearrange("p (i n) -> p i n", i=4)).then_inc(
                    s_kt_copied[parity], 1)

        def od_dec_dve(v):
            def outputs_copy(g):
                v.wait_ge(s_ot1, g + 1)
                for s in range(2):
                    rows = slice(HD * s, HD * s + HD)
                    dst = mixT[rows, 0:4, NPR + 16 * g:NPR + 16 * g + 16].rearrange("p i (b t) -> p i b t", t=TS)
                    src = ps[rows, 4, 0:P].rearrange("p (b i s t) -> p s i b t", b=4, i=4, s=2)[:, s]
                    v.tensor_copy(dst, src).then_inc(s_mix[1], 1)

            for g in range(2):
                for ck in range(7):
                    od_dec_keys(v, v.tensor_copy, 1, g, ck)
                    if g and ck == 1:
                        outputs_copy(0)
                steps = 8 * g

                def step(ins):
                    nonlocal steps
                    steps += 1
                    ins.then_inc(s_sm1, 1)
                    v.wait_ge(s_sm1, steps)
                v.wait_ge(s_sd1, 8 * g + 8)
                v.wait_ge(s_dd1, 16 * (g + 1))
                if g:
                    v.wait_ge(s_p1, 1)
                c = lambda k: sm1[:, 4 * g + k:4 * g + k + 1]
                step(v.scalar_tensor_tensor(out=s1, in0=dd1, scalar=row_slope,
                                            in1=banks(2, DEC_W), op0=ALU.mult, op1=ALU.add))
                step(v.tensor_reduce(c(0), s1, AX.X, ALU.max))
                step(v.tensor_scalar(c(1), c(0), -SCALE, None, ALU.mult))
                v.wait_ge(s_ex1, g + 1)
                step(v.reciprocal(c(3), c(2)))
                v.wait_ge(s_o1, g + 1)
                own = row_head.unsqueeze(2).broadcast_to([P, NH, HD])
                step(v.tensor_tensor(o_all.rearrange("p (h d) -> p h d", h=NH),
                                     ps[:, 7, :].rearrange("p (h d) -> p h d", h=NH), own, ALU.mult))
                step(v.tensor_reduce(o_own, o_all.rearrange("p (h d) -> p d h", h=NH), AX.X, ALU.add))
                for s in range(2):
                    step(v.tensor_scalar(o_twice[:, s * HD:(s + 1) * HD], o_own, c(3), None, ALU.mult))
            outputs_copy(1)

        def od_dec_act(act):
            copy = lambda dst, src: act.activation(dst, src, ACT.Copy)
            for g in range(2):
                for ck in range(7):
                    od_dec_keys(act, copy, 0, g, ck)
                c = lambda k: sm1[:, 4 * g + k:4 * g + k + 1]
                act.wait_ge(s_sm1, 8 * g + 3)
                act.activation(s1, s1, ACT.Exp, bias=c(1), scale=SCALE, accum_out=c(2)).then_inc(s_ex1, 1)
                act.wait_ge(s_p1, g + 1)
                flat = ps[:, 4:7, :].rearrange("p b n -> p (b n)")
                if g:
                    act.wait_ge(s_o1, 1)
                act.activation(pt1[:, 0:7, :], flat[:, 0:7 * P].rearrange("p (k r) -> p k r", k=7),
                               ACT.Copy).then_inc(s_p1c, 1)
                act.activation(pt1[0:NSA, 7:10, :], flat[0:NSA, 7 * P:10 * P].rearrange("p (k r) -> p k r", k=3),
                               ACT.Copy).then_inc(s_p1c, 1)

        s_small = sem("s_small")
        s_copy = sem("s_copy")
        block = ctx.enter_context(nc.Block())

        even = Prompt(0, 1, EV["s"], EV["pt"], EV["osb"], EV["sm"],
                      (EV["dist"][:, 0:P], EV["dist"][:, P:3 * P]),
                      lambda g, h, qb: (EV["q"][64 * (h // 4):64 * (h // 4) + 64, h % 4, qb * P:(qb + 1) * P],
                                        EV["kv"][64 * (h // 4):64 * (h // 4) + 64, 0, 0:(qb + 1) * P]),
                      lambda g, h, kb: EV["vtok"][:, kb, 64 * (h // 4):64 * (h // 4) + 64],
                      lambda h: ((h % 4) * 2 + h // 4) * HD)
        odd = Prompt(1, 3, OP["s"], OP["pt"], OP["osb"], OP["sm"], (OP["dist"][:, 0:3 * P], OP["dist"][:, 3 * P:9 * P]),
                     lambda g, h, qb: (OD["q"][64 * (h % 2):64 * (h % 2) + 64, g, h // 2, qb * P:(qb + 1) * P],
                                       OD["k"][64 * (h % 2):64 * (h % 2) + 64, g, h // 2, 0:(qb + 1) * P]),
                     lambda g, h, kb: OD["v"][:, g, kb, h * HD:(h + 1) * HD],
                     lambda h: h * HD)
        N_OUT = {"l0": 0}

        @block.sync
        def _(sp):
            def load(layer, m, parts):
                n = reads_before(layer, m)
                if n:
                    sp.wait_ge(s_free[layer][slot_of(m)], n)
                for dst, src in parts:
                    sp.dma_start(dst, src).then_inc(s_ring[layer][slot_of(m)], 16)

            def rows8(w):
                return w.rearrange("(p c) n -> p c n", c=NC)

            def in_cols(w, m, total):
                n = min(768, total - 768 * m)
                dst = ring[:, slot_of(m), 0:NC * n].rearrange("p (c n) -> p c n", c=NC)
                return [(dst, rows8(w)[:, :, 768 * m:768 * m + n])]

            def glu(slot, wg, wu, wd):
                return [(ring[:, slot, 0:2048].rearrange("p (c n) -> p c n", c=NC), rows8(wg)),
                        (ring[:, slot, 2048:4096].rearrange("p (c n) -> p c n", c=NC), rows8(wu)),
                        (ring[:, slot, 4096:6144].rearrange("p (j n) -> p j n", j=2), wd.rearrange("(j p) n -> p j n", p=P))]

            def experts(L):
                w = (a["w_exp_gate"][L], a["w_exp_up"][L], a["w_exp_down"][L])

                def four(i, first):
                    for u in range(4):
                        q = u // 2
                        s = slot_of(EXP0[L] + u)
                        e = u if first else (i % 16) * 4 + u
                        one = [x[e] if first else x[bass.ds(e, 1)].rearrange("a k n -> (a k) n") for x in w]
                        gate, up, down = glu(s, *one)
                        if first:
                            sp.wait_ge(s_free[L][s], static_reads[L][s])
                        else:
                            sp.wait_ge(s_gu[L], 2 * i - 1 + q)
                        for dst, src in (gate, up):
                            sp.dma_start(dst, src).then_inc(s_ring[L][s], 16)
                        downs = [down] if u % 2 == 0 else [*downs, down]
                        if u % 2:
                            if not first:
                                sp.wait_ge(s_dn[L], 2 * i - 1 + q)
                            for dst, src in downs:
                                sp.dma_start(dst, src).then_inc(s_ring_dn[L][q], 16)

                four(0, True)
                with sp.Fori(1, NE // 4) as i:
                    four(i, False)
                sp.wait_ge(s_disp, L + 1)
                more = iterations(sp)
                with sp.If(more > NE // 4 - 1):
                    with sp.Fori(NE // 4, more + 1) as i:
                        four(i, False)
                with sp.Else():
                    sp.nop()
                return more

            def gain_bias(turn, g, b):
                if turn:
                    sp.wait_ge(s_gb_free, turn)
                else:
                    sp.wait_ge(s_od, 1)
                sp.dma_start(gb[:, 0, :], g.rearrange("(a n) -> a n", a=1).broadcast_to([P, D])).then_inc(s_gb, 16)
                sp.dma_start(gb[:, 1, :], b.rearrange("(a n) -> a n", a=1).broadcast_to([P, D])).then_inc(s_gb, 16)

            def router(L):
                sp.dma_start(MO["wr"], rows8(a["w_router"][L])).then_inc(s_wr, 16)
                sp.dma_start(MO["rb"], a["router_bias"][L:L + 1, :].broadcast_to([P, NE])).then_inc(s_wr, 16)

            sp.dma_start(square[:, :], a["c_square"]).then_inc(s_const, 16)
            sp.dma_start(misc[:, :], a["c_misc"]).then_inc(s_const, 16)
            xp = a["x_prompt"][0].rearrange("(t p) n -> t p n", p=P)
            for t in range(2):
                sp.dma_start(x_tok[:, t, :], xp[t]).then_inc(s_x, 16)
            sp.wait_ge(s_pad, 1)
            sp.dma_start(x_tok[0:NSA, 2, :], a["x_sample"].rearrange("b t n -> (b t) n")).then_inc(s_x, 16)
            load(0, 0, in_cols(a["w_in_even"][0], 0, EV_COLS))
            st = EV["st_in"]
            for dst, src in ((st[0:24, :], a["state_lru_conv"][0].rearrange("b k n -> (b k) n")),
                             (st[24:32, :], a["state_lru_h"][0]), (st[32:36, :], a["conv_w"][0]),
                             (st[36:37, :], a["conv_b"]), (st[37:38, :], a["b_rgate"]), (st[38:39, :], a["b_igate"]),
                             (st[39:40, :], a["lru_lambda"])):
                sp.dma_start(dst, src).then_inc(s_ev_par, 16)
            w1 = ring[:, 1, :].rearrange("p (c n) -> p c n", c=NC)
            src = rows8(a["w_in_even"][0])
            parts = [(w1[:, :, 0:256], src[:, :, 768:q0])]
            for h in range(NH):
                at = 256 + ((h % 4) * 2 + h // 4) * HD
                parts.append((w1[:, :, at:at + HD], src[:, :, q0 + h * HD:q0 + (h + 1) * HD]))
            load(0, 1, parts)
            sp.wait_ge(s_wg0, 1)
            for kind, w in enumerate((a["w_rgate"][0], a["w_igate"][0])):
                for s in range(2):
                    rows = slice(HD * s, HD * s + HD)
                    sp.dma_start(EV["wg"][rows, kind:8:2, rows],
                                 w.rearrange("(j s) c d -> s c j d", s=2)[s]).then_inc(s_wg, 16)
            load(0, 2, in_cols(a["w_in_even"][0], 2, EV_COLS))
            sp.dma_start(EV["sink"][:, 0:NH], a["swa_sinks"].broadcast_to([P, NH])).then_inc(s_small, 16)
            sp.dma_start(EV["dist"][:, 0:P], a["c_prompt"][:, 0:P]).then_inc(s_small, 16)
            sp.dma_start(EV["dist"][:, P:3 * P], a["c_prompt"][:, 3 * P:5 * P]).then_inc(s_small, 16)
            sp.dma_start(EV["dd"], a["c_even"].rearrange("g p n -> p g n")).then_inc(s_small, 16)
            sp.dma_start(gb[:, :, :].rearrange("p a n -> p (a n)").rearrange("p (b n) -> p b n", b=NB),
                         a["cache_swa_kv"][0].rearrange("b k a h d -> k b (a h d)")).then_inc(s_cache, 16)

            def out_even(hf):
                w = a["w_out_even"][0]
                s = slot_of(3 + hf)
                dst = ring[:, s, 0:8 * BANK].rearrange("p (j n) -> p j n", n=BANK)
                cols = slice(hf * BANK, (hf + 1) * BANK)
                parts = [(dst[:, 0:4, :], w[0:512, cols].rearrange("(j p) n -> p j n", p=P))]
                for x in range(2):
                    parts.append((dst[HD * x:HD * x + HD, 4:8, :],
                                  w[512 + 256 * x:768 + 256 * x, cols].rearrange("(i d) n -> d i n", d=HD)))
                return parts
            load(0, 3, out_even(0))
            load(0, 4, out_even(1))
            load(0, 5, glu(slot_of(5), a["w_sh_gate"][0], a["w_sh_up"][0], a["w_sh_down"][0]))
            gain_bias(0, a["ln1_g"][0], a["ln1_b"][0])
            sp.wait_ge(s_f, 3)
            sp.wait_ge(s_sout, OUT0)
            router(0)
            gain_bias(1, a["ln2_g"][0], a["ln2_b"][0])
            more = experts(0)

            for m in range(RING):
                sp.wait_ge(s_dn[0], 2 * more + 1 + (m - EXP0[0]) % RING // 2)
                load(1, m, in_cols(a["w_in_odd"][0], m, 6 * 768))
            gain_bias(2, a["ln1_g"][1], a["ln1_b"][1])
            for m in range(4, 6):
                load(1, m, in_cols(a["w_in_odd"][0], m, 6 * 768))
            sp.wait_ge(s_kst[0], 16 * 2)
            sp.wait_ge(s_kst[1], 16 * 6)
            sp.wait_ge(s_tk, 18)
            sp.dma_start(OP["dist"], a["c_prompt"]).then_inc(s_dp, 16)

            def rows_of(b, ck):
                if ck < 4:
                    return a["cache_dil2_kv"][0, b].rearrange("(k p) a h d -> k p (a h d)", p=P)[ck]
                if ck == 4:
                    return a["cache_dil1_kv"][0, b].rearrange("k a h d -> k (a h d)")
                d3 = a["cache_dil3_kv"][0, b].rearrange("(s r) a h d -> s r (a h d)", r=16)
                return d3[32 * (ck - 5):32 * (ck - 4), 0:TS, :]

            for b in range(4):
                d2 = a["cache_dil2_kv"][0, b].rearrange("(k p) a h d -> p k (a h d)", p=P)
                parts = [(ring[:, slot_of(6 + b), 0:4 * D].rearrange("p (k n) -> p k n", k=4), d2)]
                load(1, 6 + b, parts + [(chunk_of(b, ck), rows_of(b, ck)) for ck in (5, 6)])
            sp.wait_ge(s_op, OD_TILES)
            for b in range(4):
                if b == 3:
                    sp.wait_ge(s_qz1, 26)
                sp.dma_start(chunk_of(b, 4), rows_of(b, 4)).then_inc(s_g1[b], 16)
            sp.dma_start(dd1, a["c_odd"][0]).then_inc(s_dd1, 16)
            for ck in range(7):
                for bb in range(4):
                    sp.wait_ge(s_kt, 4 * ck + bb + 1)
                    sp.dma_start(chunk_of(4 + bb, ck)[:, 0:512], rows_of(4 + bb, ck)[..., 0:512]).then_inc(s_k1[ck // 2], 16)
            sp.wait_ge(s_sm1, 1)
            sp.dma_start(dd1, a["c_odd"][1]).then_inc(s_dd1, 16)
            for bb in range(4):
                b, s = 4 + bb, slot_of(6 + bb)
                sp.wait_ge(s_free[1][s], reads_before(1, 6 + b))
                d2 = a["cache_dil2_kv"][0, b].rearrange("(k p) a h d -> p k (a h d)", p=P)
                sp.dma_start(ring[:, s, 0:4 * D].rearrange("p (k n) -> p k n", k=4)[:, :, 512:1024],
                             d2[:, :, 512:1024]).then_inc(s_v1, 16)
                for ck in (4, 5, 6):
                    sp.dma_start(chunk_of(b, ck)[:, 512:1024], rows_of(b, ck)[..., 512:1024]).then_inc(s_v1, 16)
            load(1, 14, [(ring[:, slot_of(14), 0:4 * D].rearrange("p (j n) -> p j n", j=4),
                          a["w_out_odd"][0].rearrange("(j p) n -> p j n", p=P))])
            load(1, 15, glu(slot_of(15), a["w_sh_gate"][1], a["w_sh_up"][1], a["w_sh_down"][1]))
            sp.wait_ge(s_f, 9)
            sp.wait_ge(s_sout, OUT1)
            router(1)
            gain_bias(3, a["ln2_g"][1], a["ln2_b"][1])
            experts(1)
            for t in range(3):
                sp.wait_ge(s_xn, 9 + t + 1)
                if t < 2:
                    dst = o["y_prompt"][0].rearrange("(t p) n -> t p n", p=P)[t]
                else:
                    dst = o["y_sample"].rearrange("b t n -> (b t) n")
                sp.dma_start(dst, x_tok[0:ROWS[t], t, :]).then_inc(s_x, 16)
            sp.wait_ge(s_x, 16 * 3 + 16 * 3)

        @block.gpsimd
        def _(pool):
            pool.memset(EV["wg"], 0.0).then_inc(s_wg0, 1)

            def shift(dst, src, w):
                for b in range(NB):
                    pool.dma_start(dst[0, b, 0:w - TS].rearrange("k a h d -> k (a h d)"),
                                   src[0, b, TS:w].rearrange("k a h d -> k (a h d)")).then_inc(s_copy, 16)
            names = (("swa_kv_sample", "cache_swa_kv", P), ("dil1_kv_sample", "cache_dil1_kv", WIN[0]),
                     ("dil2_kv_sample", "cache_dil2_kv", WIN[1]), ("dil3_kv_sample", "cache_dil3_kv", WIN[2]))
            pool.wait_ge(s_ring[0][slot_of(2)], loaded(0, 2))
            shift(o[names[3][0]], a[names[3][1]], names[3][2])
            n = 0

            def store(dst, src):
                nonlocal n
                n += 1
                pool.dma_start(dst, src).then_inc(s_sout, 16)
            pool.wait_ge(s_kvt_copied, 2)
            for kind, name in enumerate(("ktok", "vtok")):
                store(o["swa_kv_prompt"][0, 0, :, kind].rearrange("t h d -> t (h d)"), EV[name][:, 1, :])
                store(o["swa_kv_sample"][0, :, P - TS:P, kind].rearrange("b t h d -> b t (h d)"), EV[name][0:NSA, 2, :])
            pool.wait_ge(s_so_copied, 1)
            so = EV["st_out"]
            store(o["lru_h_prompt"][0], so[0:1, :])
            store(o["lru_h_sample"][0], so[1:9, :])
            store(o["lru_conv_prompt"][0, 0], so[9:12, :])
            store(o["lru_conv_sample"][0].rearrange("b k n -> (b k) n"), so[12:36, :])
            assert 16 * n == OUT0
            moe_pairs_pool(pool, 0)
            pool.wait_ge(s_ring[1][slot_of(5)], loaded(1, 5))
            for dst, src, w in names[:3]:
                shift(o[dst], a[src], w)
            for g in range(3):
                keep = WIN[g] if g == 0 else NPR
                o_p, o_s = o[f"dil{g + 1}_kv_prompt"], o[f"dil{g + 1}_kv_sample"]
                for kind in range(2):
                    for par in range(2):
                        last = (2 * g + kind) * 3 + 2
                        k, v_ = turn_copied(last if last % 2 == par else last - 1)
                        pool.wait_ge(k, v_)
                    src = (lambda t, m: kst[0:m, g % 2, t, :]) if kind == 0 else (lambda t, m: OD["v"][0:m, g, t, :])
                    for t in range(2):
                        at = t * P - (NPR - keep)
                        if at >= 0:
                            ins = (o_p[0, 0, at:at + P, kind].rearrange("t h d -> t (h d)"), src(t, P))
                            if kind == 0:
                                pool.dma_start(*ins).then_inc(s_kst[g > 0], 16)
                            else:
                                store(*ins)
                    ins = (o_s[0, :, WIN[g] - TS:WIN[g], kind].rearrange("b t h d -> b t (h d)"), src(2, NSA))
                    if kind == 0:
                        pool.dma_start(*ins).then_inc(s_kst[g > 0], 16)
                    else:
                        store(*ins)
            assert 16 * n == OUT1
            moe_pairs_pool(pool, 1)
            pool.wait_ge(s_sout, OUT1)
            pool.wait_ge(s_copy, 16 * 4 * NB)

        @block.scalar
        def _(act):
            copy = lambda dst, src: act.activation(dst, src, ACT.Copy)
            xt_copy(act, copy, 0, 0)
            ev_proj_act(act)
            ev_kvt_act(act)
            ev_lru_act(act)
            prompt_act(act, even)
            ev_dec_act(act)
            act.wait_ge(s_so, 1)
            copy(EV["st_out"][0:36, :], ps[0:36, 7, :]).then_inc(s_so_copied, 1)
            ln_act(act, 0)
            for L in range(2):
                xt_copy(act, copy, 2 * L + 1, 0)
                moe_act_head(act, L)
                moe_shared_acc_act(act, L)
                moe_pairs_act(act, L)
                ln_act(act, 2 * L + 1)
                if L == 0:
                    xt_copy(act, copy, 2, 0)
                    od_proj_copy(act, copy, 0)
                    prompt_act(act, odd)
                    od_dec_act(act)
                    ln_act(act, 2)

        @block.vector
        def _(v):
            v.wait_ge(s_const, 32)
            v.tensor_copy(ident_b[:, :], ident).then_inc(s_const, 1)
            v.memset(x_tok[:, 2, :], 0.0).then_inc(s_pad, 1)
            xt_copy(v, v.tensor_copy, 0, 1)
            ev_proj_dve(v)
            ev_lru_dve(v)
            v.memset(xT[:, :, NT:NTP], 0.0).then_inc(s_pad, 1)
            ev_dec_qz(None, v)
            v.wait_ge(s_small, 64)
            ch = lru["chain"]
            ch(v.tensor_scalar(EV["sink"][:, NH:2 * NH], EV["sink"][:, 0:NH], -1.0, None, ALU.mult))
            ch(v.tensor_tensor(EV["sink"][:, 2 * NH:3 * NH], EV["sink"][:, 0:NH], row_head, ALU.mult))
            ch(v.tensor_reduce(EV["sink"][:, 24:25], EV["sink"][:, 2 * NH:3 * NH], AX.X, ALU.add))
            prompt_dve(v, even)
            ev_dec_dve(v)
            ln_dve(v, 0, False)
            for L in range(2):
                xt_copy(v, v.tensor_copy, 2 * L + 1, 1)
                moe_route_dve(v, L)
                moe_shared_dve(v, L)
                moe_pos_dve(v, L)
                moe_pairs_dve(v, L)
                ln_dve(v, 2 * L + 1, True)
                if L == 0:
                    xt_copy(v, v.tensor_copy, 2, 1)
                    od_proj_copy(v, v.tensor_copy, 1)
                    v.wait_ge(s_dp, 16)
                    prompt_dve(v, odd)
                    od_dec_prepare(v)
                    od_dec_dve(v)
                    v.memset(xT[:, :, NT:NTP], 0.0).then_inc(s_pad, 1)
                    ln_dve(v, 2, False)

        @block.tensor
        def _(pe):
            pe.wait_ge(s_const, 33)
            xt_pe(pe, 0)
            ev_state_pe(pe)
            ev_proj_pe(pe)
            ev_kvt_pe(pe)
            ev_gate_pe(pe)
            pe.wait_ge(s_gate_act, 8)
            pe.wait_ge(s_kvt_copied, 2)
            prompt_pe(pe, even)
            ev_dec_pe(pe)
            pe.wait_ge(s_otc, 2)
            ev_state_out_pe(pe)
            pe.wait_ge(s_mix[0], 8)
            out_proj_pe(pe, 0, 8, (3, 4))
            for L in range(2):
                xt_pe(pe, 2 * L + 1)
                moe_route_pe(pe, L)
                moe_shared_pe(pe, L)
                moe_pos_pe(pe, L)
                moe_shared_down_pe(pe, L)
                moe_pairs_pe(pe, L)
                if L == 0:
                    xt_pe(pe, 2)
                    od_proj_pe(pe)
                    pe.wait_ge(s_op_copied[0], OD_TILES // 2)
                    pe.wait_ge(s_op_copied[1], OD_TILES // 2)
                    pe.wait_ge(s_tk_copied[0], 9)
                    pe.wait_ge(s_tk_copied[1], 9)
                    prompt_pe(pe, odd)
                    od_dec_pe(pe)
                    pe.wait_ge(s_mix[1], 4)
                    pe.wait_ge(s_otc, 2 + 2)
                    pe.wait_ge(s_pad, 3)
                    out_proj_pe(pe, 1, 4, (14,))


_INS = ['x_prompt', 'x_sample', 'state_lru_h', 'state_lru_conv', 'cache_swa_kv', 'cache_dil1_kv', 'cache_dil2_kv',
        'cache_dil3_kv', 'w_in_even', 'conv_w', 'conv_b', 'w_rgate', 'b_rgate', 'w_igate', 'b_igate', 'lru_lambda',
        'swa_sinks', 'w_out_even', 'w_in_odd', 'w_out_odd', 'ln1_g', 'ln1_b', 'ln2_g', 'ln2_b', 'w_router',
        'router_bias', 'w_exp_gate', 'w_exp_up', 'w_exp_down', 'w_sh_gate', 'w_sh_up', 'w_sh_down']
_OUTS = [("y_prompt", (1, 256, 1024)), ("y_sample", (8, 4, 1024)), ("lru_h_prompt", (1, 1, 512)),
         ("lru_h_sample", (1, 8, 512)), ("lru_conv_prompt", (1, 1, 3, 512)), ("lru_conv_sample", (1, 8, 3, 512)),
         ("swa_kv_prompt", (1, 1, 128, 2, 2, 64)), ("swa_kv_sample", (1, 8, 128, 2, 2, 64)),
         ("dil1_kv_prompt", (1, 1, 128, 2, 8, 64)), ("dil1_kv_sample", (1, 8, 128, 2, 8, 64)),
         ("dil2_kv_prompt", (1, 1, 256, 2, 8, 64)), ("dil2_kv_sample", (1, 8, 512, 2, 8, 64)),
         ("dil3_kv_prompt", (1, 1, 256, 2, 8, 64)), ("dil3_kv_sample", (1, 8, 1024, 2, 8, 64))]


def kernel(**inputs):
    import numpy as _np
    import concourse.bacc as _bacc
    from concourse import mybir as _mybir
    from concourse.bass_utils import run_bass_kernel_spmd as _run

    nc = _bacc.Bacc("TRN2", target_bir_lowering=False, num_devices=1)
    arrays, a, o = {}, {}, {}
    for name in _INS:
        arrays[f"in_{name}"] = _np.ascontiguousarray(inputs[name])
    for name, table in tables().items():
        arrays[f"in_{name}"] = table
    for name, x in arrays.items():
        a[name[3:]] = nc.dram_tensor(name, x.shape, _mybir.dt.from_np(x.dtype), kind="ExternalInput").ap()
    for name, shape in _OUTS:
        o[name] = nc.dram_tensor(f"out_{name}", shape, F32, kind="ExternalOutput").ap()
    build(nc, a, o)
    r = _run(nc, [arrays], core_ids=[0])
    return tuple(r.results[0][f"out_{name}"] for name, _ in _OUTS)
```

```python
from contextlib import ExitStack

import numpy as np

import concourse.bass as bass
from concourse import mybir

F32 = mybir.dt.float32
I32 = mybir.dt.int32
BF16 = mybir.dt.bfloat16
ALU = mybir.AluOpType
ACT = mybir.ActivationFunctionType
AX = mybir.AxisListType

P = 128
D = 1024
NC = D // P
NPR, NSA = 256, 32
NT = NPR + NSA
NTP = 3 * P
NB, TS = 8, 4
ROWS = (P, P, NSA)
HD = 64
NH = 8
NE = 64
DE = 256
CAP = 64
PASSES = -(-NT // CAP)
SLOT = 6144
RING = 4
BANK = 512
ALPHA = float(4 ** 0.25)
EPS = 1e-5
SCALE = HD ** -0.5
BIG = 1e30
LRU_TILES = 4
CONVW = 4
SEQ_S = CONVW - 1 + TS
XRW = CONVW - 1 + NPR + NB * SEQ_S
CW = XRW - (CONVW - 1)
SAMP0 = NPR + CONVW - 1
WIN = (P, 512, 1024)
DIL = (1, 4, 16)
OLD = 7 * P
DEC_W = OLD + 3 * NSA
EV_COLS = 1792
OD_TILES = 36
OUT0 = 16 * 8
OUT1 = OUT0 + 16 * 8
MISC = 6 + PASSES + PASSES * CAP + 64 + 1 + NH


def tables():
    slopes = 2.0 ** -(np.arange(1, NH + 1))
    row = np.arange(P)
    bb, h, t = row // 32, (row % 32) // TS, row % TS
    far = 1e30

    def dist(d, ok):
        return np.where(ok, d, far).astype(np.float32)

    q, k = np.arange(NPR)[:, None], np.arange(NPR)[None, :]
    d = q - k
    win = dist(d, (d >= 0) & (d <= P))
    d4 = dist(d, (d >= 0) & (d % 4 == 0) & (d <= 512))
    d16 = dist(d, (d >= 0) & (d % 16 == 0) & (d <= 2048))
    prompt = np.concatenate([m[:P, :P] for m in (win, d4, d16)] + [m[P:] for m in (win, d4, d16)], axis=1)
    old1 = P + t[:, None] - np.arange(P)[None, :]
    old1 = dist(old1, (old1 <= P) & (old1 >= 0))
    d2 = WIN[1] + t[:, None] - np.arange(WIN[1])[None, :]
    d2 = dist(d2, (d2 % 4 == 0) & (d2 <= 512))
    pos3 = (np.arange(256) // TS) * 16 + np.arange(256) % TS
    d3 = WIN[2] + t[:, None] - pos3[None, :]
    d3 = dist(d3, d3 % 16 == 0)
    even, odd = [], []
    for g in range(2):
        nb_, nt_ = np.arange(NSA) // TS, np.arange(NSA) % TS
        same = (4 * g + bb)[:, None] == nb_[None, :]
        dn = t[:, None] - nt_[None, :]
        n1 = dist(dn, same & (dn >= 0))
        n4 = dist(dn, same & (dn == 0))
        even.append(np.concatenate([old1, n1], axis=1))
        odd.append(np.concatenate([d2, old1, d3, n1, n4, n4], axis=1))
    tri = (row[:, None] < row[None, :]).astype(np.float32)
    square = np.concatenate([np.eye(P), tri, np.ones((P, P))], axis=1)
    valid = np.ones((P, 3))
    valid[NSA:, 2] = 0
    g8 = np.arange(NH)
    before = (g8[None, :] < g8[:, None]).astype(np.float32).reshape(1, 64)
    misc = np.concatenate([
        valid, 1 - valid, np.tile(np.arange(1, PASSES + 1) * CAP, (P, 1)),
        np.tile(np.arange(PASSES * CAP), (P, 1)), np.tile(before, (P, 1)), (-8 * slopes[h])[:, None],
        (h[:, None] == g8[None, :])], axis=1)
    f = lambda a: np.ascontiguousarray(a, np.float32)
    return {"c_square": f(square), "c_misc": f(misc), "c_prompt": f(prompt),
            "c_even": f(np.stack(even)), "c_odd": f(np.stack(odd))}


class Chain:

    def __init__(self, eng, sem):
        self.eng, self.sem, self.n = eng, sem, 0

    def __call__(self, ins):
        self.n += 1
        ins.then_inc(self.sem, 1)
        self.eng.wait_ge(self.sem, self.n)


def slope8(h):
    return -8.0 * 2.0 ** -(h + 1)


def build(nc, a, o):
    ctx = ExitStack()
    with ctx:
        def sb(name, shape, dt=F32):
            return ctx.enter_context(nc.sbuf_tensor(name, shape, dt))

        def sem(name):
            return ctx.enter_context(nc.semaphore(name))

        def per_layer(name):
            return [sem(f"{name}_{layer}") for layer in range(2)]

        ps = ctx.enter_context(nc.psum_tensor("ps", [P, 8, BANK], F32))
        ring = sb("ring", [P, RING, SLOT])
        x_tok = sb("x_tok", [P, 3, D])
        xT = sb("xT", [P, NC, NTP])
        mixT = sb("mixT", [P, 8, NT])
        square = sb("square", [P, 3 * P])
        misc = sb("misc", [P, MISC])
        gb = sb("gb", [P, 2, D])
        stats = sb("stats", [P, 3, 8])
        ident, tri, ones = (square[:, i * P:(i + 1) * P] for i in range(3))
        ident_b = sb("ident_b", [P, P], BF16)
        valid, invalid = misc[:, 0:3], misc[:, 3:6]
        thresholds = misc[:, 6:6 + PASSES]
        iota0 = 6 + PASSES
        before = misc[:, iota0 + PASSES * CAP:iota0 + PASSES * CAP + 64]
        row_slope = misc[:, iota0 + PASSES * CAP + 64:iota0 + PASSES * CAP + 65]

        row_head = misc[:, MISC - NH:MISC]

        arena = sb("arena", [P, 16900])

        def cut(sizes, base=0):
            views, at = {}, base
            for name, shape in sizes:
                n = int(np.prod(shape))
                v = arena[:, at:at + n]
                if len(shape) == 2:
                    v = v.rearrange("p (a b) -> p a b", b=shape[1])
                elif len(shape) == 3:
                    v = v.rearrange("p (a b c) -> p a b c", b=shape[1], c=shape[2])
                views[name] = v
                at += n
            assert at <= 16900, at
            return views, at

        EV, _ = cut([("xr", (LRU_TILES, XRW)), ("xc", (LRU_TILES, CW)), ("rg", (LRU_TILES, CW)),
                     ("ig", (LRU_TILES, CW)), ("gel", (4, NT)), ("q", (4, NT)),
                     ("kv", (2, NT)), ("vtok", (3, P)), ("ktok", (3, P)), ("ktd", (NB, P)), ("qz", (NB, 32)),
                     ("s", (4, 256)), ("pt", (2, 256)), ("dist", (384,)), ("dd", (2, 160)), ("sd", (2, 160)),
                     ("ptd", (2, 2 * P)), ("osb", (512,)), ("st_in", (512,)), ("stc", (4, 36)), ("st_out", (512,)),
                     ("wg", (8, P)), ("st", (4, 40)), ("sp", (8, 4)), ("sink", (25,)), ("sm", (8, 16))])
        OD, _ = cut([("qk", (2, 3, 4 * NT)), ("v", (3, 3, 512)), ("work", (5380,))])
        OD["q"] = OD["qk"][:, 0].rearrange("p g (i t) -> p g i t", t=NT)
        OD["k"] = OD["qk"][:, 1].rearrange("p g (i t) -> p g i t", t=NT)
        MO, _ = cut([("acc", (NC, NT)), ("x_rest2", (D,)), ("xg", (NC, P)), ("yb", (3, D // 2)), ("y_rest", (D,)),
                     ("xb", (8, D // 2)), ("own_gate", (2,)), ("h", (DE,)), ("hT", (2, P)),
                     ("sg", (DE,)), ("pgt", (2, NT // 2)), ("pm", (2, 3, P // 2)), ("pg", (2, 3, P)),
                     ("wr", (NC, NE)), ("rb", (NE,)), ("scores", (3, NE)), ("biased", (3, NE)), ("top", (24, 8)),
                     ("gs", (3, 8)), ("gt", (3, 64)), ("eq", (3, 64)), ("rank", (3, 8)), ("t8", (3, 8)),
                     ("rep", (3, NE)), ("sel", (3, NE)), ("gate", (3, NE)), ("pos", (3, NE)), ("cnt", (16,)), ("cur", (2, CAP + 12))])
        MO["shg"], MO["sh"] = (MO["yb"].rearrange("p k n -> p (k n)")[:, k * 2 * NT:(k + 1) * 2 * NT].rearrange(
            "p (j t) -> p j t", j=2) for k in range(2))
        xb = MO["xb"].rearrange("p k n -> p (k n)").bitcast(BF16).rearrange("p (k n) -> p k n", k=8)
        x_rest = [mixT[:, :, :].rearrange("p j t -> p (j t)")[:, t * D:(t + 1) * D] for t in range(2)] + [MO["x_rest2"]]
        yb = MO["yb"].rearrange("p k n -> p (k n)").bitcast(BF16).rearrange("p (k n) -> p k n", k=3)
        pgt = MO["pgt"].rearrange("p q n -> p (q n)").bitcast(BF16).rearrange("p (q n) -> p q n", q=2)
        pm = MO["pm"].rearrange("p q t n -> p (q t n)").bitcast(BF16).rearrange("p (q t n) -> p q t n", q=2, t=3)
        n_iter = sb("n_iter", [P, 1], I32)

        s_const = sem("s_const")
        s_x = sem("s_x")
        s_pad = sem("s_pad")
        s_ring = [[sem(f"s_ring_{layer}_{s}") for s in range(RING)] for layer in range(2)]
        s_free = [[sem(f"s_free_{layer}_{s}") for s in range(RING)] for layer in range(2)]
        s_ring_dn = [[sem(f"s_ring_dn_{layer}_{q}") for q in range(2)] for layer in range(2)]
        EXP0 = (6, 16)
        SHARED = (5, 15)
        n_dma = [{0: 1, 1: 9, 2: 1, 3: 3, 4: 3, 5: 3},
                 {**{m: 1 for m in range(6)}, **{m: 3 for m in range(6, 10)}, **{m: 0 for m in range(10, 14)}, 14: 1, 15: 3}]

        def slot_of(m):
            return m % RING

        def loaded(layer, m):
            return 16 * sum(n for k, n in n_dma[layer].items() if k % RING == m % RING and k <= m)

        def reads_before(layer, m):
            return len([k for k in n_dma[layer] if k % RING == m % RING and k < m])

        static_dma = [[16 * sum(n for k, n in n_dma[layer].items() if k % RING == s) for s in range(RING)]
                      for layer in range(2)]
        static_reads = [[len([k for k in n_dma[layer] if k % RING == s]) for s in range(RING)] for layer in range(2)]

        def wait_slot(eng, layer, m):
            eng.wait_ge(s_ring[layer][slot_of(m)], loaded(layer, m))
            return ring[:, slot_of(m), :]

        def free_slot(ins, layer, m):
            ins.then_inc(s_free[layer][slot_of(m)], 1)

        s_tp = sem("s_tp")
        s_tp_copied = [sem("s_tp_copied_act"), sem("s_tp_copied_dve")]

        def xt_pe(pe, turn):
            for t in range(3):
                if turn == 0:
                    pe.wait_ge(s_x, 16 * 3)
                else:
                    wait_residual(pe, turn - 1, t)
                for hf in range(2):
                    n = turn * 3 + t
                    if n:
                        pe.wait_ge(s_tp_copied[hf], n)
                    for j in range(4):
                        c = 4 * hf + j
                        src = x_tok[0:ROWS[t], t, :].rearrange("t (p c) -> t c p", c=NC)[:, c, :]
                        ins = pe.transpose(ps[:, hf, j * P:j * P + ROWS[t]], src, ident[0:ROWS[t], 0:ROWS[t]])
                    ins.then_inc(s_tp, 1)

        def xt_copy(eng, copy, turn, hf):
            for t in range(3):
                eng.wait_ge(s_tp, 2 * (turn * 3 + t) + hf + 1)
                m = ROWS[t]
                src = ps[:, hf, :].rearrange("p (c t) -> p c t", t=P)[:, :, 0:m]
                copy(xT[:, 4 * hf:4 * hf + 4, t * P:t * P + m], src).then_inc(s_tp_copied[hf], 1)

        s_f = sem("s_f")
        s_ln = sem("s_ln")
        s_gb = sem("s_gb")
        s_gb_free = sem("s_gb_free")
        s_xn = sem("s_xn")
        s_rt_ln = sem("s_rt_ln")
        LN_S, LN_O, LN_G, LN_B, LN_ALL = (3, 6, 11), (8, 13, 17), (14, 18, 20), (15, 19, 21), 21
        LN_R, LN_N, LN_ALL_ACT = (2, 4, 7), (5, 8, 9), 9
        SUM0, SUM1, MINUS_MEAN, SQUARES, ROOT, RSTD, OFFSET, EPS_COL = range(8)

        def col(t, k):
            return stats[0:ROWS[t], t, k:k + 1]

        def wait_residual(eng, turn, t):
            eng.wait_ge(s_xn, 3 * turn + t + 1)
            eng.wait_ge(s_ln, LN_ALL * turn + LN_B[t])

        def ln_act(act, turn):
            def root(t):
                act.wait_ge(s_ln, LN_ALL * turn + LN_S[t])
                m = ROWS[t]
                scratch = ps[0:m, 2 * t:2 * t + 2, :].rearrange("p b n -> p (b n)")
                act.activation(scratch, x_tok[0:m, t, :], ACT.Square, bias=col(t, MINUS_MEAN),
                               accum_out=col(t, SQUARES)).then_inc(s_rt_ln, 1)
                act.wait_ge(s_rt_ln, LN_ALL_ACT * turn + LN_R[t] - 1)
                act.activation(col(t, ROOT), col(t, SQUARES), ACT.Sqrt, bias=col(t, EPS_COL),
                               scale=1 / D).then_inc(s_rt_ln, 1)

            def norm(t):
                act.wait_ge(s_ln, LN_ALL * turn + LN_O[t])
                z = x_tok[0:ROWS[t], t, :]
                act.activation(z, z, ACT.Identity, bias=col(t, OFFSET), scale=col(t, RSTD)).then_inc(s_rt_ln, 1)

            root(0)
            root(1)
            norm(0)
            root(2)
            norm(1)
            norm(2)

        def ln_pool(pool, turn):
            pool.wait_ge(s_gb, 32 * (turn + 1))
            for t in range(3):
                z = x_tok[0:ROWS[t], t, BANK:D]
                pool.wait_ge(s_ln, LN_ALL * turn + LN_G[t])
                pool.tensor_tensor(z, z, gb[0:ROWS[t], 1, BANK:D], ALU.add).then_inc(s_xn, 1)
            pool.wait_ge(s_xn, 3 * turn + 3)
            pool.wait_ge(s_ln, LN_ALL * (turn + 1))
            pool.sem_inc(s_gb_free, 1)

        def ln_dve(v, turn, permuted):
            n = LN_ALL * turn

            def done(ins, wait=True):
                nonlocal n
                n += 1
                ins.then_inc(s_ln, 1)
                if wait:
                    v.wait_ge(s_ln, n)

            def statistics(t):
                m = ROWS[t]
                z = x_tok[0:m, t, :]
                v.wait_ge(s_f, 3 * turn + t + 1)
                for hf in range(2):
                    f, x = ps[0:m, 2 * t + hf, :], z[:, hf * BANK:(hf + 1) * BANK]
                    if permuted:
                        f = f.rearrange("t (c p) -> t p c", c=4)
                        x = z.rearrange("t (p h c) -> t h p c", h=2, c=4)[:, hf]
                    done(v.scalar_tensor_tensor(out=x, in0=x, scalar=ALPHA, in1=f, op0=ALU.mult, op1=ALU.add,
                                                accum_out=col(t, SUM0 + hf)), hf)
                done(v.tensor_scalar(col(t, MINUS_MEAN), col(t, SUM0), col(t, SUM1), -1 / D, ALU.add, ALU.mult), False)

            def offset(t):
                v.wait_ge(s_rt_ln, LN_ALL_ACT * turn + LN_R[t])
                done(v.reciprocal(col(t, RSTD), col(t, ROOT)))
                done(v.tensor_tensor(col(t, OFFSET), col(t, MINUS_MEAN), col(t, RSTD), ALU.mult), False)

            def gain(t):
                z = x_tok[0:ROWS[t], t, :]
                v.wait_ge(s_rt_ln, LN_ALL_ACT * turn + LN_N[t])
                v.wait_ge(s_gb, 32 * (turn + 1))
                done(v.tensor_tensor(z, z, gb[0:ROWS[t], 0, :], ALU.mult))
                done(v.tensor_tensor(z[:, 0:BANK], z[:, 0:BANK], gb[0:ROWS[t], 1, 0:BANK], ALU.add), False)

            statistics(0)
            statistics(1)
            offset(0)
            statistics(2)
            offset(1)
            gain(0)
            offset(2)
            gain(1)
            gain(2)

        s_ep = sem("s_ep")
        s_ep_copied = [sem("s_ep_copied_act"), sem("s_ep_copied_dve")]
        s_ev_par = sem("s_ev_par")
        s_wg0 = sem("s_wg0")
        s_wg = sem("s_wg")
        s_arg = sem("s_arg")
        s_root = sem("s_root")
        s_st = sem("s_st")
        s_xr = sem("s_xr")
        s_conv = sem("s_conv")
        s_gate = sem("s_gate")
        s_gate_act = sem("s_gate_act")
        s_lru = sem("s_lru")
        s_lru_act = sem("s_lru_act")
        s_aout = sem("s_aout")
        s_so = sem("s_so")
        s_so_copied = sem("s_so_copied")
        s_kvt = sem("s_kvt")
        s_kvt_copied = sem("s_kvt_copied")
        s_qz = sem("s_qz")
        s_kd = sem("s_kd")
        s_kd_copied = sem("s_kd_copied")
        s_sd = sem("s_sd")
        s_sd_dve = sem("s_sd_dve")
        s_sd_exp = sem("s_sd_exp")
        s_ptd = sem("s_ptd")
        s_ptd_copied = sem("s_ptd_copied")
        s_od = sem("s_od")
        s_mix = [sem("s_mix_0"), sem("s_mix_1")]
        s_sout = sem("s_sout")
        q0, k0, v0 = D, D + 512, D + 640
        DVE_TILES = range(4)

        def copied_value(k):
            return (s_ep_copied[0], k - 4 + 1) if k >= 4 else (s_ep_copied[1], k + 1)

        def ev_proj_pe(pe, tiles):
            pe.wait_ge(s_tp_copied[0], 3)
            pe.wait_ge(s_tp_copied[1], 3)
            for k in tiles:
                m = k // 6
                w = wait_slot(pe, 0, m)
                w = w[:, 0:NC * min(768, EV_COLS - 768 * m)].rearrange("p (c n) -> p c n", c=NC)
                if k >= 4:
                    pe.wait_ge(*copied_value(k - 4))
                bank = 2 + k % 4
                for c in range(NC):
                    lhs = w[:, c, k * P - 768 * m:(k + 1) * P - 768 * m]
                    ins = pe.matmul(ps[:, bank, 0:NT], lhs, xT[:, c, 0:NT], start=c == 0, stop=c == NC - 1)
                ins.then_inc(s_ep, 1)
                if k % 6 == 5 or k == 13:
                    pe.wait_ge(s_ep, k + 1)
                    pe.sem_inc(s_free[0][slot_of(m)], 1)

        def ev_xr_dst(j):
            samp = EV["xr"][:, j, SAMP0:XRW].rearrange("p (b s) -> p b s", s=SEQ_S)
            return EV["xr"][:, j, CONVW - 1:CONVW - 1 + NPR], samp
        decay = mixT[:, :, :].rearrange("p j t -> p (j t)")[:, 8 * NT - LRU_TILES * CW:].rearrange(
            "p (j n) -> p j n", j=LRU_TILES)

        def ev_proj_act(act, tiles):
            for k in tiles:
                act.wait_ge(s_ep, k + 1)
                src = ps[:, 2 + k % 4, 0:NT]
                if k < 8:
                    ins = act.activation(EV["gel"][:, k - 4, :], src, ACT.Gelu_apprx_tanh)
                else:
                    dst = EV["q"][:, k - 8, :] if k < 12 else EV["kv"][:, k - 12, :]
                    ins = act.activation(dst, src, ACT.Copy)
                ins.then_inc(s_ep_copied[0], 1)

        lru = {}

        def ev_proj_dve(v):
            ch = lru["chain"] = Chain(v, s_lru)
            xr, xc = EV["xr"], EV["xc"]
            ch(v.memset(xr[:, :, 0:CONVW - 1], 0.0))
            v.wait_ge(s_st, 1)
            st = EV["st"]
            ch(v.tensor_copy(st, ps[:, 6, 0:160].rearrange("p (j n) -> p j n", n=40)))
            for j in range(LRU_TILES):
                _, samp = ev_xr_dst(j)
                ch(v.tensor_copy(samp[:, :, 0:CONVW - 1], st[:, j, 0:24].rearrange("p (b s) -> p b s", s=CONVW - 1)))

            lam, sp = st[:, :, 39], EV["sp"]
            ch(v.scalar_tensor_tensor(out=sp[:, 0, :], in0=lam, scalar=-1.0, in1=lam, op0=ALU.mult, op1=ALU.max))
            v.sem_inc(s_xr, 1)
            for j in DVE_TILES:
                v.wait_ge(s_ep, j + 1)
                prompt, samp = ev_xr_dst(j)
                ch(v.tensor_copy(prompt, ps[:, 2 + j, 0:NPR]))
                v.tensor_copy(samp[:, :, CONVW - 1:SEQ_S],
                              ps[:, 2 + j, NPR:NT].rearrange("p (b s) -> p b s", s=TS)).then_inc(s_ep_copied[1], 1)
                v.wait_ge(s_ep_copied[1], j + 1)
                ch(v.tensor_scalar(xc[:, j, :], xr[:, j, 0:CW], st[:, j, 32:33], st[:, j, 36:37], ALU.mult, ALU.add))
                for tap in range(1, CONVW):
                    ch(v.scalar_tensor_tensor(out=xc[:, j, :], in0=xr[:, j, tap:tap + CW],
                                              scalar=st[:, j, 32 + tap:33 + tap], in1=xc[:, j, :],
                                              op0=ALU.mult, op1=ALU.add))
                v.sem_inc(s_conv, 1)
            v.wait_ge(s_lru_act, 1)
            ch(v.tensor_scalar(sp[:, 2, :], sp[:, 1, :], 2.0, None, ALU.add))
            ch(v.reciprocal(sp[:, 3, :], sp[:, 2, :]))
            ch(v.tensor_tensor(sp[:, 2, :], sp[:, 1, :], sp[:, 3, :], ALU.mult))
            ch(v.tensor_tensor(sp[:, 3, :], sp[:, 2, :], sp[:, 2, :], ALU.mult))
            ch(v.tensor_scalar(sp[:, 4, :], sp[:, 3, :], 1 / 19, 1 / 17, ALU.mult, ALU.add))
            for n in range(15, 0, -2):
                ch(v.tensor_tensor(sp[:, 4, :], sp[:, 4, :], sp[:, 3, :], ALU.mult))
                ch(v.tensor_scalar(sp[:, 4, :], sp[:, 4, :], 1 / n, None, ALU.add))
            ch(v.scalar_tensor_tensor(out=sp[:, 4, :], in0=sp[:, 2, :], scalar=2.0, in1=sp[:, 4, :], op0=ALU.mult,
                                      op1=ALU.mult))
            ch(v.tensor_scalar(sp[:, 5, :], lam, -1.0, 0.0, ALU.mult, ALU.max))
            ch(v.tensor_tensor(sp[:, 5, :], sp[:, 5, :], sp[:, 4, :], ALU.add))
            ch(v.tensor_scalar(sp[:, 6, :], sp[:, 5, :], 8.0, None, ALU.mult))
            ch(v.tensor_scalar(sp[:, 7, :], sp[:, 5, :], -8.0, None, ALU.mult))
            v.sem_inc(s_xr, 1)

        def ev_lru_dve(v):
            ch, st = lru["chain"], EV["st"]
            xr, xc = EV["xr"], EV["xc"]

            def scan_input(j):
                v.wait_ge(s_lru_act, 1 + LRU_TILES + j + 1)
                aa, rg, ig = decay[:, j], EV["rg"][:, j, :], EV["ig"][:, j, :]
                ch(v.tensor_tensor(ig, ig, xc[:, j, :], ALU.mult))
                ch(v.tensor_tensor(xc[:, j, :], aa, aa, ALU.mult))
                ch(v.scalar_tensor_tensor(out=rg, in0=xc[:, j, :], scalar=1.0, in1=rg, op0=ALU.add, op1=ALU.mult))
                v.sem_inc(s_arg, 1)

            def scan(j):
                aa, rg, ig = decay[:, j], EV["rg"][:, j, :], EV["ig"][:, j, :]
                v.wait_ge(s_root, j + 1)
                ch(v.tensor_tensor(ig, ig, rg, ALU.mult))
                first = slice(SAMP0 - 1, SAMP0 - 1 + SEQ_S * (NB - 1) + 1, SEQ_S)
                ch(v.memset(aa[:, first], 0.0))
                ch(v.tensor_copy(ig[:, first], st[:, j, 24:32]))
                ch(v.tensor_tensor_scan(xc[:, j, :], aa, ig, 0.0, ALU.mult, ALU.add))
                gel = EV["gel"][:, j, :]
                v.wait_ge(s_ep_copied[0], j + 1)
                ch(v.tensor_tensor(mixT[:, j, 0:NPR], xc[:, j, 0:NPR], gel[:, 0:NPR], ALU.mult))
                samp = EV["xc"].rearrange("p j n -> p (j n)")[:, j * CW + SAMP0:j * CW + SAMP0 + (NB - 1) * SEQ_S]
                dst = mixT[:, j, NPR:NT].rearrange("p (b s) -> p b s", s=TS)
                g3 = gel[:, NPR:NT].rearrange("p (b s) -> p b s", s=TS)
                ch(v.tensor_tensor(dst[:, 0:NB - 1], samp.rearrange("p (b s) -> p b s", s=SEQ_S)[:, :, 0:TS],
                                   g3[:, 0:NB - 1], ALU.mult))
                last = SAMP0 + (NB - 1) * SEQ_S
                ch(v.tensor_tensor(dst[:, NB - 1], xc[:, j, last:last + TS], g3[:, NB - 1], ALU.mult))

            scan_input(0)
            for j in range(LRU_TILES):
                if j + 1 < LRU_TILES:
                    scan_input(j + 1)
                scan(j)
            stc = EV["stc"]
            ch(v.tensor_copy(stc[:, :, 0:1], xc[:, :, NPR - 1:NPR]))
            ch(v.tensor_copy(stc[:, :, 1:9], xc[:, :, SAMP0 + TS - 1:SAMP0 + TS + SEQ_S * (NB - 1):SEQ_S]))
            ch(v.tensor_copy(stc[:, :, 9:12], xr[:, :, NPR:NPR + 3]))
            for j in range(LRU_TILES):
                _, samp = ev_xr_dst(j)
                ch(v.tensor_copy(stc[:, j, 12:36].rearrange("p (b s) -> p b s", s=3), samp[:, :, TS:SEQ_S]))
            v.sem_inc(s_aout, 1)

        def ev_softplus_act(act):
            sp = EV["sp"]
            act.wait_ge(s_xr, 1)
            act.activation(sp[:, 1, :], sp[:, 0, :], ACT.Exp, scale=-1.0).then_inc(s_lru_act, 1)

        def ev_lru_act(act):
            sp, st = EV["sp"], EV["st"]
            for n in range(8):
                j = n // 2
                act.wait_ge(s_gate, n + 1)
                dst = EV["ig"] if n % 2 else EV["rg"]
                act.activation(dst[:, j, :], ps[:, GATE_BANKS[n % 4], 0:CW], ACT.Sigmoid,
                               bias=st[:, j, 37 + n % 2:38 + n % 2]).then_inc(s_gate_act, 1)
            act.wait_ge(s_gate_act, 8)
            act.wait_ge(s_xr, 2)
            for j in range(LRU_TILES):
                act.activation(decay[:, j], EV["rg"][:, j, :], ACT.Exp,
                               scale=sp[:, 7, j:j + 1]).then_inc(s_lru_act, 1)
            act.wait_ge(s_lru_act, 1 + LRU_TILES)
            for j in range(LRU_TILES):
                act.activation(EV["rg"][:, j, :], EV["rg"][:, j, :], ACT.Tanh,
                               scale=sp[:, 6, j:j + 1]).then_inc(s_lru_act, 1)

        def ev_root_act(act):
            for j in range(LRU_TILES):
                act.wait_ge(s_arg, j + 1)
                act.activation(EV["rg"][:, j, :], EV["rg"][:, j, :], ACT.Sqrt).then_inc(s_root, 1)

        def ev_state_pe(pe):
            pe.wait_ge(s_ev_par, 16 * 7)
            for j in range(4):
                ins = pe.transpose(ps[:, 6, 40 * j:40 * j + 40], EV["st_in"][0:40, j * P:(j + 1) * P], ident[0:40, 0:40])
            ins.then_inc(s_st, 1)

        GATE_BANKS = (0, 1, 6, 7)

        def ev_gate_pe(pe):
            pe.wait_ge(s_wg, 16 * 4)
            for n in range(8):
                j = n // 2
                pe.wait_ge(s_conv, j + 1)
                if n >= 4:
                    pe.wait_ge(s_gate_act, n - 3)
                pe.matmul(ps[:, GATE_BANKS[n % 4], 0:CW], EV["wg"][:, n, :], EV["xc"][:, j, :], start=True,
                          stop=True).then_inc(s_gate, 1)

        def ev_kvt_pe(pe):
            pe.wait_ge(s_ep_copied[0], 10)
            pe.wait_ge(s_gate_act, 8)
            for kind, bank in ((1, 6), (0, 7)):
                for t in range(3):
                    m = ROWS[t]
                    ins = pe.transpose(ps[0:m, bank, t * P:(t + 1) * P], EV["kv"][:, kind, t * P:t * P + m], ident)
                ins.then_inc(s_kvt, 1)

        def ev_kvt_act(act):
            for n, (dst, bank) in enumerate((("vtok", 6), ("ktok", 7))):
                act.wait_ge(s_kvt, n + 1)
                act.activation(EV[dst][:, 0:2, :], ps[:, bank, 0:2 * P].rearrange("p (t n) -> p t n", n=P), ACT.Copy)
                act.activation(EV[dst][0:NSA, 2, :], ps[0:NSA, bank, 2 * P:3 * P], ACT.Copy).then_inc(s_kvt_copied, 1)

        s_s = sem("s_s")
        s_sp = sem("s_sp")
        s_mx = sem("s_mx")
        s_nb = sem("s_nb")
        s_exp = sem("s_exp")
        s_pt = sem("s_pt")
        s_ptc = sem("s_ptc")
        s_pv = sem("s_pv")
        s_den = per_layer("s_den")
        s_sinkx = sem("s_sinkx")
        s_oc = sem("s_oc")
        s_ot = sem("s_ot")
        s_otc = sem("s_otc")

        class Prompt:
            def __init__(self, layer, groups, depth, s, pt, osb, sm, dist, score, value, out_col):
                self.depth = depth
                self.layer, self.groups, self.s, self.pt, self.osb = layer, groups, s, pt, osb
                self.sm, self.dist, self.score, self.value, self.out_col = sm, dist, score, value, out_col

            def width(self, qb):
                return self.groups * P * (qb + 1)

            def scores(self, n, width):
                first = n % self.depth * (4 // self.depth)
                return ps[:, first:first + 4 // self.depth, :].rearrange("p b n -> p (b n)")[:, 0:width]

        def banks(first, width):
            return ps[:, first:first + 2, :].rearrange("p b n -> p (b n)")[:, 0:width]

        def prompt_pe(pe, c, between={}):
            L = c.layer

            def scores(n):
                qb, h = divmod(n, NH)
                if n >= c.depth:
                    pe.wait_ge(s_sp, 16 * L + n - c.depth + 1)
                for g in range(c.groups):
                    nk = P * (qb + 1)
                    lhs, rhs = c.score(g, h, qb)
                    ins = pe.matmul(c.scores(n, c.width(qb))[:, g * nk:(g + 1) * nk], lhs, rhs, start=True, stop=True)
                ins.then_inc(s_s, 1)

            def weights_t(n):
                qb = n // NH
                pe.wait_ge(s_exp, 16 * L + n + 1)
                if n:
                    pe.wait_ge(s_ptc, 16 * L + n)
                for u in range(c.groups * (qb + 1)):
                    ins = pe.transpose(banks(4, 2 * BANK)[:, u * P:(u + 1) * P], c.s[:, n % c.depth, u * P:(u + 1) * P], ident)
                ins.then_inc(s_pt, 1)

            def values(n):
                qb, h = divmod(n, NH)
                pe.wait_ge(s_ptc, 16 * L + n + 1)
                if h == 0 and qb:
                    pe.wait_ge(s_oc, 2 * L + qb)
                units = c.groups * (qb + 1)
                col = c.out_col(h)
                for u in range(units):
                    g, kb = divmod(u, qb + 1)
                    ins = pe.matmul(ps[:, 6, col:col + HD], c.pt[:, n % 2, u * P:(u + 1) * P], c.value(g, h, kb),
                                    start=u == 0, stop=u == units - 1)
                ins.then_inc(s_pv, 1)

            def turn(qb):
                pe.wait_ge(s_oc, 2 * L + qb + 1)
                if qb:
                    pe.wait_ge(s_otc, 2 * L + qb)
                if L == 0:
                    pe.wait_ge(*((s_ptd_copied, 4), (s_so_copied, 1))[qb])
                for i in range(4):
                    ins = pe.transpose(ps[:, 7, i * P:(i + 1) * P], c.osb[:, i * P:(i + 1) * P], ident)
                ins.then_inc(s_ot, 1)

            for n in range(c.depth - 1):
                scores(n)
            for n in range(2 * NH):
                if n + c.depth - 1 < 2 * NH:
                    scores(n + c.depth - 1)
                weights_t(n)
                if n:
                    values(n - 1)
                if n == NH + 1:
                    turn(0)
                if n in between:
                    between[n]()
            values(2 * NH - 1)
            turn(1)

        def prompt_dve(v, c, between={}):
            L = c.layer
            mx, nb, den, rin, snb, sx = (c.sm[:, i, :] for i in range(6))
            ch = Chain(v, s_den[L])

            def finish(qb):
                cols = slice(NH * qb, NH * qb + NH)
                v.wait_ge(s_exp, 16 * L + NH * (qb + 1))
                if L == 0:
                    ch(v.tensor_tensor(snb[:, cols], nb[:, cols], EV["sink"][:, 0:NH], ALU.add))
                    v.wait_ge(s_sinkx, qb + 1)
                    ch(v.tensor_tensor(den[:, cols], den[:, cols], sx[:, cols], ALU.add))
                ch(v.reciprocal(rin[:, cols], den[:, cols]))
                v.wait_ge(s_pv, 16 * L + NH * (qb + 1))
                if qb:
                    v.wait_ge(s_ot, 2 * L + qb)
                scale = rin[:, cols]
                if L == 0:
                    scale = scale.rearrange("p (s i) -> p i s", s=2)
                    dst = c.osb.rearrange("p (i s d) -> p i s d", i=4, s=2)
                    src = ps[:, 6, :].rearrange("p (i s d) -> p i s d", i=4, s=2)
                    scale = scale.unsqueeze(3).broadcast_to([P, 4, 2, HD])
                else:
                    dst = c.osb.rearrange("p (h d) -> p h d", h=NH)
                    src = ps[:, 6, :].rearrange("p (h d) -> p h d", h=NH)
                    scale = scale.unsqueeze(2).broadcast_to([P, NH, HD])
                v.tensor_tensor(dst, src, scale, ALU.mult).then_inc(s_oc, 1)

            for n in range(2 * NH):
                qb, h = divmod(n, NH)
                w = c.width(qb)
                v.wait_ge(s_s, 16 * L + n + 1)
                if n >= c.depth:
                    v.wait_ge(s_pt, 16 * L + n - c.depth + 1)
                v.scalar_tensor_tensor(out=c.s[:, n % c.depth, 0:w], in0=c.dist[qb], scalar=slope8(h),
                                       in1=c.scores(n, w), op0=ALU.mult, op1=ALU.add).then_inc(s_sp, 1)
                v.wait_ge(s_sp, 16 * L + n + 1)
                v.tensor_reduce(mx[:, n:n + 1], c.s[:, n % c.depth, 0:w], AX.X, ALU.max).then_inc(s_mx, 1)
                v.wait_ge(s_mx, 16 * L + n + 1)
                if L == 0:
                    ins = v.tensor_scalar(nb[:, n:n + 1], mx[:, n:n + 1], -SCALE, EV["sink"][:, NH + h:NH + h + 1],
                                          ALU.mult, ALU.min)
                else:
                    ins = v.tensor_scalar(nb[:, n:n + 1], mx[:, n:n + 1], -SCALE, None, ALU.mult)
                ins.then_inc(s_nb, 1)
                if n == NH + c.depth // 2:
                    finish(0)
                if n in between:
                    between[n]()
            finish(1)

        def prompt_act(act, c, between={}):
            L = c.layer
            mx, nb, den, rin, snb, sx = (c.sm[:, i, :] for i in range(6))

            def exps(n):
                w = c.width(n // NH)
                act.wait_ge(s_nb, 16 * L + n + 1)
                act.activation(c.s[:, n % c.depth, 0:w], c.s[:, n % c.depth, 0:w], ACT.Exp, bias=nb[:, n:n + 1], scale=SCALE,
                               accum_out=den[:, n:n + 1]).then_inc(s_exp, 1)

            def copy(n):
                w = c.width(n // NH)
                act.wait_ge(s_pt, 16 * L + n + 1)
                if n >= 2:
                    act.wait_ge(s_pv, 16 * L + n - 1)
                act.activation(c.pt[:, n % 2, 0:w], banks(4, w), ACT.Copy).then_inc(s_ptc, 1)

            def sinks(qb):
                if L == 0:
                    cols = slice(NH * qb, NH * qb + NH)
                    act.wait_ge(s_den[L], 1 + 3 * qb)
                    act.activation(sx[:, cols], snb[:, cols], ACT.Exp).then_inc(s_sinkx, 1)

            def turned(qb):
                act.wait_ge(s_ot, 2 * L + qb + 1)
                tile0 = 4 if L == 0 else 0
                act.activation(mixT[:, tile0:tile0 + 4, qb * P:(qb + 1) * P],
                               ps[:, 7, :].rearrange("p (i t) -> p i t", i=4), ACT.Copy).then_inc(s_otc, 1)

            ahead = c.depth // 2
            for n in range(ahead):
                exps(n)
            for n in range(2 * NH):
                if n == NH + 1:
                    sinks(0)
                if c.depth == 4:
                    copy(n)
                if n + ahead < 2 * NH:
                    exps(n + ahead)
                if c.depth == 2:
                    copy(n)
                if n == NH + 1:
                    turned(0)
                if n in between:
                    between[n]()
            sinks(1)
            turned(1)

        s_cache = sem("s_cache")

        def ev_dec_qz(v):
            qz = EV["qz"].rearrange("p b (h t) -> p h b t", h=NH)
            ch = lru["chain"]
            ch(v.memset(EV["qz"], 0.0))
            v.wait_ge(s_ep_copied[0], 10)
            src = EV["q"][:, :, NPR:NT].rearrange("p i (b t) -> p i b t", t=TS)
            for s in range(2):
                rows = slice(HD * s, HD * s + HD)
                for i in range(4):
                    ch(v.tensor_copy(qz[rows, 4 * s + i], src[rows, i]))
            v.sem_inc(s_qz, 1)

        cache = gb[:, :, :].rearrange("p a n -> p (a n)").rearrange("p (b n) -> p b n", b=NB)
        dec_sm = EV["sm"][:, 6, :]

        def dec_col(g, k):
            return dec_sm[:, 8 * g + k:8 * g + k + 1]

        def ev_dec_pe(pe):
            def keys(g):
                if g:
                    pe.wait_ge(s_kd_copied, g)
                else:
                    pe.wait_ge(s_cache, 16)
                for bb in range(4):
                    ins = pe.transpose(ps[:, 7, bb * P:(bb + 1) * P], cache[:, 4 * g + bb, 0:P], ident)
                ins.then_inc(s_kd, 1)

            def scores():
                pe.wait_ge(s_qz, 1)
                pe.wait_ge(s_kd_copied, 2)
                for g in range(2):
                    for bb in range(4):
                        b = 4 * g + bb
                        rows, at = slice(32 * bb, 32 * bb + 32), g * (P + NSA)
                        pe.matmul(ps[rows, 7, at:at + P], EV["qz"][:, b, :], EV["ktd"][:, b, :], start=True, stop=True)
                        ins = pe.matmul(ps[rows, 7, at + P:at + P + NSA], EV["qz"][:, b, :], EV["kv"][:, 0, NPR:NT],
                                        start=True, stop=True)
                ins.then_inc(s_sd, 1)

            def turn():
                pe.wait_ge(s_sd_dve, 14)
                for g in range(2):
                    pe.transpose(ps[:, 7, 2 * g * P:(2 * g + 1) * P], EV["sd"][:, g, 0:P], ident)
                    ins = pe.transpose(ps[0:NSA, 7, (2 * g + 1) * P:(2 * g + 2) * P], EV["sd"][:, g, P:P + NSA], ident)
                ins.then_inc(s_ptd, 1)

            def values():
                pe.wait_ge(s_otc, 1)
                pe.wait_ge(s_kvt_copied, 1)
                pe.wait_ge(s_ptd_copied, 4)
                for b in range(NB):
                    out, bb = ps[:, 7, b * 32:b * 32 + 32], b % 4
                    rhs = EV["ptd"][:, b // 4, :].rearrange("p (k r) -> p k r", k=2)
                    pe.matmul(out, cache[:, b, P:2 * P], rhs[:, 0, 32 * bb:32 * bb + 32], start=True, stop=False)
                    ins = pe.matmul(out, EV["vtok"][0:NSA, 2, :], rhs[0:NSA, 1, 32 * bb:32 * bb + 32], start=False,
                                    stop=True)
                ins.then_inc(s_od, 1)

            def states():
                pe.wait_ge(s_aout, 1)
                pe.wait_ge(s_mix[0], 8)
                for j in range(4):
                    ins = pe.transpose(ps[0:36, 7, j * P:(j + 1) * P], EV["stc"][:, j, :], ident)
                ins.then_inc(s_so, 1)
            return {1: lambda: keys(0), 2: lambda: keys(1), 4: scores, 8: turn, 11: values, 14: states}

        def ev_dec_dve(v):
            dm, row_sink = EV["sd"], EV["sink"][:, 24:25]
            steps = 0

            def step(ins):
                nonlocal steps
                steps += 1
                ins.then_inc(s_sd_dve, 1)
                v.wait_ge(s_sd_dve, steps)

            def keys(g):
                v.wait_ge(s_kd, g + 1)
                v.tensor_copy(EV["ktd"][:, 4 * g:4 * g + 4, :],
                              ps[:, 7, :].rearrange("p (b n) -> p b n", b=4)).then_inc(s_kd_copied, 1)

            def maxima():
                v.wait_ge(s_sd, 1)
                for g in range(2):
                    at = g * (P + NSA)
                    step(v.scalar_tensor_tensor(out=dm[:, g, :], in0=EV["dd"][:, g, :], scalar=row_slope,
                                                in1=ps[:, 7, at:at + P + NSA], op0=ALU.mult, op1=ALU.add))
                    step(v.tensor_reduce(dec_col(g, 0), dm[:, g, :], AX.X, ALU.max))
                    step(v.tensor_scalar(dec_col(g, 1), dec_col(g, 0), SCALE, row_sink, ALU.mult, ALU.max))
                    step(v.tensor_scalar(dec_col(g, 2), dec_col(g, 1), -1.0, None, ALU.mult))

            def normalise():
                v.wait_ge(s_sd_exp, 4)
                for g in range(2):
                    step(v.tensor_scalar(dec_col(g, 5), dec_col(g, 3), dec_col(g, 4), None, ALU.add))
                    step(v.reciprocal(dec_col(g, 6), dec_col(g, 5)))
                    step(v.tensor_scalar(dm[:, g, :], dm[:, g, :], dec_col(g, 6), None, ALU.mult))

            def outputs():
                v.wait_ge(s_od, 1)
                src = ps[:, 7, 0:256].rearrange("p (b h t) -> p b h t", h=NH, t=TS)
                for s in range(2):
                    rows = slice(HD * s, HD * s + HD)
                    for i in range(4):
                        dst = mixT[rows, 4 + i, NPR:NT].rearrange("p (b t) -> p b t", t=TS)
                        v.tensor_copy(dst, src[rows, :, 4 * s + i, :]).then_inc(s_mix[0], 1)
            return {2: lambda: keys(0), 3: lambda: keys(1), 5: maxima, 7: normalise, 13: outputs}

        def ev_dec_act(act):
            def exps():
                act.wait_ge(s_sd_dve, 8)
                for g in range(2):
                    act.activation(EV["sd"][:, g, :], EV["sd"][:, g, :], ACT.Exp, bias=dec_col(g, 2), scale=SCALE,
                                   accum_out=dec_col(g, 3)).then_inc(s_sd_exp, 1)
                    act.activation(dec_col(g, 4), EV["sink"][:, 24:25], ACT.Exp, bias=dec_col(g, 2)).then_inc(s_sd_exp, 1)

            def turned():
                act.wait_ge(s_ptd, 1)
                for g in range(2):
                    act.activation(EV["ptd"][:, g, 0:P], ps[:, 7, 2 * g * P:(2 * g + 1) * P],
                                   ACT.Copy).then_inc(s_ptd_copied, 1)
                    act.activation(EV["ptd"][0:NSA, g, P:2 * P], ps[0:NSA, 7, (2 * g + 1) * P:(2 * g + 2) * P],
                                   ACT.Copy).then_inc(s_ptd_copied, 1)

            def states():
                act.wait_ge(s_so, 1)
                act.activation(EV["st_out"][0:36, :], ps[0:36, 7, :], ACT.Copy).then_inc(s_so_copied, 1)
            return {5: exps, 8: turned, 14: states}

        s_mid = sem("s_mid")

        def out_proj_pe(pe):
            for hf, m in enumerate((3, 4)):
                w = wait_slot(pe, 0, m)
                for t in range(3):
                    rows = ROWS[t]
                    for j in range(8):
                        ins = pe.matmul(ps[0:rows, 2 * t + hf, :], mixT[:, j, t * P:t * P + rows],
                                        w[:, j * BANK:(j + 1) * BANK], start=j == 0, stop=j == 7)
                    if hf:
                        ins.then_inc(s_f, 1)
                    elif t == 2:
                        ins.then_inc(s_mid, 1)
                if hf:
                    pe.wait_ge(s_f, 3)
                else:
                    pe.wait_ge(s_mid, 1)
                pe.sem_inc(s_free[0][slot_of(m)], 1)

        s_wr = sem("s_wr")
        s_lg = sem("s_lg")
        s_sc = sem("s_sc")
        s_rt = per_layer("s_rt")
        s_sel = sem("s_sel")
        s_ps = sem("s_ps")
        s_disp = sem("s_disp")
        s_sgu = sem("s_sgu")
        s_sact = sem("s_sact")
        s_sh = sem("s_sh")
        s_sy = sem("s_sy")
        s_acc0 = sem("s_acc0")
        s_xb = sem("s_xb")
        s_pm = per_layer("s_pm")
        s_ga = per_layer("s_ga")
        s_pgt = per_layer("s_pgt")
        s_pgtc = per_layer("s_pgtc")
        s_xg = per_layer("s_xg")
        s_gu = per_layer("s_gu")
        s_si = per_layer("s_si")
        s_h2 = per_layer("s_h2")
        s_ht = per_layer("s_ht")
        s_htc = per_layer("s_htc")
        s_dn = per_layer("s_dn")
        s_yb = per_layer("s_yb")
        s_yc = per_layer("s_yc")
        s_scat = per_layer("s_scat")
        s_add = per_layer("s_add")

        def iterations(eng):
            return eng.value_load(n_iter[0:1, 0:1], min_val=NE // 4 - 1, max_val=PASSES * NE // 4 - 1)

        def moe_route_pe(pe, L):
            pe.wait_ge(s_tp_copied[0], 3 * (2 * L + 2))
            pe.wait_ge(s_tp_copied[1], 3 * (2 * L + 2))
            pe.wait_ge(s_wr, 32 * (L + 1))
            for t in range(3):
                for c in range(NC):
                    ins = pe.matmul(ps[:, 2, t * NE:(t + 1) * NE], xT[:, c, t * P:(t + 1) * P], MO["wr"][:, c, :],
                                    start=c == 0, stop=c == NC - 1)
            ins.then_inc(s_lg, 1)

        def moe_pos_pe(pe, L):
            pe.wait_ge(s_sel, L + 1)
            sel = MO["sel"]
            for t in range(3):
                for u in range(t + 1):
                    ins = pe.matmul(ps[:, 2, t * NE:(t + 1) * NE], tri if u == t else ones, sel[:, u, :],
                                    start=u == 0, stop=u == t)
            for u in range(3):
                ins = pe.matmul(ps[:, 2, 3 * NE:4 * NE], ones, sel[:, u, :], start=u == 0, stop=u == 2)
            ins.then_inc(s_ps, 1)

        def moe_shared_pe(pe, L):
            w = wait_slot(pe, L, SHARED[L])
            wg, wu = (w[:, i * 2048:(i + 1) * 2048].rearrange("p (c n) -> p c n", c=NC) for i in range(2))
            for j in range(2):
                for c in range(NC):
                    pe.matmul(ps[:, 4 + j, 0:NT], wg[:, c, j * P:(j + 1) * P], xT[:, c, 0:NT], start=c == 0,
                              stop=c == NC - 1)
                for c in range(NC):
                    ins = pe.matmul(ps[:, 6 + j, 0:NT], wu[:, c, j * P:(j + 1) * P], xT[:, c, 0:NT], start=c == 0,
                                    stop=c == NC - 1)
                ins.then_inc(s_sgu, 1)

        def moe_shared_down_pe(pe, L):
            w = wait_slot(pe, L, SHARED[L])
            wd = w[:, 4096:6144].rearrange("p (j n) -> p j n", j=2)
            pe.wait_ge(s_sh, 2 * L + 2)
            for c in range(NC):
                if c >= 2:
                    pe.wait_ge(s_acc0, 8 * L + c - 1)
                for j in range(2):
                    lhs = wd[:, j, :].rearrange("p (f c) -> p c f", c=NC)[:, c, :]
                    ins = pe.matmul(ps[:, c % 2, 0:NT], lhs, MO["sh"][:, j, :], start=j == 0, stop=j == 1)
                ins.then_inc(s_sy, 1)
            pe.wait_ge(s_sy, 8 * L + NC)
            pe.sem_inc(s_free[L][slot_of(SHARED[L])], 1)

        route_chain = {}

        def moe_route_dve(v, L):
            ch = route_chain[L] = Chain(v, s_rt[L])
            M = MO
            sc, bi, sel, gate = M["scores"], M["biased"], M["sel"], M["gate"]
            v.wait_ge(s_sc, L + 1)
            v.wait_ge(s_wr, 32 * (L + 1))
            ch(v.tensor_tensor(bi, sc, M["rb"].unsqueeze(1).broadcast_to([P, 3, NE]), ALU.add))
            for n in range(24):
                t, g = divmod(n, 8)
                ins = v.max(M["top"][:, n, :], bi[:, t, g * 8:g * 8 + 8])
            ch(ins)
            ch(v.tensor_tensor(M["gs"], M["top"][:, :, 0].rearrange("p (t g) -> p t g", t=3),
                               M["top"][:, :, 1].rearrange("p (t g) -> p t g", t=3), ALU.add))
            gt = M["gt"].rearrange("p t (g f) -> p t g f", g=8)
            eq = M["eq"].rearrange("p t (g f) -> p t g f", g=8)
            tie = before.rearrange("p (g f) -> p g f", g=8)
            for t in range(3):
                mine = M["gs"][:, t, :].unsqueeze(2).broadcast_to([P, 8, 8])
                other = M["gs"][:, t, :].unsqueeze(1).broadcast_to([P, 8, 8])
                ch(v.tensor_tensor(gt[:, t], other, mine, ALU.is_gt))
                ch(v.tensor_tensor(eq[:, t], other, mine, ALU.is_equal))
                ch(v.tensor_tensor(eq[:, t], eq[:, t], tie, ALU.mult))
            ch(v.tensor_tensor(gt, gt, eq, ALU.add))
            ch(v.tensor_reduce(M["rank"], gt, AX.X, ALU.add))
            keep = M["rank"]
            ch(v.tensor_scalar(keep, keep, 3.5, None, ALU.is_lt))
            kb = keep.unsqueeze(3).broadcast_to([P, 3, 8, 8])
            b4 = bi.rearrange("p t (g f) -> p t g f", g=8)
            ch(v.tensor_tensor(b4, b4, kb, ALU.mult))
            ch(v.tensor_scalar(M["gs"], keep, BIG, -BIG, ALU.mult, ALU.add))
            ch(v.tensor_tensor(b4, b4, M["gs"].unsqueeze(3).broadcast_to([P, 3, 8, 8]), ALU.add))
            for t in range(3):
                ch(v.max(M["t8"][:, t, :], bi[:, t, :]))
                ch(v.match_replace(M["rep"][:, t, :], M["t8"][:, t, :], bi[:, t, :], -3e38))
            ch(v.tensor_tensor(sel, M["rep"], bi, ALU.not_equal))
            ch(v.tensor_tensor(sel, sel, valid.unsqueeze(2).broadcast_to([P, 3, NE]), ALU.mult))
            v.sem_inc(s_sel, 1)
            ch(v.tensor_tensor(gate, sc, sel, ALU.mult))
            sm = M["cnt"]
            ch(v.tensor_reduce(sm[:, 0:3], gate, AX.X, ALU.add))
            ch(v.tensor_tensor(sm[:, 0:3], sm[:, 0:3], invalid, ALU.add))
            ch(v.reciprocal(sm[:, 3:6], sm[:, 0:3]))
            ch(v.tensor_scalar(sm[:, 3:6], sm[:, 3:6], 2.5, None, ALU.mult))
            ch(v.tensor_tensor(gate, gate, sm[:, 3:6].unsqueeze(2).broadcast_to([P, 3, NE]), ALU.mult))

        def moe_pos_dve(v, L):
            M, ch = MO, route_chain[L]
            sm, sel, pos = M["cnt"], M["sel"], M["pos"]
            v.wait_ge(s_ps, L + 1)
            ch(v.scalar_tensor_tensor(out=pos, in0=ps[:, 2, 0:3 * NE].rearrange("p (t e) -> p t e", t=3), scalar=1.0,
                                      in1=sel, op0=ALU.add, op1=ALU.mult))
            ch(v.tensor_scalar(pos, pos, -1.0, None, ALU.add))
            for part in range(1, 3):
                v.tensor_copy(pos[NSA * part:NSA * (part + 1), 2, :], pos[0:NSA, 2, :]).then_inc(s_rt[L], 1)
                ch.n += 1
            v.wait_ge(s_rt[L], ch.n)
            ch(v.tensor_reduce(sm[:, 6:7], ps[:, 2, 3 * NE:4 * NE], AX.X, ALU.max))
            ch(v.tensor_scalar(sm[:, 8:8 + PASSES], thresholds, sm[:, 6:7], None, ALU.is_lt))
            ch(v.tensor_reduce(sm[:, 7:8], sm[:, 8:8 + PASSES], AX.X, ALU.add))
            ch(v.tensor_scalar(sm[:, 7:8], sm[:, 7:8], float(NE // 4), float(NE // 4 - 1), ALU.mult, ALU.add))
            ch(v.tensor_copy(n_iter[:, :], sm[:, 7:8]))
            v.sem_inc(s_disp, 1)

        def moe_shared_dve(v, L):
            for j in range(2):
                v.wait_ge(s_sact, 2 * L + j + 1)
                v.tensor_tensor(MO["sh"][:, j, :], MO["shg"][:, j, :], ps[:, 6 + j, 0:NT], ALU.mult).then_inc(s_sh, 1)

        def moe_shared_acc_act(act, L):
            for c in range(NC):
                act.wait_ge(s_sy, 8 * L + c + 1)
                act.activation(MO["acc"][:, c, :], ps[:, c % 2, 0:NT], ACT.Copy).then_inc(s_acc0, 1)

        def part_at(t, part):
            return 3 * t + part if t < 2 else 6 + part

        def moe_act_head(act, L):
            act.wait_ge(s_sout, (OUT0, OUT1)[L])
            for t in range(3):
                rows = slice(0, ROWS[t])
                act.activation(xb[rows, part_at(t, 0)], x_tok[rows, t, :], ACT.Copy).then_inc(s_xb, 1)
            act.wait_ge(s_lg, L + 1)
            act.activation(MO["scores"], ps[:, 2, 0:3 * NE].rearrange("p (t e) -> p t e", t=3),
                           ACT.Sigmoid).then_inc(s_sc, 1)
            for t in range(3):
                rows = slice(0, ROWS[t])
                act.wait_ge(s_pm[L], t + 1)
                act.activation(xb[rows, part_at(t, 1)], x_rest[t][rows], ACT.Copy).then_inc(s_xb, 1)
            act.activation(xb[NSA:2 * NSA, 6], x_rest[2][0:NSA], ACT.Copy).then_inc(s_xb, 1)
            for j in range(2):
                act.wait_ge(s_sgu, 2 * L + j + 1)
                act.activation(MO["shg"][:, j, :], ps[:, 4 + j, 0:NT], ACT.Silu).then_inc(s_sact, 1)
            for t in range(3):
                act.wait_ge(s_pm[L], 3 + t + 1)
                out, rows = (xb[:, 3 * t + 2], P) if t < 2 else (xb[2 * NSA:3 * NSA, 6], NSA)
                act.activation(out, x_rest[t][0:rows], ACT.Copy).then_inc(s_xb, 1)

        def moe_pairs_pool(pool, L):
            for part in range(2):
                for t in range(3):
                    rows = slice(0, ROWS[t])
                    pool.wait_ge(s_xb, 10 * L + (t + 1, (4, 5, 7)[t])[part])
                    pool.tensor_tensor(x_rest[t][rows], (x_rest[t] if part else x_tok[:, t, :])[rows],
                                       xb[rows, part_at(t, part)], ALU.subtract).then_inc(s_pm[L], 1)
            pool.wait_ge(s_pm[L], 6)
            pool.wait_ge(s_disp, L + 1)
            pool.sem_inc(s_pgt[L], 2)
            cur = MO["cur"]
            column = lambda q, k: cur[:, q, CAP + 6 * k:CAP + 6 * k + 6].rearrange("p (t u) -> p t u", u=2)
            with pool.Fori(0, iterations(pool) + 1) as i:
                for q in range(2):
                    n = 2 * i + q
                    pool.wait_ge(s_pgt[L], n + 1)
                    pool.sem_inc(s_pm[L], 1)
                    e = (i % 16) * 4 + 2 * q
                    slots, pos, gate = cur[:, q, 0:CAP], column(q, 0), column(q, 1)
                    pool.tensor_copy(slots, misc[:, bass.ds(iota0 + (i // 16) * CAP, CAP)]).then_inc(s_pm[L], 1)
                    pool.tensor_copy(pos, MO["pos"][:, :, bass.ds(e, 2)]).then_inc(s_pm[L], 1)
                    pool.tensor_copy(gate, MO["gate"][:, :, bass.ds(e, 2)]).then_inc(s_pm[L], 1)
                    pool.wait_ge(s_pm[L], 7 * n + 10)
                    pool.sem_inc(s_pm[L], 1)
                    for name in ("pm", "pg"):
                        for t in range(3):
                            for u in range(2):
                                out = (pm if name == "pm" else MO["pg"])[:, q, t, u * CAP:(u + 1) * CAP]
                                if name == "pm":
                                    ins = pool.tensor_scalar(out, slots, pos[:, t, u:u + 1], None, ALU.is_equal)
                                else:
                                    ins = pool.tensor_scalar(out, slots, pos[:, t, u:u + 1], gate[:, t, u:u + 1],
                                                             ALU.is_equal, ALU.mult)
                        ins.then_inc(s_pm[L], 1)
                    pool.wait_ge(s_pm[L], 7 * n + 13)

        def gather_pe(pe, L, n, q, hf):
            pe.wait_ge(s_pm[L], 7 * n + 13)
            for c in range(4 * hf, 4 * hf + 4):
                for k in range(7):
                    m = 3 * NSA if k == 6 else P
                    lhs = xb[0:m, k].rearrange("t (f c) -> t c f", c=NC)[:, c, :]
                    ins = pe.matmul(ps[:, hf, (c % 4) * P:(c % 4 + 1) * P], lhs, pm[0:m, q, k // 3, :],
                                    start=k == 0, stop=k == 6)
            ins.then_inc(s_ga[L], 1)

        def turn_pe(pe, L, n, q):
            for t in range(3):
                m = ROWS[t]
                pe.transpose(ps[:, 3, :].bitcast(BF16)[:, t * P:t * P + m], pm[0:m, q, t, :], ident_b[0:m, 0:m])
            for t in range(3):
                m = ROWS[t]
                ins = pe.matmul(ps[:, 3, NT:NT + 1], MO["pg"][0:m, q, t, :], ones[0:m, 0:1], start=t == 0, stop=t == 2)
            ins.then_inc(s_pgt[L], 1)

        def up_pe(pe, L, n, q, it, scatter=None):
            pe.wait_ge(s_xg[L], 2 * n + 2)
            for u in range(2):
                s = slot_of(EXP0[L] + 2 * q + u)
                pe.wait_ge(s_ring[L][s], static_dma[L][s] + (it + 1) * 32)
            for c in range(NC):
                for u in range(2):
                    w = ring[:, slot_of(EXP0[L] + 2 * q + u), 0:4096].rearrange("p (g c n) -> p c g n", g=2, c=NC)
                    ins = pe.matmul(ps[64 * u:64 * u + CAP, 2, :], MO["xg"][:, c, u * CAP:(u + 1) * CAP], w[:, c],
                                    start=c == 0, stop=c == NC - 1)
                if c == NC - 1:
                    ins.then_inc(s_gu[L], 1)
                for chunk in {4: (0, 1), 5: (2, 3), 6: (4, 5), 7: (6, 7)}.get(c, ()) if scatter else ():
                    scatter(chunk)

        def hidden_pe(pe, L, n):
            pe.wait_ge(s_h2[L], n + 1)
            for j in range(2):
                ins = pe.transpose(ps[:, 2, j * P:(j + 1) * P], MO["h"][:, j * P:(j + 1) * P], ident)
            ins.then_inc(s_ht[L], 1)

        def down_pe(pe, L, n, q, it):
            pe.wait_ge(s_htc[L], n + 1)
            pe.wait_ge(s_ring_dn[L][q], (it + 1) * 32)
            for hf in range(2):
                for j in range(2):
                    for u in range(2):
                        w = ring[:, slot_of(EXP0[L] + 2 * q + u), 4096:6144].rearrange("p (j n) -> p j n", j=2)
                        ins = pe.matmul(ps[64 * u:64 * u + CAP, 4 + hf, :], MO["hT"][:, j, 64 * u:64 * u + CAP],
                                        w[:, j, hf * BANK:(hf + 1) * BANK], start=j == 0, stop=j == 1)
            ins.then_inc(s_dn[L], 1)

        def scatter_pe(pe, L, n, q, c):
            if c == 0:
                pe.wait_ge(s_yc[L], 4 * n + 4)
                pe.wait_ge(s_pgtc[L], n + 1)
            pe.wait_ge(s_add[L], NC * n + c + NC - 1)
            for k in range(3):
                lhs = yb[:, k].rearrange("p (f c) -> p c f", c=NC)[:, c, :]
                ins = pe.matmul(ps[:, 6 + c % 2, 0:NT], lhs, pgt[:, q, :], start=k == 0, stop=k == 2)
            ins.then_inc(s_scat[L], 1)

        def over_pairs(eng, L, first, step, last):
            more = iterations(eng)
            first(0, 0, 0)
            with eng.Fori(0, more) as i:
                step(2 * i + 1, 1, i)
                step(2 * i + 2, 0, i + 1)
            step(2 * more + 1, 1, more)
            last(2 * more + 1, 1, more)
            return more

        def moe_pairs_pe(pe, L):
            pe.wait_ge(s_acc0, 8 * L + NC)
            pe.wait_ge(s_disp, L + 1)
            pe.wait_ge(s_xb, 10 * (L + 1))

            def first(n, q, it):
                gather_pe(pe, L, n, q, 0)
                gather_pe(pe, L, n, q, 1)
                turn_pe(pe, L, n, q)
                up_pe(pe, L, n, q, it)

            def step(n, q, it):
                gather_pe(pe, L, n, q, 0)
                hidden_pe(pe, L, n - 1)
                gather_pe(pe, L, n, q, 1)
                turn_pe(pe, L, n, q)
                down_pe(pe, L, n - 1, 1 - q, it if q else it - 1)
                up_pe(pe, L, n, q, it, lambda c: scatter_pe(pe, L, n - 1, 1 - q, c))

            def last(n, q, it):
                hidden_pe(pe, L, n)
                down_pe(pe, L, n, q, it)
                for c in range(NC):
                    scatter_pe(pe, L, n, q, c)

            more = over_pairs(pe, L, first, step, last)
            pe.wait_ge(s_add[L], more * (2 * NC) + 3 * NC)
            for t in range(3):
                m = ROWS[t]
                for c in range(NC):
                    ins = pe.transpose(ps[0:m, 2 * t + c // 4, (c % 4) * P:(c % 4 + 1) * P],
                                       MO["acc"][:, c, t * P:t * P + m], ident)
                ins.then_inc(s_f, 1)

        def moe_pairs_act(act, L):
            act.wait_ge(s_disp, L + 1)

            def tokens(n):
                act.wait_ge(s_ga[L], 2 * n + 1)
                act.activation(MO["xg"][:, 0:4, :], ps[:, 0, :].rearrange("p (c s) -> p c s", c=4),
                               ACT.Copy).then_inc(s_xg[L], 1)

            def tokens2(n):
                act.wait_ge(s_ga[L], 2 * n + 2)
                act.activation(MO["xg"][:, 4:8, :], ps[:, 1, :].rearrange("p (c s) -> p c s", c=4),
                               ACT.Copy).then_inc(s_xg[L], 1)

            def hidden(n):
                act.wait_ge(s_ht[L], n + 1)
                act.activation(MO["hT"], ps[:, 2, 0:2 * P].rearrange("p (j s) -> p j s", j=2),
                               ACT.Copy).then_inc(s_htc[L], 1)

            def turned(n, q):
                act.wait_ge(s_pgt[L], n + 3)
                act.activation(MO["own_gate"][:, q:q + 1], ps[:, 3, NT:NT + 1], ACT.Copy)
                act.activation(pgt[:, q, :], ps[:, 3, :].bitcast(BF16)[:, 0:NT], ACT.Copy).then_inc(s_pgtc[L], 1)

            def parts(n):
                act.wait_ge(s_dn[L], n + 1)
                for hf in range(2):
                    act.activation(yb[:, 0, hf * BANK:(hf + 1) * BANK], ps[:, 4 + hf, :], ACT.Copy).then_inc(s_yb[L], 1)
                for hf in range(2):
                    act.wait_ge(s_yc[L], 4 * n + hf + 1)
                    half = slice(hf * BANK, (hf + 1) * BANK)
                    act.activation(yb[:, 1, half], MO["y_rest"][:, half], ACT.Copy).then_inc(s_yb[L], 1)

            def silu(n):
                act.wait_ge(s_gu[L], n + 1)
                act.activation(MO["sg"], ps[:, 2, 0:DE], ACT.Silu).then_inc(s_si[L], 1)

            def first(n, q, it):
                tokens(n)
                tokens2(n)
                turned(n, q)
                silu(n)

            def step(n, q, it):
                tokens(n)
                hidden(n - 1)
                tokens2(n)
                turned(n, q)
                parts(n - 1)
                silu(n)

            def last(n, q, it):
                hidden(n)
                parts(n)

            over_pairs(act, L, first, step, last)

        def moe_pairs_dve(v, L):
            v.wait_ge(s_disp, L + 1)
            v.wait_ge(s_acc0, 8 * L + NC)
            v.sem_inc(s_add[L], NC)

            def outputs(n):
                for hf in range(2):
                    half = slice(hf * BANK, (hf + 1) * BANK)
                    v.wait_ge(s_yb[L], 4 * n + hf + 1)
                    v.tensor_tensor(MO["y_rest"][:, half], ps[:, 4 + hf, :], yb[:, 0, half],
                                    ALU.subtract).then_inc(s_yc[L], 1)
                for hf in range(2):
                    half = slice(hf * BANK, (hf + 1) * BANK)
                    v.wait_ge(s_yb[L], 4 * n + hf + 3)
                    v.tensor_tensor(yb[:, 2, half], MO["y_rest"][:, half], yb[:, 1, half],
                                    ALU.subtract).then_inc(s_yc[L], 1)

            def hidden(n, q):
                v.wait_ge(s_si[L], n + 1)
                v.scalar_tensor_tensor(out=MO["h"], in0=MO["sg"], scalar=MO["own_gate"][:, q:q + 1],
                                       in1=ps[:, 2, DE:2 * DE], op0=ALU.mult, op1=ALU.mult).then_inc(s_h2[L], 1)

            def add(n, chunks=range(NC)):
                for c in chunks:
                    v.wait_ge(s_scat[L], NC * n + c + 1)
                    v.wait_ge(s_add[L], NC * n + c + 1)
                    v.tensor_tensor(MO["acc"][:, c, :], MO["acc"][:, c, :], ps[:, 6 + c % 2, 0:NT],
                                    ALU.add).then_inc(s_add[L], 1)

            def first(n, q, it):
                hidden(n, q)

            def step(n, q, it):
                outputs(n - 1)
                add(n - 1, range(NC - 2))
                hidden(n, q)
                add(n - 1, range(NC - 2, NC))

            def last(n, q, it):
                outputs(n)
                add(n)

            more = over_pairs(v, L, first, step, last)
            v.wait_ge(s_add[L], more * (2 * NC) + 3 * NC)

        s_op = sem("s_op")
        s_op_copied = [sem("s_op_copied_act"), sem("s_op_copied_dve")]
        s_tk = sem("s_tk")
        s_tk_copied = [sem("s_tk_copied_act"), sem("s_tk_copied_dve")]
        s_kst = [sem("s_kst_0"), sem("s_kst_1")]
        s_dp = sem("s_dp")
        s_w1 = sem("s_w1")
        s_qz1 = sem("s_qz1")
        s_g1 = [sem(f"s_g1_{b}") for b in range(4)]
        s_dd1 = sem("s_dd1")
        s_kt = sem("s_kt")
        s_kt_copied = [sem("s_kt_copied_act"), sem("s_kt_copied_dve")]
        s_sd1 = sem("s_sd1")
        s_sm1 = sem("s_sm1")
        s_ex1 = sem("s_ex1")
        s_p1 = sem("s_p1")
        s_p1c = sem("s_p1c")
        s_o1 = sem("s_o1")
        s_ot1 = sem("s_ot1")
        s_k1 = [sem(f"s_k1_{ck}") for ck in range(4)]
        s_v1 = sem("s_v1")

        W = OD["work"]
        kst = W[:, 0:3072].rearrange("p (b t n) -> p b t n", b=2, t=3)
        vst = W[:, 3072:3072 + 2304].rearrange("p (b i n) -> p b i n", b=2, i=4)
        OP = {"s": W[:, 0:1536].rearrange("p (b n) -> p b n", b=2), "pt": W[:, 1536:3072].rearrange("p (b n) -> p b n", b=2),
              "osb": W[:, 3072:3584], "dist": W[:, 3584:4736], "sm": W[:, 4736:4864].rearrange("p (k n) -> p k n", k=8)}
        qz1 = W[:, 0:3072].rearrange("p (g i r) -> p g i r", g=3, i=4)
        kns = W[:, 3072:3456].rearrange("p (g i n) -> p g i n", g=3, i=4)
        sm1 = W[:, 3456:3472]
        QK = OD["qk"].rearrange("p a g n -> p (a g n)")
        kt1 = QK[:, 0:4096].rearrange("p (f b i n) -> p f b i n", f=2, b=4, i=4)
        pt1 = QK[:, 4096:5376].rearrange("p (k r) -> p k r", k=10)
        dd1 = QK[:, 5376:5376 + DEC_W]
        w_out = [OD["v"][:, g, 0:2, :].rearrange("p t n -> p (t n)") for g in range(3)]
        o_all, o_own, o_twice = W[:, 4608:5120], W[:, 5120:5184], W[:, 5184:5312]
        xflat = xT[:, :, :].rearrange("p c t -> p (c t)")
        g1c = [xflat[:, 0:D], xflat[:, D:2 * D], xflat[:, 2 * D:3 * D], W[:, 3584:3584 + D]]
        s1 = mixT[:, 4:8, :].rearrange("p j t -> p (j t)")[:, 0:DEC_W]

        def chunk_of(b, ck):
            if ck == 4:
                return g1c[b % 4]
            at = ck * D if ck < 4 else 4 * D + (ck - 5) * D
            return ring[:, slot_of(6 + b), at:at + D]

        def tile_copied(k):
            return s_op_copied[k % 2], k // 2 + 1

        def turn_copied(n):
            return s_tk_copied[n % 2], n // 2 + 1

        def od_proj_pe(pe):
            pe.wait_ge(s_tp_copied[0], 9)
            pe.wait_ge(s_tp_copied[1], 9)
            for k in range(OD_TILES):
                g, kind, i = k // 12, k % 12 // 4, k % 4
                m = k // 6
                w = wait_slot(pe, 1, m).rearrange("p (c n) -> p c n", c=NC)
                if k >= 4:
                    pe.wait_ge(*tile_copied(k - 4))
                for c in range(NC):
                    ins = pe.matmul(ps[:, 2 + k % 4, 0:NT], w[:, c, (k % 6) * P:(k % 6 + 1) * P], xT[:, c, 0:NT],
                                    start=c == 0, stop=c == NC - 1)
                ins.then_inc(s_op, 1)
                if k % 6 == 5:
                    pe.wait_ge(s_op, k + 1)
                    pe.sem_inc(s_free[1][slot_of(m)], 1)
                if k % 12 in (7, 11):
                    pe.wait_ge(*tile_copied(k))
                    pe.wait_ge(*tile_copied(k - 1))
                    for t in range(3):
                        n = (2 * g + (kind == 2)) * 3 + t
                        if n >= 2:
                            pe.wait_ge(*turn_copied(n - 2))
                        mrow = ROWS[t]
                        for ii in range(4):
                            src = OD["k"][:, g, ii] if kind == 1 else vst[:, g % 2, ii]
                            ins = pe.transpose(ps[0:mrow, 6 + n % 2, ii * P:(ii + 1) * P],
                                               src[:, t * P:t * P + mrow], ident)
                        ins.then_inc(s_tk, 1)

        def od_proj_copy(eng, copy, parity):
            for k in range(OD_TILES):
                g, kind, i = k // 12, k % 12 // 4, k % 4
                if k % 2 == parity:
                    eng.wait_ge(s_op, k + 1)
                    dst = (OD["q"][:, g, i], OD["k"][:, g, i], vst[:, g % 2, i])[kind]
                    copy(dst, ps[:, 2 + k % 4, 0:NT]).then_inc(s_op_copied[parity], 1)
                if k % 12 in (7, 11):
                    for t in range(3):
                        n = (2 * g + (kind == 2)) * 3 + t
                        if n % 2 != parity:
                            continue
                        eng.wait_ge(s_tk, n + 1)
                        mrow = ROWS[t]
                        if kind == 1:
                            if g == 2:
                                eng.wait_ge(s_kst[0], 16 * 2)
                            dst = kst[0:mrow, g % 2, t, :]
                        else:
                            dst = OD["v"][0:mrow, g, t, :]
                        copy(dst, ps[0:mrow, 6 + n % 2, :]).then_inc(s_tk_copied[parity], 1)

        def od_dec_prepare(v):
            v.wait_ge(s_ot, 2 + 2)
            ch = Chain(v, s_qz1)
            ch(v.memset(qz1, 0.0))
            q8 = qz1.rearrange("p g i (b h t) -> p g i h b t", h=NH, t=TS)
            for g in range(3):
                for i in range(4):
                    src = OD["q"][:, g, i, NPR:NT].rearrange("p (b t) -> p b t", t=TS)
                    for s in range(2):
                        rows = slice(HD * s, HD * s + HD)
                        v.tensor_copy(q8[rows, g, i, 2 * i + s], src[rows]).then_inc(s_qz1, 1)
            v.tensor_copy(kns, OD["k"][:, :, :, NPR:NT]).then_inc(s_qz1, 1)
            v.wait_ge(s_qz1, 26)

        def kt_copied(n):
            return s_kt_copied[n % 2], n // 2 + 1

        def od_dec_pe(pe):
            pe.wait_ge(s_qz1, 26)

            def turn(g, ck):
                for bb in range(4):
                    n = 28 * g + 4 * ck + bb
                    if g == 0 and ck == 0:
                        wait_slot(pe, 1, 6 + bb)
                    if g == 0 and ck == 4:
                        pe.wait_ge(s_g1[bb], 16)
                    if g and bb == 0:
                        pe.wait_ge(s_k1[ck // 2], 16 * (8 if ck < 6 else 4))
                    if n >= 2:
                        pe.wait_ge(*kt_copied(n - 2))
                    for i in range(4):
                        ins = pe.transpose(ps[:, n % 2, i * P:(i + 1) * P],
                                           chunk_of(4 * g + bb, ck)[:, i * P:(i + 1) * P], ident)
                    ins.then_inc(s_kt, 1)

            turn(0, 0)
            for g in range(2):
                def scores(ck):
                    pe.wait_ge(*kt_copied(28 * g + 4 * ck + 2))
                    pe.wait_ge(*kt_copied(28 * g + 4 * ck + 3))
                    if ck == 0 and g:
                        pe.wait_ge(s_sm1, 1)
                    bank, col, gg = (2, ck * P, 1) if ck < 4 else (3, (ck - 4) * P, 0 if ck == 4 else 2)
                    for i in range(4):
                        for bb in range(4):
                            b = 4 * g + bb
                            ins = pe.matmul(ps[32 * bb:32 * bb + 32, bank, col:col + P],
                                            qz1[:, gg, i, 32 * b:32 * b + 32], kt1[:, ck % 2, bb, i, :],
                                            start=i == 0, stop=i == 3)
                    ins.then_inc(s_sd1, 1)

                for ck in range(7):
                    if ck < 6:
                        turn(g, ck + 1)
                    scores(ck)
                    if g and ck == 0:
                        outputs_t(pe, 0)
                for gg in range(3):
                    for i in range(4):
                        ins = pe.matmul(ps[:, 3, 384 + 32 * gg:416 + 32 * gg], qz1[:, gg, i, P * g:P * g + P],
                                        kns[:, gg, i, :], start=i == 0, stop=i == 3)
                ins.then_inc(s_sd1, 1)
                if g == 0:
                    turn(1, 0)
                else:
                    pe.wait_ge(s_w1, 16 * 3)
                    pe.wait_ge(s_otc, 2 + 2)
                    od_out_pe(pe, 0, range(3))
                pe.wait_ge(s_ex1, g + 1)
                flat = ps[:, 4:7, :].rearrange("p b n -> p (b n)")
                if g:
                    pe.wait_ge(s_p1c, 2)
                    pe.wait_ge(s_mix[1], 2)
                for ck in range(7):
                    pe.transpose(flat[:, ck * P:(ck + 1) * P], s1[:, ck * P:(ck + 1) * P], ident)
                for gg in range(3):
                    ins = pe.transpose(flat[0:NSA, (7 + gg) * P:(8 + gg) * P], s1[:, OLD + gg * NSA:OLD + (gg + 1) * NSA],
                                       ident)
                ins.then_inc(s_p1, 1)
                pe.wait_ge(s_p1c, 2 * g + 2)
                if g:
                    pe.wait_ge(s_sm1, 5)
                    pe.wait_ge(s_v1, 16 * 16)
                for ck in range(7):
                    for bb in range(4):
                        pe.matmul(ps[32 * bb:32 * bb + 32, 7, :], pt1[:, ck, 32 * bb:32 * bb + 32],
                                  chunk_of(4 * g + bb, ck)[:, 512:1024], start=ck == 0, stop=False)
                for gg in range(3):
                    ins = pe.matmul(ps[:, 7, :], pt1[0:NSA, 7 + gg, :], OD["v"][0:NSA, gg, 2, :], start=False,
                                    stop=gg == 2)
                ins.then_inc(s_o1, 1)
                pe.wait_ge(s_o1, g + 1)
                for bb in range(4):
                    pe.sem_inc(s_free[1][slot_of(6 + 4 * g + bb)], 1)
            od_out_pe(pe, 1, range(3))
            outputs_t(pe, 1)
            wait_slot(pe, 1, 14)
            od_out_pe(pe, 0, (3,)).then_inc(s_f, 1)
            od_out_pe(pe, 1, (3,)).then_inc(s_f, 1)
            pe.wait_ge(s_mix[1], 4)
            od_out_pe(pe, 2, range(4)).then_inc(s_f, 1)
            pe.wait_ge(s_f, 6 + 3)
            pe.sem_inc(s_free[1][slot_of(14)], 1)

        def od_out_pe(pe, t, blocks):
            rows = ROWS[t]
            for j in blocks:
                w = w_out[j] if j < 3 else ring[:, slot_of(14), 0:D]
                for x in range(2):
                    ins = pe.matmul(ps[0:rows, 2 * t + x, :], mixT[:, j, t * P:t * P + rows],
                                    w[:, x * BANK:(x + 1) * BANK], start=j == 0, stop=j == 3)
            return ins

        def outputs_t(pe, g):
            pe.wait_ge(s_sm1, 8 * g + 8)
            pe.transpose(ps[:, 4, 0:P], o_twice, ident).then_inc(s_ot1, 1)

        def od_dec_keys(eng, copy, parity, g, ck):
            for bb in range(parity, 4, 2):
                n = 28 * g + 4 * ck + bb
                eng.wait_ge(s_kt, n + 1)
                if g or ck >= 2:
                    eng.wait_ge(s_sd1, 8 * g + max(ck - 1, 0))
                copy(kt1[:, ck % 2, bb], ps[:, n % 2, :].rearrange("p (i n) -> p i n", i=4)).then_inc(
                    s_kt_copied[parity], 1)

        def od_dec_dve(v):
            def outputs_copy(g):
                v.wait_ge(s_ot1, g + 1)
                for s in range(2):
                    rows = slice(HD * s, HD * s + HD)
                    dst = mixT[rows, 0:4, NPR + 16 * g:NPR + 16 * g + 16].rearrange("p i (b t) -> p i b t", t=TS)
                    src = ps[rows, 4, 0:P].rearrange("p (b i s t) -> p s i b t", b=4, i=4, s=2)[:, s]
                    v.tensor_copy(dst, src).then_inc(s_mix[1], 1)

            for g in range(2):
                for ck in range(g, 7):
                    od_dec_keys(v, v.tensor_copy, 1, g, ck)
                    if g and ck == 1:
                        outputs_copy(0)
                steps = 8 * g

                def step(ins):
                    nonlocal steps
                    steps += 1
                    ins.then_inc(s_sm1, 1)
                    v.wait_ge(s_sm1, steps)
                v.wait_ge(s_sd1, 8 * g + 8)
                v.wait_ge(s_dd1, 16 * (g + 1))
                if g:
                    v.wait_ge(s_p1, 1)
                c = lambda k: sm1[:, 4 * g + k:4 * g + k + 1]
                step(v.scalar_tensor_tensor(out=s1, in0=dd1, scalar=row_slope,
                                            in1=banks(2, DEC_W), op0=ALU.mult, op1=ALU.add))
                step(v.tensor_reduce(c(0), s1, AX.X, ALU.max))
                step(v.tensor_scalar(c(1), c(0), -SCALE, None, ALU.mult))
                if g == 0:
                    od_dec_keys(v, v.tensor_copy, 1, 1, 0)
                v.wait_ge(s_ex1, g + 1)
                step(v.reciprocal(c(3), c(2)))
                v.wait_ge(s_o1, g + 1)
                own = row_head.unsqueeze(2).broadcast_to([P, NH, HD])
                step(v.tensor_tensor(o_all.rearrange("p (h d) -> p h d", h=NH),
                                     ps[:, 7, :].rearrange("p (h d) -> p h d", h=NH), own, ALU.mult))
                step(v.tensor_reduce(o_own, o_all.rearrange("p (h d) -> p d h", h=NH), AX.X, ALU.add))
                for s in range(2):
                    step(v.tensor_scalar(o_twice[:, s * HD:(s + 1) * HD], o_own, c(3), None, ALU.mult))
            outputs_copy(1)

        def od_dec_act(act):
            copy = lambda dst, src: act.activation(dst, src, ACT.Copy)
            for g in range(2):
                for ck in range(g, 7):
                    od_dec_keys(act, copy, 0, g, ck)
                c = lambda k: sm1[:, 4 * g + k:4 * g + k + 1]
                if g == 0:
                    od_dec_keys(act, copy, 0, 1, 0)
                act.wait_ge(s_sm1, 8 * g + 3)
                act.activation(s1, s1, ACT.Exp, bias=c(1), scale=SCALE, accum_out=c(2)).then_inc(s_ex1, 1)
                act.wait_ge(s_p1, g + 1)
                flat = ps[:, 4:7, :].rearrange("p b n -> p (b n)")
                if g:
                    act.wait_ge(s_o1, 1)
                act.activation(pt1[:, 0:7, :], flat[:, 0:7 * P].rearrange("p (k r) -> p k r", k=7),
                               ACT.Copy).then_inc(s_p1c, 1)
                act.activation(pt1[0:NSA, 7:10, :], flat[0:NSA, 7 * P:10 * P].rearrange("p (k r) -> p k r", k=3),
                               ACT.Copy).then_inc(s_p1c, 1)

        s_small = sem("s_small")
        s_copy = sem("s_copy")
        block = ctx.enter_context(nc.Block())

        even = Prompt(0, 1, 4, EV["s"], EV["pt"], EV["osb"], EV["sm"],
                      (EV["dist"][:, 0:P], EV["dist"][:, P:3 * P]),
                      lambda g, h, qb: (EV["q"][64 * (h // 4):64 * (h // 4) + 64, h % 4, qb * P:(qb + 1) * P],
                                        EV["kv"][64 * (h // 4):64 * (h // 4) + 64, 0, 0:(qb + 1) * P]),
                      lambda g, h, kb: EV["vtok"][:, kb, 64 * (h // 4):64 * (h // 4) + 64],
                      lambda h: ((h % 4) * 2 + h // 4) * HD)
        odd = Prompt(1, 3, 2, OP["s"], OP["pt"], OP["osb"], OP["sm"], (OP["dist"][:, 0:3 * P], OP["dist"][:, 3 * P:9 * P]),
                     lambda g, h, qb: (OD["q"][64 * (h % 2):64 * (h % 2) + 64, g, h // 2, qb * P:(qb + 1) * P],
                                       OD["k"][64 * (h % 2):64 * (h % 2) + 64, g, h // 2, 0:(qb + 1) * P]),
                     lambda g, h, kb: OD["v"][:, g, kb, h * HD:(h + 1) * HD],
                     lambda h: h * HD)

        @block.sync
        def _(sp):
            def load(layer, m, parts):
                n = reads_before(layer, m)
                if n:
                    sp.wait_ge(s_free[layer][slot_of(m)], n)
                for dst, src in parts:
                    sp.dma_start(dst, src).then_inc(s_ring[layer][slot_of(m)], 16)

            def rows8(w):
                return w.rearrange("(p c) n -> p c n", c=NC)

            def in_cols(w, m, total):
                n = min(768, total - 768 * m)
                dst = ring[:, slot_of(m), 0:NC * n].rearrange("p (c n) -> p c n", c=NC)
                return [(dst, rows8(w)[:, :, 768 * m:768 * m + n])]

            def glu(slot, wg, wu, wd):
                return [(ring[:, slot, 0:2048].rearrange("p (c n) -> p c n", c=NC), rows8(wg)),
                        (ring[:, slot, 2048:4096].rearrange("p (c n) -> p c n", c=NC), rows8(wu)),
                        (ring[:, slot, 4096:6144].rearrange("p (j n) -> p j n", j=2), wd.rearrange("(j p) n -> p j n", p=P))]

            def expert(L, i, u, first=False):
                q, s = u // 2, slot_of(EXP0[L] + u)
                w = (a["w_exp_gate"][L], a["w_exp_up"][L], a["w_exp_down"][L])
                e = u if first else (i % 16) * 4 + u
                gate, up, down = glu(s, *[x[e] if first else x[bass.ds(e, 1)].rearrange("a k n -> (a k) n") for x in w])
                if first:
                    sp.wait_ge(s_free[L][s], static_reads[L][s])
                else:
                    sp.wait_ge(s_gu[L], 2 * i - 1 + q)
                for dst, src in (gate, up):
                    sp.dma_start(dst, src).then_inc(s_ring[L][s], 16)
                downs.append(down)
                if u % 2:
                    if not first:
                        sp.wait_ge(s_dn[L], 2 * i - 1 + q)
                    while downs:
                        dst, src = downs.pop(0)
                        sp.dma_start(dst, src).then_inc(s_ring_dn[L][q], 16)
            downs = []

            def more_experts(L):
                with sp.Fori(1, NE // 4) as i:
                    for u in range(4):
                        expert(L, i, u)
                sp.wait_ge(s_disp, L + 1)
                more = iterations(sp)
                with sp.If(more > NE // 4 - 1):
                    with sp.Fori(NE // 4, more + 1) as i:
                        for u in range(4):
                            expert(L, i, u)
                with sp.Else():
                    sp.nop()
                return more

            def gain_bias(turn, g, b):
                if turn:
                    sp.wait_ge(s_gb_free, turn)
                else:
                    sp.wait_ge(s_od, 1)
                sp.dma_start(gb[:, 0, :], g.rearrange("(a n) -> a n", a=1).broadcast_to([P, D])).then_inc(s_gb, 16)
                sp.dma_start(gb[:, 1, :], b.rearrange("(a n) -> a n", a=1).broadcast_to([P, D])).then_inc(s_gb, 16)

            def router(L):
                sp.dma_start(MO["wr"], rows8(a["w_router"][L])).then_inc(s_wr, 16)
                sp.dma_start(MO["rb"], a["router_bias"][L:L + 1, :].broadcast_to([P, NE])).then_inc(s_wr, 16)

            sp.dma_start(square[:, :], a["c_square"]).then_inc(s_const, 16)
            sp.dma_start(misc[:, :], a["c_misc"]).then_inc(s_const, 16)
            xp = a["x_prompt"][0].rearrange("(t p) n -> t p n", p=P)
            for t in range(2):
                sp.dma_start(x_tok[:, t, :], xp[t]).then_inc(s_x, 16)
            sp.wait_ge(s_pad, 1)
            sp.dma_start(x_tok[0:NSA, 2, :], a["x_sample"].rearrange("b t n -> (b t) n")).then_inc(s_x, 16)
            load(0, 0, in_cols(a["w_in_even"][0], 0, EV_COLS))
            w1 = ring[:, 1, :].rearrange("p (c n) -> p c n", c=NC)
            src = rows8(a["w_in_even"][0])
            parts = [(w1[:, :, 0:256], src[:, :, 768:q0])]
            for h in range(NH):
                at = 256 + ((h % 4) * 2 + h // 4) * HD
                parts.append((w1[:, :, at:at + HD], src[:, :, q0 + h * HD:q0 + (h + 1) * HD]))
            load(0, 1, parts)
            sp.wait_ge(s_wg0, 1)
            for kind, w in enumerate((a["w_rgate"][0], a["w_igate"][0])):
                for s in range(2):
                    rows = slice(HD * s, HD * s + HD)
                    sp.dma_start(EV["wg"][rows, kind:8:2, rows],
                                 w.rearrange("(j s) c d -> s c j d", s=2)[s]).then_inc(s_wg, 16)
            load(0, 2, in_cols(a["w_in_even"][0], 2, EV_COLS))
            sp.dma_start(EV["sink"][:, 0:NH], a["swa_sinks"].broadcast_to([P, NH])).then_inc(s_small, 16)
            sp.dma_start(EV["dist"][:, 0:P], a["c_prompt"][:, 0:P]).then_inc(s_small, 16)
            sp.dma_start(EV["dist"][:, P:3 * P], a["c_prompt"][:, 3 * P:5 * P]).then_inc(s_small, 16)
            sp.dma_start(EV["dd"], a["c_even"].rearrange("g p n -> p g n")).then_inc(s_small, 16)
            sp.dma_start(gb[:, :, :].rearrange("p a n -> p (a n)").rearrange("p (b n) -> p b n", b=NB),
                         a["cache_swa_kv"][0].rearrange("b k a h d -> k b (a h d)")).then_inc(s_cache, 16)

            def out_even(hf):
                w = a["w_out_even"][0]
                s = slot_of(3 + hf)
                dst = ring[:, s, 0:8 * BANK].rearrange("p (j n) -> p j n", n=BANK)
                cols = slice(hf * BANK, (hf + 1) * BANK)
                parts = [(dst[:, 0:4, :], w[0:512, cols].rearrange("(j p) n -> p j n", p=P))]
                for x in range(2):
                    parts.append((dst[HD * x:HD * x + HD, 4:8, :],
                                  w[512 + 256 * x:768 + 256 * x, cols].rearrange("(i d) n -> d i n", d=HD)))
                return parts
            load(0, 3, out_even(0))
            load(0, 4, out_even(1))
            load(0, 5, glu(slot_of(5), a["w_sh_gate"][0], a["w_sh_up"][0], a["w_sh_down"][0]))
            gain_bias(0, a["ln1_g"][0], a["ln1_b"][0])
            expert(0, 0, 0, True)
            expert(0, 0, 1, True)
            sp.wait_ge(s_f, 3)
            sp.wait_ge(s_sout, OUT0)
            router(0)
            expert(0, 0, 2, True)
            gain_bias(1, a["ln2_g"][0], a["ln2_b"][0])
            expert(0, 0, 3, True)
            more = more_experts(0)

            for m in range(RING):
                sp.wait_ge(s_dn[0], 2 * more + 1 + (m - EXP0[0]) % RING // 2)
                load(1, m, in_cols(a["w_in_odd"][0], m, 6 * 768))
            gain_bias(2, a["ln1_g"][1], a["ln1_b"][1])
            for m in range(4, 6):
                load(1, m, in_cols(a["w_in_odd"][0], m, 6 * 768))
            sp.wait_ge(s_kst[0], 16 * 2)
            sp.wait_ge(s_kst[1], 16 * 6)
            sp.wait_ge(s_tk, 18)
            sp.dma_start(OP["dist"], a["c_prompt"]).then_inc(s_dp, 16)

            def rows_of(b, ck):
                if ck < 4:
                    return a["cache_dil2_kv"][0, b].rearrange("(k p) a h d -> k p (a h d)", p=P)[ck]
                if ck == 4:
                    return a["cache_dil1_kv"][0, b].rearrange("k a h d -> k (a h d)")
                d3 = a["cache_dil3_kv"][0, b].rearrange("(s r) a h d -> s r (a h d)", r=16)
                return d3[32 * (ck - 5):32 * (ck - 4), 0:TS, :]

            for b in range(4):
                d2 = a["cache_dil2_kv"][0, b].rearrange("(k p) a h d -> p k (a h d)", p=P)
                parts = [(ring[:, slot_of(6 + b), 0:4 * D].rearrange("p (k n) -> p k n", k=4), d2)]
                load(1, 6 + b, parts + [(chunk_of(b, ck), rows_of(b, ck)) for ck in (5, 6)])
            sp.wait_ge(s_op, OD_TILES)
            for b in range(4):
                if b == 3:
                    sp.wait_ge(s_qz1, 26)
                sp.dma_start(chunk_of(b, 4), rows_of(b, 4)).then_inc(s_g1[b], 16)
            sp.dma_start(dd1, a["c_odd"][0]).then_inc(s_dd1, 16)
            sp.wait_ge(s_sout, OUT1)
            for j in range(3):
                sp.dma_start(w_out[j], a["w_out_odd"][0, j * P:(j + 1) * P, :]).then_inc(s_w1, 16)
            for ck in range(7):
                for bb in range(4):
                    sp.wait_ge(s_kt, 4 * ck + bb + 1)
                    sp.dma_start(chunk_of(4 + bb, ck)[:, 0:512], rows_of(4 + bb, ck)[..., 0:512]).then_inc(s_k1[ck // 2], 16)
            sp.wait_ge(s_sm1, 1)
            sp.dma_start(dd1, a["c_odd"][1]).then_inc(s_dd1, 16)
            for bb in range(4):
                b, s = 4 + bb, slot_of(6 + bb)
                sp.wait_ge(s_free[1][s], reads_before(1, 6 + b))
                d2 = a["cache_dil2_kv"][0, b].rearrange("(k p) a h d -> p k (a h d)", p=P)
                sp.dma_start(ring[:, s, 0:4 * D].rearrange("p (k n) -> p k n", k=4)[:, :, 512:1024],
                             d2[:, :, 512:1024]).then_inc(s_v1, 16)
                for ck in (4, 5, 6):
                    sp.dma_start(chunk_of(b, ck)[:, 512:1024], rows_of(b, ck)[..., 512:1024]).then_inc(s_v1, 16)
            load(1, 14, [(ring[:, slot_of(14), 0:D], a["w_out_odd"][0, 3 * P:4 * P, :])])
            load(1, 15, glu(slot_of(15), a["w_sh_gate"][1], a["w_sh_up"][1], a["w_sh_down"][1]))
            expert(1, 0, 0, True)
            expert(1, 0, 1, True)
            sp.wait_ge(s_f, 9)
            router(1)
            expert(1, 0, 2, True)
            gain_bias(3, a["ln2_g"][1], a["ln2_b"][1])
            expert(1, 0, 3, True)
            more_experts(1)
            for t in range(3):
                wait_residual(sp, 3, t)
                if t < 2:
                    dst = o["y_prompt"][0].rearrange("(t p) n -> t p n", p=P)[t]
                else:
                    dst = o["y_sample"].rearrange("b t n -> (b t) n")
                sp.dma_start(dst, x_tok[0:ROWS[t], t, :]).then_inc(s_x, 16)
            sp.wait_ge(s_x, 16 * 3 + 16 * 3)

        @block.gpsimd
        def _(pool):
            pool.memset(EV["wg"], 0.0).then_inc(s_wg0, 1)

            def shift(dst, src, w):
                for b in range(NB):
                    pool.dma_start(dst[0, b, 0:w - TS].rearrange("k a h d -> k (a h d)"),
                                   src[0, b, TS:w].rearrange("k a h d -> k (a h d)")).then_inc(s_copy, 16)
            names = (("swa_kv_sample", "cache_swa_kv", P), ("dil1_kv_sample", "cache_dil1_kv", WIN[0]),
                     ("dil2_kv_sample", "cache_dil2_kv", WIN[1]), ("dil3_kv_sample", "cache_dil3_kv", WIN[2]))
            pool.wait_ge(s_ring[0][slot_of(2)], loaded(0, 2))
            shift(o[names[3][0]], a[names[3][1]], names[3][2])
            n = 0

            def store(dst, src):
                nonlocal n
                n += 1
                pool.dma_start(dst, src).then_inc(s_sout, 16)
            pool.wait_ge(s_kvt_copied, 2)
            for kind, name in enumerate(("ktok", "vtok")):
                store(o["swa_kv_prompt"][0, 0, :, kind].rearrange("t h d -> t (h d)"), EV[name][:, 1, :])
                store(o["swa_kv_sample"][0, :, P - TS:P, kind].rearrange("b t h d -> b t (h d)"), EV[name][0:NSA, 2, :])
            pool.wait_ge(s_so_copied, 1)
            so = EV["st_out"]
            store(o["lru_h_prompt"][0], so[0:1, :])
            store(o["lru_h_sample"][0], so[1:9, :])
            store(o["lru_conv_prompt"][0, 0], so[9:12, :])
            store(o["lru_conv_sample"][0].rearrange("b k n -> (b k) n"), so[12:36, :])
            assert 16 * n == OUT0
            ln_pool(pool, 0)
            moe_pairs_pool(pool, 0)
            ln_pool(pool, 1)
            pool.wait_ge(s_ring[1][slot_of(5)], loaded(1, 5))
            for dst, src, w in names[:3]:
                shift(o[dst], a[src], w)
            for g in range(3):
                keep = WIN[g] if g == 0 else NPR
                o_p, o_s = o[f"dil{g + 1}_kv_prompt"], o[f"dil{g + 1}_kv_sample"]
                for kind in range(2):
                    for par in range(2):
                        last = (2 * g + kind) * 3 + 2
                        k, v_ = turn_copied(last if last % 2 == par else last - 1)
                        pool.wait_ge(k, v_)
                    src = (lambda t, m: kst[0:m, g % 2, t, :]) if kind == 0 else (lambda t, m: OD["v"][0:m, g, t, :])
                    for t in range(2):
                        at = t * P - (NPR - keep)
                        if at >= 0:
                            ins = (o_p[0, 0, at:at + P, kind].rearrange("t h d -> t (h d)"), src(t, P))
                            if kind == 0:
                                pool.dma_start(*ins).then_inc(s_kst[g > 0], 16)
                            else:
                                store(*ins)
                    ins = (o_s[0, :, WIN[g] - TS:WIN[g], kind].rearrange("b t h d -> b t (h d)"), src(2, NSA))
                    if kind == 0:
                        pool.dma_start(*ins).then_inc(s_kst[g > 0], 16)
                    else:
                        store(*ins)
            assert 16 * n == OUT1
            ln_pool(pool, 2)
            moe_pairs_pool(pool, 1)
            ln_pool(pool, 3)
            pool.wait_ge(s_sout, OUT1)
            pool.wait_ge(s_copy, 16 * 4 * NB)

        @block.scalar
        def _(act):
            st = EV["st_in"]
            for dst, src in ((st[0:24, :], a["state_lru_conv"][0].rearrange("b k n -> (b k) n")),
                             (st[24:32, :], a["state_lru_h"][0]), (st[32:36, :], a["conv_w"][0]),
                             (st[36:37, :], a["conv_b"]), (st[37:38, :], a["b_rgate"]), (st[38:39, :], a["b_igate"]),
                             (st[39:40, :], a["lru_lambda"])):
                act.dma_start(dst, src).then_inc(s_ev_par, 16)
            copy = lambda dst, src: act.activation(dst, src, ACT.Copy)
            xt_copy(act, copy, 0, 0)
            ev_softplus_act(act)
            ev_proj_act(act, range(4, 10))
            ev_lru_act(act)
            ev_proj_act(act, range(10, 12))
            ev_root_act(act)
            ev_proj_act(act, range(12, 14))
            ev_kvt_act(act)
            prompt_act(act, even, ev_dec_act(act))
            ln_act(act, 0)
            for L in range(2):
                xt_copy(act, copy, 2 * L + 1, 0)
                moe_act_head(act, L)
                moe_shared_acc_act(act, L)
                moe_pairs_act(act, L)
                ln_act(act, 2 * L + 1)
                if L == 0:
                    xt_copy(act, copy, 2, 0)
                    od_proj_copy(act, copy, 0)
                    prompt_act(act, odd)
                    od_dec_act(act)
                    ln_act(act, 2)

        @block.vector
        def _(v):
            v.wait_ge(s_const, 32)
            v.tensor_copy(ident_b[:, :], ident).then_inc(s_const, 1)
            v.memset(x_tok[:, 2, :], 0.0).then_inc(s_pad, 1)
            v.memset(xT[:, :, NT:NTP], 0.0).then_inc(s_pad, 1)
            v.memset(stats[:, :, EPS_COL:EPS_COL + 1], EPS)
            xt_copy(v, v.tensor_copy, 0, 1)
            ev_proj_dve(v)
            ev_lru_dve(v)
            ev_dec_qz(v)
            v.wait_ge(s_small, 64)
            ch = lru["chain"]
            ch(v.tensor_scalar(EV["sink"][:, NH:2 * NH], EV["sink"][:, 0:NH], -1.0, None, ALU.mult))
            ch(v.tensor_tensor(EV["sink"][:, 2 * NH:3 * NH], EV["sink"][:, 0:NH], row_head, ALU.mult))
            ch(v.tensor_reduce(EV["sink"][:, 24:25], EV["sink"][:, 2 * NH:3 * NH], AX.X, ALU.add))
            prompt_dve(v, even, ev_dec_dve(v))
            ln_dve(v, 0, False)
            for L in range(2):
                xt_copy(v, v.tensor_copy, 2 * L + 1, 1)
                moe_route_dve(v, L)
                moe_shared_dve(v, L)
                moe_pos_dve(v, L)
                moe_pairs_dve(v, L)
                ln_dve(v, 2 * L + 1, True)
                if L == 0:
                    xt_copy(v, v.tensor_copy, 2, 1)
                    od_proj_copy(v, v.tensor_copy, 1)
                    v.wait_ge(s_dp, 16)
                    prompt_dve(v, odd)
                    od_dec_prepare(v)
                    od_dec_dve(v)
                    v.memset(xT[:, :, NT:NTP], 0.0).then_inc(s_pad, 1)
                    ln_dve(v, 2, False)

        @block.tensor
        def _(pe):
            pe.wait_ge(s_const, 33)
            xt_pe(pe, 0)
            ev_state_pe(pe)
            ev_proj_pe(pe, range(10))
            ev_gate_pe(pe)
            ev_proj_pe(pe, range(10, 14))
            ev_kvt_pe(pe)
            pe.wait_ge(s_kvt_copied, 2)
            prompt_pe(pe, even, ev_dec_pe(pe))
            pe.wait_ge(s_otc, 2)
            pe.wait_ge(s_mix[0], 8)
            out_proj_pe(pe)
            for L in range(2):
                xt_pe(pe, 2 * L + 1)
                moe_route_pe(pe, L)
                moe_shared_pe(pe, L)
                moe_pos_pe(pe, L)
                moe_shared_down_pe(pe, L)
                moe_pairs_pe(pe, L)
                if L == 0:
                    xt_pe(pe, 2)
                    od_proj_pe(pe)
                    pe.wait_ge(s_op_copied[0], OD_TILES // 2)
                    pe.wait_ge(s_op_copied[1], OD_TILES // 2)
                    pe.wait_ge(s_tk_copied[0], 9)
                    pe.wait_ge(s_tk_copied[1], 9)
                    prompt_pe(pe, odd)
                    od_dec_pe(pe)
                    pe.wait_ge(s_pad, 3)


_INS = ['x_prompt', 'x_sample', 'state_lru_h', 'state_lru_conv', 'cache_swa_kv', 'cache_dil1_kv', 'cache_dil2_kv',
        'cache_dil3_kv', 'w_in_even', 'conv_w', 'conv_b', 'w_rgate', 'b_rgate', 'w_igate', 'b_igate', 'lru_lambda',
        'swa_sinks', 'w_out_even', 'w_in_odd', 'w_out_odd', 'ln1_g', 'ln1_b', 'ln2_g', 'ln2_b', 'w_router',
        'router_bias', 'w_exp_gate', 'w_exp_up', 'w_exp_down', 'w_sh_gate', 'w_sh_up', 'w_sh_down']
_OUTS = [("y_prompt", (1, 256, 1024)), ("y_sample", (8, 4, 1024)), ("lru_h_prompt", (1, 1, 512)),
         ("lru_h_sample", (1, 8, 512)), ("lru_conv_prompt", (1, 1, 3, 512)), ("lru_conv_sample", (1, 8, 3, 512)),
         ("swa_kv_prompt", (1, 1, 128, 2, 2, 64)), ("swa_kv_sample", (1, 8, 128, 2, 2, 64)),
         ("dil1_kv_prompt", (1, 1, 128, 2, 8, 64)), ("dil1_kv_sample", (1, 8, 128, 2, 8, 64)),
         ("dil2_kv_prompt", (1, 1, 256, 2, 8, 64)), ("dil2_kv_sample", (1, 8, 512, 2, 8, 64)),
         ("dil3_kv_prompt", (1, 1, 256, 2, 8, 64)), ("dil3_kv_sample", (1, 8, 1024, 2, 8, 64))]


def kernel(**inputs):
    import numpy as _np
    import concourse.bacc as _bacc
    from concourse import mybir as _mybir
    from concourse.bass_utils import run_bass_kernel_spmd as _run

    nc = _bacc.Bacc("TRN2", target_bir_lowering=False, num_devices=1)
    arrays, a, o = {}, {}, {}
    for name in _INS:
        arrays[f"in_{name}"] = _np.ascontiguousarray(inputs[name])
    for name, table in tables().items():
        arrays[f"in_{name}"] = table
    for name, x in arrays.items():
        a[name[3:]] = nc.dram_tensor(name, x.shape, _mybir.dt.from_np(x.dtype), kind="ExternalInput").ap()
    for name, shape in _OUTS:
        o[name] = nc.dram_tensor(f"out_{name}", shape, F32, kind="ExternalOutput").ap()
    build(nc, a, o)
    r = _run(nc, [arrays], core_ids=[0])
    return tuple(r.results[0][f"out_{name}"] for name, _ in _OUTS)
```
